# Optimizing a Trainium2 kernel written in Bass

```python
import jax
import jax.numpy as jnp
from jax import lax
import numpy as np

D_MODEL = 1024
BATCH = 1
SEQ = 512
DEPTH = 1

GRID_W = 64
CTX_LEN = 256
HEAD_DIM = 64
A_Q_HEADS = D_MODEL // (2 * HEAD_DIM)
A_KV_HEADS = A_Q_HEADS // 4
B_Q_HEADS = D_MODEL // (2 * HEAD_DIM)
B_KV_HEADS = B_Q_HEADS // 4
A_Q_DIM = A_Q_HEADS * HEAD_DIM
A_KV_DIM = A_KV_HEADS * HEAD_DIM
B_Q_DIM = B_Q_HEADS * HEAD_DIM
B_KV_DIM = B_KV_HEADS * HEAD_DIM
PROJ_SIZES = (A_Q_DIM, A_KV_DIM, A_KV_DIM, B_Q_DIM, B_KV_DIM, B_KV_DIM)
IN_DIM = A_Q_DIM + 2 * A_KV_DIM + B_Q_DIM + 2 * B_KV_DIM
MIX_DIM = A_Q_DIM + B_Q_DIM
WINDOW = 128
BLOCK = 128
ROPE_THETA = 10000.0
N_GROUPS = 4
EXPERTS_PER_GROUP = 8
N_EXPERTS = N_GROUPS * EXPERTS_PER_GROUP
TOP_K_IN_GROUP = 2
EXPERT_FF = D_MODEL // 2
EPS = 1e-6
NEG_INF = -1e30

kernel_name = 'hymba_style_dual_attention_hier_moe_dit'

def rms_norm(x, g):
    xf = x.astype(jnp.float32)
    y = xf * lax.rsqrt(jnp.mean(xf * xf, axis=-1, keepdims=True) + EPS)
    return (y * g.astype(jnp.float32)).astype(x.dtype)

def axial_rope_tables(rows):
    row = jnp.broadcast_to(jnp.arange(rows, dtype=jnp.float32)[:, None], (rows, GRID_W)).reshape(-1)
    col = jnp.broadcast_to(jnp.arange(GRID_W, dtype=jnp.float32)[None, :], (rows, GRID_W)).reshape(-1)
    axis_dim = HEAD_DIM // 2
    inv_freq = ROPE_THETA ** (-jnp.arange(0, axis_dim, 2, dtype=jnp.float32) / axis_dim)
    ang = jnp.concatenate([row[:, None] * inv_freq, col[:, None] * inv_freq], axis=-1)
    return jnp.cos(ang), jnp.sin(ang)

def apply_rope(x, cos, sin):
    xf = x.astype(jnp.float32).reshape(*x.shape[:-1], HEAD_DIM // 2, 2)
    x0, x1 = xf[..., 0], xf[..., 1]
    cs = cos[None, :, None, :]
    sn = sin[None, :, None, :]
    out = jnp.stack([x0 * cs - x1 * sn, x0 * sn + x1 * cs], axis=-1)
    return out.reshape(x.shape).astype(x.dtype)

def project_heads(h, w_in):
    p = h @ w_in
    cuts, acc = [], 0
    for size in PROJ_SIZES[:-1]:
        acc += size
        cuts.append(acc)
    qa, ka, va, qb, kb, vb = jnp.split(p, cuts, axis=-1)
    lead = h.shape[:-1]
    return (qa.reshape(*lead, A_Q_HEADS, HEAD_DIM), ka.reshape(*lead, A_KV_HEADS, HEAD_DIM),
            va.reshape(*lead, A_KV_HEADS, HEAD_DIM), qb.reshape(*lead, B_Q_HEADS, HEAD_DIM),
            kb.reshape(*lead, B_KV_HEADS, HEAD_DIM), vb.reshape(*lead, B_KV_HEADS, HEAD_DIM))

def windowed_sink_attention(q, k, v, k_ctx, v_ctx, sink):
    bsz, n, hq, dh = q.shape
    hkv = k.shape[2]
    g = hq // hkv
    nb = n // BLOCK
    scale = dh ** -0.5
    qb = q.reshape(bsz, nb, BLOCK, hkv, g, dh)
    pad = ((0, 0), (BLOCK, BLOCK), (0, 0), (0, 0))
    kp = jnp.pad(k, pad).reshape(bsz, nb + 2, BLOCK, hkv, dh)
    vp = jnp.pad(v, pad).reshape(bsz, nb + 2, BLOCK, hkv, dh)
    kw = jnp.concatenate([kp[:, :-2], kp[:, 1:-1], kp[:, 2:]], axis=2)
    vw = jnp.concatenate([vp[:, :-2], vp[:, 1:-1], vp[:, 2:]], axis=2)
    qpos = jnp.arange(nb)[:, None, None] * BLOCK + jnp.arange(BLOCK)[None, :, None]
    kpos = jnp.arange(nb)[:, None, None] * BLOCK + jnp.arange(3 * BLOCK)[None, None, :] - BLOCK
    allowed = (jnp.abs(kpos - qpos) <= WINDOW) & (kpos >= 0) & (kpos < n)
    s_lat = jnp.einsum('bnqhgd,bnkhd->bnhgqk', qb, kw).astype(jnp.float32) * scale
    s_lat = jnp.where(allowed[None, :, None, None], s_lat, NEG_INF)
    s_ctx = jnp.einsum('bnqhgd,bchd->bnhgqc', qb, k_ctx).astype(jnp.float32) * scale
    s_sink = jnp.broadcast_to(sink.astype(jnp.float32).reshape(1, 1, hkv, g, 1, 1), s_lat.shape[:-1] + (1,))
    p = jax.nn.softmax(jnp.concatenate([s_lat, s_ctx, s_sink], axis=-1), axis=-1).astype(v.dtype)
    n_band = 3 * BLOCK
    p_lat = p[..., :n_band]
    p_ctx = p[..., n_band:n_band + k_ctx.shape[1]]
    o = (jnp.einsum('bnhgqk,bnkhd->bnqhgd', p_lat, vw)
         + jnp.einsum('bnhgqc,bchd->bnqhgd', p_ctx, v_ctx))
    return o.reshape(bsz, n, hq, dh)

def blocked_global_attention(q, k, v, k_ctx, v_ctx):
    bsz, n, hq, dh = q.shape
    hkv = k.shape[2]
    g = hq // hkv
    nb = n // BLOCK
    scale = dh ** -0.5
    k_all = jnp.concatenate([k, k_ctx], axis=1)
    v_all = jnp.concatenate([v, v_ctx], axis=1)
    q_blocks = jnp.moveaxis(q.reshape(bsz, nb, BLOCK, hkv, g, dh), 1, 0)

    def one_block(qblk):
        s = jnp.einsum('bqhgd,bkhd->bhgqk', qblk, k_all).astype(jnp.float32) * scale
        p = jax.nn.softmax(s, axis=-1).astype(v_all.dtype)
        return jnp.einsum('bhgqk,bkhd->bqhgd', p, v_all)

    o = lax.map(one_block, q_blocks)
    return jnp.moveaxis(o, 0, 1).reshape(bsz, n, hq, dh)

def context_attention(q, k, v, sink):
    bsz, n, hq, dh = q.shape
    hkv = k.shape[2]
    g = hq // hkv
    qg = q.reshape(bsz, n, hkv, g, dh)
    s = jnp.einsum('bqhgd,bkhd->bhgqk', qg, k).astype(jnp.float32) * dh ** -0.5
    if sink is not None:
        s_sink = jnp.broadcast_to(sink.astype(jnp.float32).reshape(1, hkv, g, 1, 1), s.shape[:-1] + (1,))
        s = jnp.concatenate([s, s_sink], axis=-1)
    p = jax.nn.softmax(s, axis=-1).astype(v.dtype)[..., :k.shape[1]]
    o = jnp.einsum('bhgqk,bkhd->bqhgd', p, v)
    return o.reshape(bsz, n, hq, dh)

def merge_head_groups(oa, ob, a_out_norm, b_out_norm, w_out):
    bsz, n = oa.shape[:2]
    oa = rms_norm(oa.reshape(bsz, n, A_Q_DIM), a_out_norm)
    ob = rms_norm(ob.reshape(bsz, n, B_Q_DIM), b_out_norm)
    return jnp.concatenate([oa, ob], axis=-1) @ w_out

def token_mixing(hx, hc, w_in, a_sink, b_q_norm, b_k_norm, a_out_norm, b_out_norm, w_out,
                 cos, sin, with_ctx_out):
    qa, ka, va, qb, kb, vb = project_heads(hx, w_in)
    qa_c, ka_c, va_c, qb_c, kb_c, vb_c = project_heads(hc, w_in)
    oa = windowed_sink_attention(apply_rope(qa, cos, sin), apply_rope(ka, cos, sin), va,
                                 ka_c, va_c, a_sink)
    kb_c = rms_norm(kb_c, b_k_norm)
    ob = blocked_global_attention(apply_rope(rms_norm(qb, b_q_norm), cos, sin),
                                  apply_rope(rms_norm(kb, b_k_norm), cos, sin), vb, kb_c, vb_c)
    out_x = merge_head_groups(oa, ob, a_out_norm, b_out_norm, w_out)
    if not with_ctx_out:
        return out_x, None
    oa_c = context_attention(qa_c, ka_c, va_c, a_sink)
    ob_c = context_attention(rms_norm(qb_c, b_q_norm), kb_c, vb_c, None)
    return out_x, merge_head_groups(oa_c, ob_c, a_out_norm, b_out_norm, w_out)

def hierarchical_moe(h, w_group, b_group, w_router, b_router, w_gate, w_up, w_down):
    g_logits = (h @ w_group + b_group).astype(jnp.float32)
    g_prob = jax.nn.softmax(g_logits, axis=-1)
    g_idx = jnp.argmax(g_logits, axis=-1)
    g_w = jnp.take_along_axis(g_prob, g_idx[..., None], axis=-1)
    e_logits = (h @ w_router + b_router).astype(jnp.float32)
    e_logits = e_logits.reshape(*h.shape[:-1], N_GROUPS, EXPERTS_PER_GROUP)
    sel = jnp.broadcast_to(g_idx[..., None, None], h.shape[:-1] + (1, EXPERTS_PER_GROUP))
    e_logits = jnp.take_along_axis(e_logits, sel, axis=-2)[..., 0, :]
    e_prob = jax.nn.softmax(e_logits, axis=-1)
    top_p, top_i = lax.top_k(e_prob, TOP_K_IN_GROUP)
    weights = g_w * top_p / jnp.sum(top_p, axis=-1, keepdims=True)
    expert_id = g_idx[..., None] * EXPERTS_PER_GROUP + top_i
    combine = jnp.sum(jax.nn.one_hot(expert_id, N_EXPERTS, dtype=jnp.float32) * weights[..., None],
                      axis=-2).astype(h.dtype)

    def per_sample(args):
        hs, cs = args
        gate = jnp.einsum('td,edf->tef', hs, w_gate)
        up = jnp.einsum('td,edf->tef', hs, w_up)
        act = jax.nn.silu(gate) * up * cs[..., None]
        return jnp.einsum('tef,efd->td', act, w_down)

    return lax.map(per_sample, (h, combine))

def setup_inputs(seed: int = 0) -> dict:
    key = jax.random.key(seed)
    ks = jax.random.split(key, 24)
    L, D = DEPTH, D_MODEL

    def normal(k, shape, scale):
        return jax.random.normal(k, shape, dtype=jnp.float32) * scale

    def gain(k, shape):
        return 1.0 + normal(k, shape, 0.02)

    return {
        'x': normal(ks[0], (BATCH, SEQ, D), 1.0),
        'c': normal(ks[1], (BATCH, D), 1.0),
        'ctx': normal(ks[2], (BATCH, CTX_LEN, D), 1.0),
        'c_ctx': normal(ks[3], (D,), 1.0),
        'w_mod': normal(ks[4], (L, D, 6 * D), 0.5 * D ** -0.5),
        'b_mod': normal(ks[5], (L, 6 * D), 0.02),
        'attn_pre_norm': gain(ks[6], (L, D)),
        'attn_post_norm': gain(ks[7], (L, D)),
        'w_in': normal(ks[8], (L, D, IN_DIM), D ** -0.5),
        'a_sink': normal(ks[9], (L, A_Q_HEADS), 0.5),
        'b_q_norm': gain(ks[10], (L, HEAD_DIM)),
        'b_k_norm': gain(ks[11], (L, HEAD_DIM)),
        'a_out_norm': gain(ks[12], (L, A_Q_DIM)),
        'b_out_norm': gain(ks[13], (L, B_Q_DIM)),
        'w_out': normal(ks[14], (L, MIX_DIM, D), MIX_DIM ** -0.5),
        'ffn_pre_norm': gain(ks[15], (L, D)),
        'ffn_post_norm': gain(ks[16], (L, D)),
        'w_group': normal(ks[17], (L, D, N_GROUPS), D ** -0.5),
        'b_group': normal(ks[18], (L, N_GROUPS), 0.01),
        'w_router': normal(ks[19], (L, D, N_EXPERTS), D ** -0.5),
        'b_router': normal(ks[20], (L, N_EXPERTS), 0.01),
        'w_gate': normal(ks[21], (L, N_EXPERTS, D, EXPERT_FF), D ** -0.5),
        'w_up': normal(ks[22], (L, N_EXPERTS, D, EXPERT_FF), D ** -0.5),
        'w_down': normal(ks[23], (L, N_EXPERTS, EXPERT_FF, D), EXPERT_FF ** -0.5),
    }

def reference(x, c, ctx, c_ctx, w_mod, b_mod, attn_pre_norm, attn_post_norm, w_in, a_sink,
              b_q_norm, b_k_norm, a_out_norm, b_out_norm, w_out, ffn_pre_norm, ffn_post_norm,
              w_group, b_group, w_router, b_router, w_gate, w_up, w_down):
    rows = x.shape[1] // GRID_W
    cos, sin = axial_rope_tables(rows)
    silu_c = jax.nn.silu(c)
    silu_c_ctx = jax.nn.silu(c_ctx)
    for l in range(DEPTH):
        last = l == DEPTH - 1
        mod_x = (silu_c @ w_mod[l] + b_mod[l])[:, None, :]
        mod_c = (silu_c_ctx @ w_mod[l] + b_mod[l])[None, None, :]
        sh1, sc1, g1, sh2, sc2, g2 = jnp.split(mod_x, 6, axis=-1)
        csh1, csc1, cg1, csh2, csc2, cg2 = jnp.split(mod_c, 6, axis=-1)
        hx = rms_norm(x, attn_pre_norm[l]) * (1 + sc1) + sh1
        hc = rms_norm(ctx, attn_pre_norm[l]) * (1 + csc1) + csh1
        ox, oc = token_mixing(hx, hc, w_in[l], a_sink[l], b_q_norm[l], b_k_norm[l], a_out_norm[l],
                              b_out_norm[l], w_out[l], cos, sin, not last)
        x = x + g1 * rms_norm(ox, attn_post_norm[l])
        hx = rms_norm(x, ffn_pre_norm[l]) * (1 + sc2) + sh2
        fx = hierarchical_moe(hx, w_group[l], b_group[l], w_router[l], b_router[l],
                              w_gate[l], w_up[l], w_down[l])
        x = x + g2 * rms_norm(fx, ffn_post_norm[l])
        if not last:
            ctx = ctx + cg1 * rms_norm(oc, attn_post_norm[l])
            hc = rms_norm(ctx, ffn_pre_norm[l]) * (1 + csc2) + csh2
            fc = hierarchical_moe(hc, w_group[l], b_group[l], w_router[l], b_router[l],
                                  w_gate[l], w_up[l], w_down[l])
            ctx = ctx + cg2 * rms_norm(fc, ffn_post_norm[l])
    return x


_drawn_inputs = setup_inputs


def setup_inputs(seed=0):
    import zlib

    import numpy as np

    out = dict(_drawn_inputs(seed))
    spreads = {}
    factors = {'attn_pre_norm': 3.969,
     'attn_post_norm': 3.997,
     'a_sink': 8.0,
     'b_q_norm': 8.0,
     'b_k_norm': 8.0,
     'a_out_norm': 3.803,
     'b_out_norm': 4.438,
     'ffn_post_norm': 8.0,
     'b_router': 4.312}
    for name, (base, spread) in spreads.items():
        noise = np.random.default_rng([zlib.crc32(name.encode()), seed]).standard_normal(out[name].shape)
        drawn = base * np.exp(spread * noise) if base else spread * noise
        out[name] = jnp.asarray(drawn.astype(out[name].dtype))
    for name, factor in factors.items():
        out[name] = (out[name] * factor).astype(out[name].dtype)
    return out
```

```python
import numpy as np
import concourse.bass as bass
from concourse import mybir
from contextlib import ExitStack

F32 = mybir.dt.float32
F32R = mybir.dt.float32r
BF16 = mybir.dt.bfloat16
I32 = mybir.dt.int32
ALU = mybir.AluOpType
ACT = mybir.ActivationFunctionType
AX = mybir.AxisListType

P = 128
D = 1024
SEQ, CTX = 512, 256
NT, NC = SEQ // P, CTX // P
KEYS = SEQ + CTX
NKB = KEYS // P
KD = D // P
IN_DIM = 1536
HD = 64
HEADS = 16
KVH = 4
NG, EPG = 4, 8
NE = NG * EPG
FF = 512
KF = FF // P
EPS = 1e-6
NEG = -1e30
CHUNK = 512
NMOD = 6 * D // CHUNK
CAP = 64
PAIRS = NE // 2
ROUNDS = SEQ // CAP
SCALE = HD ** -0.5
GRID_W = 64
THETA = 10000.0

CST = {}
_at = 0
for _name, _width in (("ident", P), ("cos", NT * HD), ("sin", NT * HD), ("selb", P), ("sel2", 2),
                      ("iota", CAP), ("rev", EPG), ("half", 8), ("prev", P), ("next", P), ("before", P)):
    CST[_name] = (_at, _at + _width)
    _at += _width
CST_WIDTH = _at
CST_KEPT = CST["prev"][0]


def shape_constants():
    t = np.zeros((P, CST_WIDTH), np.float32)
    i, j = np.arange(P)[:, None], np.arange(P)[None, :]

    def put(name, v):
        t[:, CST[name][0]:CST[name][1]] = v

    put("ident", (i == j).astype(np.float32))
    axis = HD // 2
    inv = (THETA ** (-np.arange(0, axis, 2, dtype=np.float32) / axis)).astype(np.float32)
    tok = np.arange(SEQ)
    ang = np.concatenate([(tok // GRID_W).astype(np.float32)[:, None] * inv,
                          (tok % GRID_W).astype(np.float32)[:, None] * inv], axis=1)
    cos = np.repeat(np.cos(ang), 2, axis=1).reshape(NT, P, HD)
    sin = np.repeat(np.sin(ang), 2, axis=1).reshape(NT, P, HD)
    sin[:, :, 0::2] *= -1
    put("cos", cos.transpose(1, 0, 2).reshape(P, -1))
    put("sin", sin.transpose(1, 0, 2).reshape(P, -1))
    put("selb", np.repeat((np.arange(P) % 32 == 0)[:, None], P, axis=1))
    put("sel2", np.stack([np.arange(P) % 32 == 0, np.arange(P) % 32 == 1], axis=1))
    put("iota", np.arange(CAP)[None, :])
    put("rev", EPG - np.arange(EPG)[None, :])
    put("half", -0.5)
    put("prev", np.where(j >= i, 0.0, NEG))
    put("next", np.where(j <= i, 0.0, NEG))
    put("before", (i < j).astype(np.float32))
    return t


def backbone_layer(nc, x, c, ctx_tok, c_ctx, w_mod, b_mod, attn_pre, attn_post, w_in, a_sink, bq_norm, bk_norm,
                   a_out, b_out, w_out, ffn_pre, ffn_post, w_group, b_group, w_router, b_router,
                   w_gate, w_up, w_down, cst_dram, out):
    KB = 1024
    BASE = 16512
    END = 229344
    placed = [BASE + 192 * KB]

    def at(name, shape, dt, off):
        return nc.alloc_sbuf_tensor_at(name, shape, dt, offset=BASE + off)

    def keep(name, shape, dt):
        size = int(np.prod(shape[1:])) * (2 if dt == BF16 else 4)
        t = nc.alloc_sbuf_tensor_at(name, shape, dt, offset=placed[0])
        placed[0] += (size + 31) // 32 * 32
        assert placed[0] <= END, (name, placed[0])
        return t

    slot = [at(f"slot{j}", [P, 2, 4, CHUNK], F32, 16 * KB * j) for j in range(6)]
    mslot = [at(f"mslot{j}", [P, KD, CHUNK], F32, 16 * KB * j) for j in range(4)]
    Q = at("Q", [P, HEADS, SEQ], F32R, 32 * KB)
    junk_in = at("junk_in", [P, D], F32, 144 * KB)
    V = at("V", [P, NKB, KVH * HD], F32, 64 * KB)
    pn = at("pn", [P, IN_DIM], F32, 70 * KB)
    QS = at("QS", [P, HEADS, 2 * HD], F32R, 76 * KB)
    rope_tmp = at("rope_tmp", [P, 2, 10, HD], F32, 76 * KB)
    KS = at("KS", [P, KVH, 2, 2 * HD], F32R, 84 * KB)
    gains = at("gains", [P, 10, HD], F32, 88 * KB)
    bmod = at("bmod", [NMOD, CHUNK], F32, 88 * KB + 2560)
    modrow = at("modrow", [P, CHUNK], F32, 88 * KB + 2560 + 2048)
    spad = at("spad", [P, KD, 32], F32, 88 * KB + 2560 + 4096)
    PT = [at(f"PT{j}", [P, 2, NKB, SEQ], F32, o * KB) for j, o in enumerate((70, 0))]
    mix_tmp = at("mix_tmp", [P, D], F32, 64 * KB)
    rest_tmp = at("rest_tmp", [P, D], F32, 68 * KB)
    junk = at("junk", [P, D], F32, 72 * KB)
    grp_junk = at("grp_junk", [P, 512], F32, 158 * KB)
    end_junk = at("end_junk", [P, D], F32, 120 * KB)
    oT = at("oT", [P, KD, SEQ], F32, 80 * KB)
    win = at("win", [P, KD, IN_DIM], F32, 96 * KB)
    wout = at("wout", [P, KD, D], F32, 96 * KB)
    onat = at("onat", [P, NT, D], F32, 128 * KB)
    h2T = at("h2T", [P, KD, SEQ], F32, 128 * KB)
    hT = at("hT", [P, KD, KEYS], F32, 144 * KB)
    Pb = at("Pb", [P, 4, KEYS], F32, 144 * KB)
    oTs = at("oTs", [P, SEQ], F32, 156 * KB)
    xparts = at("xparts", [P, 3, NT, D], BF16, 144 * KB)
    xin = at("xin", [P, NT + NC, D], F32, 168 * KB)
    K = at("K", [P, KVH, 2, KEYS], F32R, 168 * KB)
    x1 = at("x1", [P, NT, D], F32, 168 * KB)
    xn2 = at("xn2", [P, 2, D], F32, 184 * KB)
    acc = at("acc", [P, NT, D], F32, 96 * KB)
    xT = at("xT", [P, KD, P], F32, 112 * KB)
    MT = at("MT", [P, SEQ], F32R, 116 * KB)
    MW = at("MW", [P, NT, 2, CAP], F32, 118 * KB)
    gate_act = at("gate_act", [P, FF], F32, 120 * KB)
    hid = at("hid", [P, FF], F32, 122 * KB)
    hidT = at("hidT", [P, KF, P], F32, 124 * KB)
    M = at("M", [P, NT, 2, CAP], BF16, 126 * KB)
    yH = at("yH", [P, D], F32R, 184 * KB)
    yL = at("yL", [P, D], F32R, 188 * KB)
    r_at = [136 * KB]

    def rt(name, shape, dt=F32):
        size = int(np.prod(shape[1:])) * (2 if dt == BF16 else 4)
        t = at(name, shape, dt, r_at[0])
        r_at[0] += (size + 31) // 32 * 32
        assert r_at[0] <= 144 * KB
        return t

    slotval = rt("slotval", [P, NT, NE + 2])
    cw = rt("cw", [P, NT, NE + 2])
    lg = rt("lg", [P, NT, NG + NE])
    gmax = rt("gmax", [P, NT])
    gexp = rt("gexp", [P, NT, NG])
    gsum = rt("gsum", [P, NT])
    gw = rt("gw", [P, NT])
    g1t = rt("g1t", [P, NT, NG])
    ohg = rt("ohg", [P, NT, NG])
    picked = rt("picked", [P, NT, NG, EPG])
    es = rt("es", [P, NT, EPG])
    e1t = rt("e1t", [P, NT, EPG])
    oh1 = rt("oh1", [P, NT, EPG])
    oh2 = rt("oh2", [P, NT, EPG])
    m1 = rt("m1", [P, NT])
    m2 = rt("m2", [P, NT])
    mt_ = rt("mt_", [P, NT])
    e21 = rt("e21", [P, NT])
    w1t = rt("w1t", [P, NT])
    w2t = rt("w2t", [P, NT])
    cwe = rt("cwe", [P, NT, EPG])
    mke = rt("mke", [P, NT, EPG])
    maskf = rt("maskf", [P, NT, NE])
    maskb = rt("maskb", [P, NT, NE], BF16)
    cmaxf = rt("cmaxf", [P, 1])
    cmax = rt("cmax", [P, 1], I32)
    wslot = rt("wslot", [P, 1])

    cst = keep("cst", [P, CST_KEPT], F32)
    cst_raw = at("cst_raw", [P, CST_WIDTH - CST_KEPT], F32, 148 * KB)
    identb = keep("identb", [P, P], BF16)
    maskw = keep("maskw", [P, 2, P], BF16)
    beforeb = keep("beforeb", [P, P], BF16)
    onesb = keep("onesb", [P, P], BF16)
    g1p = keep("g1p", [P, D], F32)
    g2p = keep("g2p", [P, D], F32)
    wr = keep("wr", [P, KD, NG + NE], F32)
    rbias = keep("rbias", [P, NG + NE], F32)
    sink = keep("sink", [P, 8], F32)
    stage = keep("stage", [40, P], F32)
    ncol = keep("ncol", [P, 24], F32)
    modcol = keep("modcol", [P, 4, 2, KD], F32)
    NS = 6 + 8 + 4 + 4 + 4
    ss = keep("ss", [P, NS], F32)
    ms = keep("ms", [P, NS], F32)
    rstd = keep("rstd", [P, NS], F32)
    bss = keep("bss", [P, 10], F32)
    bms = keep("bms", [P, 10], F32)
    brs = keep("brs", [P, 10], F32)
    mx = keep("mx", [P, 2], F32)
    nm = keep("nm", [P, 8], F32)
    rs = keep("rs", [P, 64], F32)
    esn = keep("esn", [P, 32], F32)
    neg_sink = keep("neg_sink", [P, 8], F32)
    dens = keep("dens", [P, 2, 8], F32)
    S_IN, S_GRP, S_MIX, S_FFN, S_END = 0, 6, 14, 18, 22

    def k_(name):
        return cst[:, CST[name][0]:CST[name][1]]

    ident = k_("ident")

    ctx = ExitStack()
    with ctx:
        PS = ctx.enter_context(nc.psum_tensor("PS", [P, 8, CHUNK], F32))

        def sem(name):
            return ctx.enter_context(nc.semaphore(name))

        (x_in, stage_in, cst_in, small_in, rowgain_in, w_out_in, x_again, outs) = map(sem, (
            "x_in", "stage_in", "cst_in", "small_in", "rowgain_in", "w_out_in", "x_again", "outs"))
        wmod_in = [sem(f"wmod_in{j}") for j in range(4)]
        w_in_in = [sem(f"w_in_in{n}") for n in range(3)]
        slot_full = [sem(f"slot_full{j}") for j in range(6)]
        slot_used = [sem(f"slot_used{j}") for j in range(6)]
        (act_own, dve_own, pool_own, bf_ready, spad_zero, cols_done, spad_ready, ncol_ready, in_sq, in_rstd, xn_ready,
         mod_done, modrow_ready, modx_done, modx_taken, xt_done, hTx_ready, hTc_ready, qkv_done,
         pn_ready, bsq_ready, brstd_ready, roped, high_ready, heads_ready, stk_t) = map(sem, (
            "act_own", "dve_own", "pool_own", "bf_ready", "spad_zero", "cols_done", "spad_ready", "ncol_ready",
            "in_sq", "in_rstd", "xn_ready", "mod_done", "modrow_ready", "modx_done", "modx_taken",
            "xt_done", "hTx_ready", "hTc_ready", "qkv_done", "pn_ready", "bsq_ready", "brstd_ready",
            "roped", "high_ready", "heads_ready", "stk_t"))
        stk_evac = [sem("stk_evac_act"), sem("stk_evac_dve")]
        (sc_done, nm_ready, p_ready, pt_done, ptl_ready, ptc_ready, sink_ready, av_done, o_evac, ot_done, onat_ready,
         grp_sq, grp_rstd, grp_ready, ont_done, proj_done, mix_sq, mix_rstd, mixed, ffn_sq, ffn_rstd,
         xn2_ready, high_cut, mid_cut, rest_ready, parts_ready, h2t_done, h2T_a, h2T_d, lg_done, gdiff, gexp_ready,
         d21_ready, e21_ready, mask_ready, pos_done, route_ready) = map(sem, (
            "sc_done", "nm_ready", "p_ready", "pt_done", "ptl_ready", "ptc_ready", "sink_ready", "av_done", "o_evac",
            "ot_done", "onat_ready", "grp_sq", "grp_rstd", "grp_ready", "ont_done", "proj_done", "mix_sq",
            "mix_rstd", "mixed", "ffn_sq", "ffn_rstd", "xn2_ready", "high_cut", "mid_cut", "rest_ready",
            "parts_ready", "h2t_done", "h2T_a", "h2T_d", "lg_done", "gdiff", "gexp_ready", "d21_ready",
            "e21_ready", "mask_ready", "pos_done", "route_ready"))
        ont_evac = [sem("ont_evac_act"), sem("ont_evac_dve")]
        (zeroed, M_ready, MW_ready, gx_done, xT_a, xT_d, silu_ready, scat_done, acc_added,
         mwt_done, mt_ready, hid_ready, hidT_done, hidT_ready, yH_ready, y_split, shifted,
         end_sq, end_rstd, end_ready) = map(sem, (
            "zeroed", "M_ready", "MW_ready", "gx_done", "xT_a", "xT_d", "silu_ready",
            "scat_done", "acc_added", "mwt_done", "mt_ready", "hid_ready", "hidT_done", "hidT_ready",
            "yH_ready", "y_split", "shifted", "end_sq", "end_rstd", "end_ready"))
        final_added, y_half = sem("final_added"), sem("y_half")

        block = ctx.enter_context(nc.Block())

        GROUPS = {ti: (range(6) if ti < NT else range(4, 6)) for ti in range(NT + NC)}
        STK = {}
        for ti in range(NT + NC):
            for g in GROUPS[ti]:
                STK[ti, g] = len(STK)

        def stk_count(upto, parity):
            return (upto + 1 - parity) // 2

        UNITS = [(pr, qt, hh) for pr in range(8) for qt in range(NT) for hh in range(2)]

        def window(pr, qt):
            return (max(0, qt - 1), min(NT - 1, qt + 1)) if pr < 4 else (0, NT - 1)

        def kv_head(pr):
            return pr // 2

        def heads_evac(ti, parity, eng, copy):
            for g in GROUPS[ti]:
                n = STK[ti, g]
                if n % 2 != parity:
                    continue
                eng.wait_ge(stk_t, n + 1)
                src = PS[:, 3 * (ti % 2) + g % 3, :]
                cols = slice(ti * P, (ti + 1) * P)
                if g < 4:
                    copy(Q[:, 4 * g:4 * g + 4, cols], src.rearrange("p (h t) -> p h t", h=4)).then_inc(stk_evac[parity], 1)
                else:
                    v = 2 * (g - 4)
                    copy(K[:, v:v + 2, :, cols],
                         src.rearrange("p (v o t) -> p v o t", v=2, o=2)).then_inc(stk_evac[parity], 1)

        def mod_slot(i):
            return i if i < 4 else i % 2

        SMALL = 16 * 8

        @block.sync
        def _(sp):
            row = lambda v, k: v.rearrange("(k p) -> k p", p=P)
            for v, a in ((c[0], 0), (c_ctx, 8), (attn_pre[0], 16), (ffn_pre[0], 24), (a_out[0], 32), (b_out[0], 36)):
                n = v.shape[0] // P
                sp.dma_start(stage[a:a + n, :], row(v, n)).then_inc(stage_in, 16)

            def load_mod(i):
                if i >= 4:
                    sp.wait_ge(mod_done, i - 3 if i < 6 else i - 1)
                sp.dma_start(mslot[mod_slot(i)][:, :, :],
                             w_mod[0][:, i * CHUNK:(i + 1) * CHUNK].rearrange("(k p) n -> p k n", p=P)
                             ).then_inc(wmod_in[mod_slot(i)], 16)

            load_mod(0)
            sp.dma_start(xin[:, 0:NT, :], x[0].rearrange("(t p) d -> p t d", p=P)).then_inc(x_in, 16)
            sp.dma_start(xin[:, NT:, :], ctx_tok[0].rearrange("(t p) d -> p t d", p=P)).then_inc(x_in, 16)
            for i in range(1, 4):
                load_mod(i)
            for n in range(3):
                sp.dma_start(win[:, :, n * 512:(n + 1) * 512],
                             w_in[0][:, n * 512:(n + 1) * 512].rearrange("(k p) n -> p k n", p=P)
                             ).then_inc(w_in_in[n], 16)
            for i in range(4, NMOD):
                load_mod(i)

            def load_slot(j, pair):
                w = (w_gate, w_up, w_down)[j // 2][0]
                rows = w.shape[1] // 2
                for e in range(2):
                    sp.dma_start(slot[j][:, e, :, :].rearrange("p k n -> p (k n)").rearrange(
                                     "p (k n) -> p k n", k=rows // P),
                                 w[bass.ds(pair * 2 + e, 1), (j % 2) * rows:(j % 2 + 1) * rows, :].rearrange(
                                     "a (k p) n -> p (a k) n", p=P)).then_inc(slot_full[j], 16)

            sp.wait_ge(qkv_done, 3 * NT + 2 * NC)
            sp.dma_start(wout[:, :, :], w_out[0].rearrange("(k p) n -> p k n", p=P)).then_inc(w_out_in, 16)
            sp.wait_ge(sc_done, len(UNITS))
            sp.dma_start(x1[:, :, :], x[0].rearrange("(t p) d -> p t d", p=P)).then_inc(x_again, 16)
            sp.wait_ge(av_done, 8)
            for j in range(4):
                load_slot(j, 0)
            sp.wait_ge(proj_done, NT)
            sp.wait_ge(parts_ready, NT)
            sp.wait_ge(ffn_sq, NT)
            load_slot(4, 0)
            load_slot(5, 0)
            with sp.Fori(1, PAIRS) as p:
                for j in range(6):
                    sp.wait_ge(slot_used[j], p)
                    load_slot(j, p)
            sp.wait_ge(route_ready, 1)
            fullest = sp.value_load(cmax[0:1, 0:1], min_val=0, max_val=SEQ)
            with sp.If(fullest > CAP):
                with sp.Fori(1, ROUNDS) as r:
                    with sp.If(fullest > r * CAP):
                        with sp.Fori(0, PAIRS) as p:
                            for j in range(6):
                                sp.wait_ge(slot_used[j], r * PAIRS + p)
                                load_slot(j, p)
            for ti in range(NT):
                sp.wait_ge(end_ready, ti + 1)
                sp.dma_start(out[0, ti * P:(ti + 1) * P, :], acc[:, ti, :]).then_inc(outs, 16)
            sp.wait_ge(outs, 16 * NT)

        @block.tensor
        def _(pe):
            mm, tr = nc.tensor.matmul, nc.tensor.transpose
            pe.wait_ge(stage_in, 96)
            pe.wait_ge(cst_in, 32)
            tr(PS[:, 7, 0:40], stage[:, :], ident[0:40, 0:40]).then_inc(cols_done, 1)

            def mod_chunk(i):
                pe.wait_ge(wmod_in[mod_slot(i)], 16 if i < 4 else 16 * ((i - 4) // 2 + 2))
                if i:
                    pe.wait_ge(modrow_ready, i)
                for kk in range(2):
                    for g in range(4):
                        mm(PS[32 * g:32 * g + 32, 6, :], spad[:, 2 * g + kk, :], mslot[mod_slot(i)][:, 2 * g + kk, :],
                           start=(kk == 0), stop=(kk == 1 and g > 0))
                mm(PS[0:32, 6, :], ident[0:NMOD, i:i + 1].to_broadcast([NMOD, 32]), bmod[:, :],
                   start=False, stop=True).then_inc(mod_done, 1)

            def mod_spread(i):
                pe.wait_ge(modrow_ready, i + 1)
                if i:
                    pe.wait_ge(modx_taken, i)
                else:
                    pe.wait_ge(ncol_ready, 1)
                if i // 2 in (2, 5):
                    last = mm(PS[:, 7, :], k_("selb"), modrow[:, :], start=True, stop=True)
                else:
                    for b in range(4):
                        last = mm(PS[:, 7, 2 * b:2 * b + 2], modrow[:, b * P:(b + 1) * P], k_("sel2"),
                                  start=True, stop=True)
                last.then_inc(modx_done, 1)

            pe.wait_ge(spad_ready, 2)
            pe.wait_ge(small_in, SMALL)
            for i in range(4):
                mod_chunk(i)
                mod_spread(i)
            pe.wait_ge(xn_ready, NT + NC)
            for k in range(KD):
                b = 2 * (k % 3)
                if k >= 3:
                    pe.wait_ge(hTx_ready, k - 2)
                    pe.wait_ge(hTc_ready, k - 2)
                for ti in range(NT + NC):
                    o = PS[:, b + ti // 4, (ti % 4) * P:(ti % 4 + 1) * P]
                    last = tr(o, xin[:, ti, k * P:(k + 1) * P], ident)
                last.then_inc(xt_done, 1)
            pe.wait_ge(hTx_ready, KD)
            pe.wait_ge(hTc_ready, KD)

            def project(ti):
                if ti >= 2:
                    done = STK[ti - 2, 5] + 1
                    pe.wait_ge(stk_evac[0], stk_count(done, 0))
                    pe.wait_ge(stk_evac[1], stk_count(done, 1))
                b = 3 * (ti % 2)
                for n in range(3 if ti < NT else 2):
                    if ti == 0:
                        pe.wait_ge(w_in_in[n], 16)
                    o, lo, hi = ((PS[:, b + n, :], 512 * n, 512 * n + 512) if ti < NT
                                 else (PS[:, b + n, 0:256], 512 + 768 * n, 768 + 768 * n))
                    for k in range(KD):
                        last = mm(o, hT[:, k, ti * P:(ti + 1) * P], win[:, k, lo:hi], start=(k == 0), stop=(k == KD - 1))
                    last.then_inc(qkv_done, 1)
                    if 1 <= ti <= 4 and n < 2:
                        i = 4 + 2 * (ti - 1) + n
                        if n:
                            mod_spread(i - 1)
                        mod_chunk(i)
                if 1 <= ti <= 4:
                    mod_spread(5 + 2 * (ti - 1))

            def head_transposes(ti):
                pe.wait_ge(heads_ready, 2 * (ti + 1))
                for g in GROUPS[ti]:
                    n = STK[ti, g]
                    b = 3 * (ti % 2) + g % 3
                    if g >= 3 and ti < NT:
                        pe.wait_ge(stk_evac[(n - 3) % 2], (n - 3) // 2 + 1)
                    for q in range(4):
                        src = QS[:, 4 * g + q, :] if g < 4 else KS[:, 2 * (g - 4) + q // 2, q % 2, :]
                        last = tr(PS[:, b, q * P:(q + 1) * P], src.bitcast(F32), ident)
                    last.then_inc(stk_t, 1)

            for ti in range(NT + NC):
                project(ti)
                if ti:
                    head_transposes(ti - 1)
            head_transposes(NT + NC - 1)
            pe.wait_ge(stk_evac[0], stk_count(len(STK), 0))
            pe.wait_ge(stk_evac[1], stk_count(len(STK), 1))
            pe.wait_ge(modx_taken, NMOD)

            pe.wait_ge(bf_ready, 1)
            def scores(u):
                pr, qt, hh = UNITS[u]
                if u >= 2:
                    pe.wait_ge(p_ready, u - 1)
                b, kv, h = 2 * (u % 2), kv_head(pr), 2 * pr + hh
                lo, hi = window(pr, qt)
                n = (hi - lo + 1) * P
                q = Q[:, h, qt * P:(qt + 1) * P]
                masks = [(m, jb) for m, jb in ((0, qt - 1), (1, qt + 1)) if pr < 4 and 0 <= jb < NT]
                o = PS[:, b, CHUNK - n:]
                mm(o, q, K[:, kv, 0, lo * P:(hi + 1) * P], start=True, stop=False)
                mm(o, q, K[:, kv, 1, lo * P:(hi + 1) * P], start=False, stop=not masks)
                for m, jb in masks:
                    at_ = CHUNK - n + (jb - lo) * P
                    mm(PS[:, b, at_:at_ + P], identb[:, :], maskw[:, m, :], start=False, stop=(m, jb) == masks[-1])
                o = PS[:, b + 1, 0:CTX]
                mm(o, q, K[:, kv, 0, SEQ:], start=True, stop=False)
                mm(o, q, K[:, kv, 1, SEQ:], start=False, stop=True).then_inc(sc_done, 1)

            def prob_transposes(u):
                pr, qt, hh = UNITS[u]
                lo, hi = window(pr, qt)
                pe.wait_ge(p_ready, u + 1)
                if u:
                    pe.wait_ge(ptl_ready, u)
                    pe.wait_ge(ptc_ready, u)
                off = CHUNK - (hi - lo + 1) * P
                for n in range(hi - lo + 1):
                    tr(PS[:, 4, n * P:(n + 1) * P], Pb[:, u % 4, off + n * P:off + (n + 1) * P], ident)
                for n in range(2):
                    last = tr(PS[:, 5, n * P:(n + 1) * P], Pb[:, u % 4, SEQ + n * P:SEQ + (n + 1) * P], ident)
                last.then_inc(pt_done, 1)

            def values(pr, n):
                kv = kv_head(pr)
                if n == 0:
                    pe.wait_ge(ptl_ready, 8 * (pr + 1))
                    pe.wait_ge(ptc_ready, 8 * (pr + 1))
                    if pr:
                        pe.wait_ge(o_evac, pr)
                kb = (4, 0, 1, 2, 3, 5)[n]
                q0, q1 = (0, SEQ) if kb >= 4 or pr >= 4 else (max(0, kb - 1) * P, (min(NT - 1, kb + 1) + 1) * P)
                for hh in range(2):
                    last = mm(PS[64 * hh:64 * hh + 64, 6, q0:q1], V[:, kb, kv * HD:(kv + 1) * HD],
                              PT[pr % 2][:, hh, kb, q0:q1], start=(n == 0), stop=(n == 5))
                if n == 5:
                    last.then_inc(av_done, 1)

            def o_transposes(pr):
                pe.wait_ge(o_evac, pr + 1)
                if pr:
                    pe.wait_ge(onat_ready, pr)
                for qt in range(NT):
                    last = tr(PS[:, 7, qt * P:(qt + 1) * P], oTs[:, qt * P:(qt + 1) * P], ident)
                last.then_inc(ot_done, 1)

            scores(0)
            scores(1)
            for u, (pr, qt, hh) in enumerate(UNITS):
                prob_transposes(u)
                if u + 2 < len(UNITS):
                    scores(u + 2)
                if pr and 1 <= u % 8 <= 6:
                    values(pr - 1, u % 8 - 1)
                if pr and u % 8 == 7:
                    o_transposes(pr - 1)
            for n in range(NKB):
                values(7, n)
            o_transposes(7)

            pe.wait_ge(p_ready, len(UNITS))
            for k in range(KD):
                if k == 0:
                    pe.wait_ge(grp_ready, 4)
                if k == 4:
                    pe.wait_ge(grp_ready, 8)
                if k >= 4:
                    pe.wait_ge(ont_evac[k % 2], (k - 4) // 2 + 1)
                for qt in range(NT):
                    last = tr(PS[:, k % 4, qt * P:(qt + 1) * P], onat[:, qt, k * P:(k + 1) * P], ident)
                last.then_inc(ont_done, 1)
            pe.wait_ge(ont_evac[0], 4)
            pe.wait_ge(ont_evac[1], 4)
            pe.wait_ge(w_out_in, 16)

            def out_project(ti):
                b = 4 + 2 * (ti % 2)
                if ti >= 2:
                    pe.wait_ge(mixed, 2 * (ti - 1))
                for n in range(2):
                    for k in range(KD):
                        last = mm(PS[:, b + n, :], oT[:, k, ti * P:(ti + 1) * P], wout[:, k, n * 512:(n + 1) * 512],
                                  start=(k == 0), stop=(k == KD - 1))
                last.then_inc(proj_done, 1)

            def h2_transposes(ti):
                pe.wait_ge(xn2_ready, ti + 1)
                if ti:
                    pe.wait_ge(h2T_a, ti)
                    pe.wait_ge(h2T_d, ti)
                for k in range(KD):
                    last = tr(PS[:, k // 4, (k % 4) * P:(k % 4 + 1) * P], xn2[:, ti % 2, k * P:(k + 1) * P], ident)
                last.then_inc(h2t_done, 1)

            def logits(ti):
                pe.wait_ge(h2T_a, ti + 1)
                pe.wait_ge(h2T_d, ti + 1)
                w = NG + NE
                for k in range(KD):
                    last = mm(PS[:, 2, ti * w:(ti + 1) * w], h2T[:, k, ti * P:(ti + 1) * P], wr[:, k, :],
                              start=(k == 0), stop=(k == KD - 1))
                last.then_inc(lg_done, 1)

            for ti in range(NT):
                out_project(ti)
                if ti:
                    h2_transposes(ti - 1)
                    logits(ti - 1)
            h2_transposes(NT - 1)
            logits(NT - 1)

            pe.wait_ge(mask_ready, 1)
            for ti in range(NT):
                for tj in range(ti + 1):
                    mm(PS[:, 3, ti * NE:(ti + 1) * NE], beforeb[:, :] if tj == ti else onesb[:, :],
                       maskb[:, tj, :], start=(tj == 0), stop=(tj == ti))
            for tj in range(NT):
                last = mm(PS[:, 3, NT * NE:(NT + 1) * NE], onesb[:, :], maskb[:, tj, :], start=(tj == 0), stop=(tj == NT - 1))
            last.then_inc(pos_done, 1)

            def gather(n):
                pe.wait_ge(M_ready, n + 1)
                for k in range(KD):
                    for part in range(3):
                        for ti in range(NT):
                            last = mm(PS[:, k // 4, (k % 4) * P:(k % 4 + 1) * P],
                                      xparts[:, part, ti, k * P:(k + 1) * P],
                                      M[:, ti, :, :].rearrange("p e c -> p (e c)"),
                                      start=(part == 0 and ti == 0), stop=(part == 2 and ti == NT - 1))
                    if k % 4 == 3:
                        last.then_inc(gx_done, 1)

            SCAT_BANKS = (6, 7, 5)

            def scatter(s17):
                pe.wait_ge(y_split, s17 + 1)
                pe.wait_ge(mt_ready, s17 + 1)
                for s in range(8):
                    if s >= 3:
                        pe.wait_ge(acc_added, s17 * 8 + (s - 2))
                    ti, n = s // 2, s % 2
                    o = PS[:, SCAT_BANKS[s % 3], :]
                    lhs = MT[:, ti * P:(ti + 1) * P]
                    mm(o, lhs, yH[:, n * 512:(n + 1) * 512], start=True, stop=False)
                    mm(o, lhs, yL[:, n * 512:(n + 1) * 512], start=False, stop=True).then_inc(scat_done, 1)

            def product(m, it):
                for k in range(KD):
                    j = 2 * m + k // 4
                    if k % 4 == 0:
                        pe.wait_ge(slot_full[j], 32 * it + 32)
                    for e in range(2):
                        last = mm(PS[CAP * e:CAP * (e + 1), 3 + m, :], xT[:, k, CAP * e:CAP * (e + 1)],
                                  slot[j][:, e, k % 4, :], start=(k == 0), stop=(k == KD - 1))
                    if k % 4 == 3:
                        last.then_inc(slot_used[j], 1)

            def expert_pair(it, s17, more=True):
                pe.wait_ge(xT_a, it + 1)
                pe.wait_ge(xT_d, it + 1)
                pe.wait_ge(hid_ready, it + 1)
                product(0, it)
                scatter(s17)
                pe.wait_ge(MW_ready, it + 1)
                for ti in range(NT):
                    last = tr(PS[:, 2, ti * P:(ti + 1) * P], MW[:, ti, :, :].rearrange("p e c -> p (e c)"), ident)
                last.then_inc(mwt_done, 1)
                product(1, it)
                if more:
                    gather(it + 1)
                pe.wait_ge(hid_ready, it + 2)
                pe.wait_ge(acc_added, s17 * 8 + 8)
                for f in range(KF):
                    last = tr(PS[:, 5, f * P:(f + 1) * P], hid[:, f * P:(f + 1) * P], ident)
                last.then_inc(hidT_done, 1)
                pe.wait_ge(hidT_ready, it + 1)
                for j in (4, 5):
                    wd = slot[j][:, :, :, :].rearrange("p e k n -> p (e k n)").rearrange("p (e k n) -> p e k n", e=2, k=2)
                    pe.wait_ge(slot_full[j], 32 * it + 32)
                    for n in range(2):
                        for f in (2 * (j - 4), 2 * (j - 4) + 1):
                            for e in range(2):
                                last = mm(PS[CAP * e:CAP * (e + 1), 6 + n, :], hidT[:, f, CAP * e:CAP * (e + 1)],
                                          wd[:, e, f % 2, n * 512:(n + 1) * 512], start=(f == 0), stop=(f == KF - 1))
                        if j == 5 and n == 0:
                            last.then_inc(y_half, 1)
                    last.then_inc(slot_used[j], 1)

            def one_round(it0, s0):
                gather(it0)
                with pe.Fori(0, PAIRS - 1) as p:
                    expert_pair(it0 + p, s0 + p)
                expert_pair(it0 + PAIRS - 1, s0 + PAIRS - 1, more=False)
                scatter(s0 + PAIRS)

            one_round(0, 0)
            fullest = pe.value_load(cmax[0:1, 0:1], min_val=0, max_val=SEQ)
            with pe.If(fullest > CAP):
                with pe.Fori(1, ROUNDS) as r:
                    with pe.If(fullest > r * CAP):
                        one_round(r * PAIRS, r * (PAIRS + 1))

        @block.scalar
        def _(act):
            fn = nc.scalar.activation
            act.dma_start(cst[:, :], cst_dram[:, 0:CST_KEPT]).then_inc(cst_in, 16)
            act.dma_start(cst_raw[:, :], cst_dram[:, CST_KEPT:]).then_inc(cst_in, 16)

            def spread(v, shape):
                return v.rearrange("(a n) -> a n", a=1).to_broadcast(shape)

            act.dma_start(bmod[:, :], b_mod[0].rearrange("(i n) -> i n", n=CHUNK)).then_inc(small_in, 16)
            act.dma_start(wr[:, :, 0:NG], w_group[0].rearrange("(k p) n -> p k n", p=P)).then_inc(small_in, 16)
            act.dma_start(wr[:, :, NG:], w_router[0].rearrange("(k p) n -> p k n", p=P)).then_inc(small_in, 16)
            act.dma_start(rbias[:, 0:NG], spread(b_group[0], [P, NG])).then_inc(small_in, 16)
            act.dma_start(rbias[:, NG:], spread(b_router[0], [P, NE])).then_inc(small_in, 16)
            act.dma_start(sink[:, :], spread(a_sink[0], [P, 8])).then_inc(small_in, 16)
            act.dma_start(gains[:, 0, :], spread(bq_norm[0], [P, HD])).then_inc(small_in, 16)
            act.dma_start(gains[:, 8, :], spread(bk_norm[0], [P, HD])).then_inc(small_in, 16)
            act.dma_start(g1p[:, :], spread(attn_post[0], [P, D])).then_inc(rowgain_in, 16)
            act.dma_start(g2p[:, :], spread(ffn_post[0], [P, D])).then_inc(rowgain_in, 16)
            act.wait_ge(cols_done, 1)
            act.wait_ge(spad_zero, 1)
            for who in range(2):
                fn(spad[:, :, who], PS[:, 7, 8 * who:8 * who + 8], ACT.Silu).then_inc(spad_ready, 1)
            act.wait_ge(x_in, 32)
            for ti in range(NT + NC):
                if ti:
                    act.wait_ge(in_sq, ti)
                fn(junk_in[:, :], xin[:, ti, :], ACT.Square, accum_out=ss[:, S_IN + ti:S_IN + ti + 1]).then_inc(in_sq, 1)
            act.wait_ge(in_rstd, 1)
            for ti in range(NT + NC):
                fn(xin[:, ti, :], xin[:, ti, :], ACT.Copy, scale=rstd[:, S_IN + ti:S_IN + ti + 1]).then_inc(xn_ready, 1)

            def mod_row(i):
                act.wait_ge(mod_done, i + 1)
                if i:
                    act.wait_ge(modx_done, i)
                fn(modrow[:, :], PS[:, 6, :], ACT.Copy).then_inc(modrow_ready, 1)

            for i in range(4):
                mod_row(i)
            act.wait_ge(modx_taken, 4)
            for k in range(KD):
                act.wait_ge(xt_done, k + 1)
                fn(hT[:, k, SEQ:], PS[:, 2 * (k % 3) + 1, 0:CTX], ACT.Identity,
                   bias=modcol[:, 0, 1, k:k + 1], scale=modcol[:, 1, 1, k:k + 1]).then_inc(hTc_ready, 1)

            def heads_out(ti):
                if ti:
                    act.wait_ge(heads_ready, 2 * ti)
                b = 3 * (ti % 2)
                done = 3 * ti if ti <= NT else 3 * NT + 2 * (ti - NT)
                for n in range(3 if ti < NT else 2):
                    act.wait_ge(qkv_done, done + n + 1)
                    if ti < NT:
                        fn(pn[:, n * 512:(n + 1) * 512], PS[:, b + n, :], ACT.Copy).then_inc(pn_ready, 1)
                    else:
                        fn(pn[:, 512 + 768 * n:768 + 768 * n], PS[:, b + n, 0:256], ACT.Copy).then_inc(pn_ready, 1)
                    if 1 <= ti <= 4 and n < 2:
                        mod_row(4 + 2 * (ti - 1) + n)
                act.wait_ge(pn_ready, done + (3 if ti < NT else 2))
                pg = pn[:, :].rearrange("p (g s) -> p g s", g=2)
                fn(V[:, ti, :].rearrange("p (g s) -> p g s", g=2), pg[:, :, 640:768], ACT.Copy).then_inc(heads_ready, 1)
                if ti:
                    heads_evac(ti - 1, 0, act, act_copy)
                act.wait_ge(roped, ti + 1)
                if ti < NT:
                    fn(QS[:, :, 0:HD].rearrange("p (g h) d -> p g h d", g=2),
                       pg[:, :, 0:512].rearrange("p g (h d) -> p g h d", d=HD), ACT.Copy)
                for g in range(2):
                    src = pg[:, g, 512:640].rearrange("p (v o d) -> p v o d", v=2, o=1).to_broadcast([P, 2, 2, HD])
                    last = fn(KS[:, 2 * g:2 * g + 2, 0, :].rearrange("p v (o d) -> p v o d", o=2), src, ACT.Copy)
                last.then_inc(high_ready, 1)

            act_copy = lambda o, i: fn(o, i, ACT.Copy)
            for ti in range(NT + NC):
                heads_out(ti)
            heads_evac(NT + NC - 1, 0, act, act_copy)

            def context_probs(u):
                pr, qt, hh = UNITS[u]
                act.wait_ge(pt_done, u + 1)
                if pr >= 2:
                    act.wait_ge(av_done, pr - 1)
                fn(PT[pr % 2][:, hh, 4:6, qt * P:(qt + 1) * P], PS[:, 5, 0:CTX].rearrange("p (b t) -> p b t", b=2),
                   ACT.Copy).then_inc(ptc_ready, 1)

            def o_copy(pr):
                act.wait_ge(av_done, pr + 1)
                if pr:
                    act.wait_ge(ot_done, pr)
                fn(oTs[:, :], PS[:, 6, :], ACT.Copy).then_inc(o_evac, 1)

            def group_squares(g):
                act.wait_ge(onat_ready, 4 * (g + 1))
                for qt in range(NT):
                    n = g * NT + qt
                    if n:
                        act.wait_ge(grp_sq, n)
                    fn(grp_junk[:, :], onat[:, qt, g * 512:(g + 1) * 512], ACT.Square,
                       accum_out=ss[:, S_GRP + n:S_GRP + n + 1]).then_inc(grp_sq, 1)

            act.wait_ge(small_in, SMALL)
            for u, (pr, qt, hh) in enumerate(UNITS):
                lo, hi = window(pr, qt)
                off = CHUNK - (hi - lo + 1) * P
                act.wait_ge(nm_ready, u + 1)
                if u >= 4:
                    act.wait_ge(pt_done, u - 3)
                S = PS[:, 2 * (u % 2):2 * (u % 2) + 2, :].rearrange("p b n -> p (b n)")
                fn(Pb[:, u % 4, off:], S[:, off:KEYS], ACT.Exp, bias=nm[:, u % 8:u % 8 + 1], scale=SCALE,
                   accum_out=rs[:, u:u + 1]).then_inc(p_ready, 1)
                if pr < 4:
                    h = 2 * pr + hh
                    fn(esn[:, u:u + 1], sink[:, h:h + 1], ACT.Exp, bias=nm[:, u % 8:u % 8 + 1]).then_inc(sink_ready, 1)
                if u:
                    context_probs(u - 1)
                if u % 8 == 7 and pr:
                    o_copy(pr - 1)
                if u == 44:
                    group_squares(0)
            context_probs(len(UNITS) - 1)
            o_copy(7)

            group_squares(1)
            for k in range(0, KD, 2):
                act.wait_ge(ont_done, k + 1)
                fn(oT[:, k, :], PS[:, k % 4, :], ACT.Copy, scale=ncol[:, 16 + k:17 + k]).then_inc(ont_evac[0], 1)

            for ti in range(NT):
                act.wait_ge(proj_done, ti + 1)
                if ti == 0:
                    act.wait_ge(grp_sq, 8)
                else:
                    act.wait_ge(ffn_sq, ti)
                b = 4 + 2 * (ti % 2)
                fn(junk[:, :], PS[:, b:b + 2, :].rearrange("p b n -> p (b n)"), ACT.Square,
                   accum_out=ss[:, S_MIX + ti:S_MIX + ti + 1]).then_inc(mix_sq, 1)
                act.wait_ge(mixed, 2 * ti + 2)
                act.wait_ge(mix_sq, ti + 1)
                fn(junk[:, :], x1[:, ti, :], ACT.Square,
                   accum_out=ss[:, S_FFN + ti:S_FFN + ti + 1]).then_inc(ffn_sq, 1)
                act.wait_ge(ffn_rstd, ti + 1)
                if ti >= 2:
                    act.wait_ge(h2t_done, ti - 1)
                    act.wait_ge(rest_ready, ti - 1)
                fn(xn2[:, ti % 2, :], x1[:, ti, :], ACT.Copy, scale=rstd[:, S_FFN + ti:S_FFN + ti + 1]).then_inc(xn2_ready, 1)
                act.wait_ge(xn2_ready, ti + 1)
                fn(xparts[:, 0, ti, :], xn2[:, ti % 2, :], ACT.Copy).then_inc(high_cut, 1)
                act.wait_ge(h2t_done, ti + 1)
                for k in range(4):
                    last = fn(h2T[:, k, ti * P:(ti + 1) * P], PS[:, 0, k * P:(k + 1) * P], ACT.Identity,
                              bias=modcol[:, 2, 0, k:k + 1], scale=modcol[:, 3, 0, k:k + 1])
                last.then_inc(h2T_a, 1)
                act.wait_ge(rest_ready, ti + 1)
                fn(xparts[:, 1, ti, :], rest_tmp[:, :], ACT.Copy).then_inc(mid_cut, 1)

            act.wait_ge(gdiff, 1)
            fn(gexp[:, :, :], g1t[:, :, :], ACT.Exp).then_inc(gexp_ready, 1)
            act.wait_ge(d21_ready, 1)
            fn(e21[:, :], mt_[:, :], ACT.Exp).then_inc(e21_ready, 1)

            def xT_upper(n):
                act.wait_ge(gx_done, n * 2 + 2)
                for k in range(4, KD):
                    last = fn(xT[:, k, :], PS[:, 1, (k - 4) * P:(k - 3) * P], ACT.Identity,
                              bias=modcol[:, 2, 0, k:k + 1], scale=modcol[:, 3, 0, k:k + 1])
                last.then_inc(xT_a, 1)

            def expert_pair(it, s17, more=True):
                act.wait_ge(slot_used[1], it + 1)
                act.wait_ge(hid_ready, it + 1)
                fn(gate_act[:, :], PS[:, 3, :], ACT.Silu).then_inc(silu_ready, 1)
                if more:
                    xT_upper(it + 1)
                act.wait_ge(scat_done, s17 * 8 + 8)
                for n, done in enumerate((y_half, slot_used[5])):
                    act.wait_ge(done, it + 1)
                    fn(yH[:, n * 512:(n + 1) * 512], PS[:, 6 + n, :], ACT.Copy).then_inc(yH_ready, 1)

            def one_round(it0, s0):
                xT_upper(it0)
                with act.Fori(0, PAIRS - 1) as p:
                    expert_pair(it0 + p, s0 + p)
                expert_pair(it0 + PAIRS - 1, s0 + PAIRS - 1, more=False)

            act.wait_ge(h2T_a, NT)
            one_round(0, 0)
            fullest = act.value_load(cmax[0:1, 0:1], min_val=0, max_val=SEQ)
            with act.If(fullest > CAP):
                with act.Fori(1, ROUNDS) as r:
                    with act.If(fullest > r * CAP):
                        one_round(r * PAIRS, r * (PAIRS + 1))
            for ti in range(NT):
                act.wait_ge(end_sq, ti)
                if ti == 0:
                    act.wait_ge(final_added, 1)
                fn(end_junk[:, :], acc[:, ti, :], ACT.Square,
                   accum_out=ss[:, S_END + ti:S_END + ti + 1]).then_inc(end_sq, 1)

        @block.vector
        def _(dve):
            V_ = nc.vector
            tt, ts, cp = V_.tensor_tensor, V_.tensor_scalar, V_.tensor_copy
            own = [0]

            def then(ins):
                own[0] += 1
                ins.then_inc(dve_own, 1)
                dve.wait_ge(dve_own, own[0])

            dve.wait_ge(cst_in, 32)
            raw = lambda n: cst_raw[:, (CST[n][0] - CST_KEPT):(CST[n][1] - CST_KEPT)]
            cp(identb[:, :], ident)
            cp(maskw[:, 0, :], raw("prev"))
            cp(maskw[:, 1, :], raw("next"))
            cp(beforeb[:, :], raw("before"))
            V_.memset(onesb[:, :], 1.0).then_inc(bf_ready, 1)
            dve.wait_ge(spad_ready, 2)
            cp(ncol[:, :], PS[:, 7, 16:40]).then_inc(ncol_ready, 1)
            dve.wait_ge(small_in, SMALL)
            then(ts(neg_sink[:, :], sink[:, :], -1.0, None, ALU.mult))
            cp(gains[:, 1:8, :], gains[:, 0:1, :].to_broadcast([P, 7, HD]))
            then(cp(gains[:, 9, :], gains[:, 8, :]))

            def mod_take(i):
                dve.wait_ge(modx_done, i + 1)
                part, half = i // 2, i % 2
                if part in (2, 5):
                    g = (g1p if part == 2 else g2p)[:, half * CHUNK:(half + 1) * CHUNK]
                    dve.wait_ge(rowgain_in, 32)
                    tt(g, PS[:, 7, :], g, ALU.mult).then_inc(modx_taken, 1)
                    return
                which = {0: 0, 1: 1, 3: 2, 4: 3}[part]
                for who in range(2):
                    src = PS[:, 7, 0:8].rearrange("p (b w) -> p b w", w=2)[:, :, who]
                    dst = modcol[:, which, who, 4 * half:4 * half + 4]
                    if which % 2 == 0:
                        last = cp(dst, src)
                    else:
                        base = 8 * (which // 2) + 4 * half
                        last = V_.scalar_tensor_tensor(out=dst, in0=src, scalar=1.0, in1=ncol[:, base:base + 4],
                                                       op0=ALU.add, op1=ALU.mult)
                last.then_inc(modx_taken, 1)

            dve.wait_ge(ncol_ready, 1)
            for i in range(4):
                mod_take(i)
            dve.wait_ge(modx_taken, 4)
            for k in range(KD):
                dve.wait_ge(xt_done, k + 1)
                ts(hT[:, k, 0:SEQ], PS[:, 2 * (k % 3), :], modcol[:, 1, 0, k:k + 1], modcol[:, 0, 0, k:k + 1],
                   ALU.mult, ALU.add).then_inc(hTx_ready, 1)

            def heads(ti):
                latent = ti < NT
                done = 3 * (ti + 1) if latent else 3 * NT + 2 * (ti - NT + 1)
                dve.wait_ge(pn_ready, done)
                if ti:
                    dve.wait_ge(stk_t, STK[ti - 1, 5] + 1)
                n0 = 0 if latent else 8
                nb = 10 - n0
                bh = pn[:, 768 + 64 * n0:768 + 640].rearrange("p (h d) -> p h d", d=HD)
                tmp = rope_tmp[:, 0, n0:10, :]
                then(tt(tmp, bh, bh, ALU.mult))
                V_.tensor_reduce(out=bss[:, n0:10], in_=tmp, axis=AX.X, op=ALU.add).then_inc(bsq_ready, 1)
                dve.wait_ge(brstd_ready, ti + 1)
                then(tt(bh, bh, brs[:, n0:10].rearrange("p (h o) -> p h o", o=1).to_broadcast([P, nb, HD]), ALU.mult))
                last = tt(bh, bh, gains[:, n0:10, :], ALU.mult)
                pg = pn[:, :].rearrange("p (g s) -> p g s", g=2)
                if latent:
                    then(last)
                    qk = pg[:, :, 0:640].rearrange("p g (h d) -> p g h d", d=HD)
                    qk2 = pg[:, :, 0:640].rearrange("p g (h i w) -> p g h i w", i=HD // 2, w=2)
                    tm2 = rope_tmp[:, :, :, :].rearrange("p g h (i w) -> p g h i w", w=2)
                    a = CST["sin"][0] + ti * HD
                    sn = cst[:, a:a + HD].rearrange("p (o q i w) -> p o q i w", o=1, q=1, w=2)
                    a = CST["cos"][0] + ti * HD
                    cs = cst[:, a:a + HD].rearrange("p (o q d) -> p o q d", o=1, q=1).to_broadcast([P, 2, 10, HD])
                    for w in range(2):
                        last = tt(tm2[:, :, :, :, w], qk2[:, :, :, :, 1 - w],
                                  sn[:, :, :, :, w].to_broadcast([P, 2, 10, HD // 2]), ALU.mult)
                    then(last)
                    then(tt(qk, qk, cs, ALU.mult))
                    last = tt(qk, qk, rope_tmp[:, :, :, :], ALU.add)
                last.then_inc(roped, 1)
                dve.wait_ge(high_ready, ti + 1)
                if latent:
                    for g in range(2):
                        tt(QS[:, 8 * g:8 * g + 8, HD:], pg[:, g, 0:512].rearrange("p (h d) -> p h d", d=HD),
                           QS[:, 8 * g:8 * g + 8, 0:HD].bitcast(F32), ALU.subtract)
                for g in range(2):
                    src = pg[:, g, 512:640].rearrange("p (v o d) -> p v o d", v=2, o=1).to_broadcast([P, 2, 2, HD])
                    last = tt(KS[:, 2 * g:2 * g + 2, 1, :].rearrange("p v (o d) -> p v o d", o=2), src,
                              KS[:, 2 * g:2 * g + 2, 0, :].rearrange("p v (o d) -> p v o d", o=2).bitcast(F32),
                              ALU.subtract)
                last.then_inc(heads_ready, 1)

            for ti in range(NT + NC):
                heads(ti)
                if ti < 4:
                    mod_take(4 + 2 * ti)
                    mod_take(5 + 2 * ti)
                heads_evac(ti, 1, dve, cp)

            def latent_probs(u):
                pr, qt, hh = UNITS[u]
                lo, hi = window(pr, qt)
                nb = hi - lo + 1
                dve.wait_ge(pt_done, u + 1)
                if pr >= 2:
                    dve.wait_ge(av_done, pr - 1)
                cp(PT[pr % 2][:, hh, lo:hi + 1, qt * P:(qt + 1) * P],
                   PS[:, 4, 0:nb * P].rearrange("p (b t) -> p b t", b=nb)).then_inc(ptl_ready, 1)

            def o_natural(pr):
                rsp = rs[:, 8 * pr:8 * pr + 8]
                den = dens[:, pr % 2, :]
                dve.wait_ge(p_ready, 8 * (pr + 1))
                if pr < 4:
                    dve.wait_ge(sink_ready, 8 * (pr + 1))
                    then(tt(den, rsp, esn[:, 8 * pr:8 * pr + 8], ALU.add))
                    rsp = den
                then(V_.reciprocal(den, rsp))
                dve.wait_ge(ot_done, pr + 1)
                r = den.rearrange("p (q h o) -> p q h o", h=2, o=1).to_broadcast([P, NT, 2, HD])
                tt(onat[:, :, pr * P:(pr + 1) * P].rearrange("p q (h d) -> p q h d", h=2),
                   PS[:, 7, :].rearrange("p (q h d) -> p q h d", q=NT, h=2), r, ALU.mult).then_inc(onat_ready, 1)

            def group_scale(g):
                dve.wait_ge(grp_rstd, g + 1)
                for qt in range(NT):
                    n = S_GRP + g * NT + qt
                    ts(onat[:, qt, g * 512:(g + 1) * 512], onat[:, qt, g * 512:(g + 1) * 512], rstd[:, n:n + 1],
                       None, ALU.mult).then_inc(grp_ready, 1)

            dve.wait_ge(qkv_done, 3 * NT + 2 * NC)
            for u, (pr, qt, hh) in enumerate(UNITS):
                lo, hi = window(pr, qt)
                off = CHUNK - (hi - lo + 1) * P
                S = PS[:, 2 * (u % 2):2 * (u % 2) + 2, :].rearrange("p b n -> p (b n)")
                dve.wait_ge(sc_done, u + 1)
                then(V_.tensor_reduce(out=mx[:, u % 2:u % 2 + 1], in_=S[:, off:KEYS], axis=AX.X, op=ALU.max))
                if u >= 8:
                    dve.wait_ge(p_ready, u - 7)
                    if 8 <= u < 40:
                        dve.wait_ge(sink_ready, u - 7)
                if pr < 4:
                    h = 2 * pr + hh
                    ts(nm[:, u % 8:u % 8 + 1], mx[:, u % 2:u % 2 + 1], -SCALE, neg_sink[:, h:h + 1],
                       ALU.mult, ALU.min).then_inc(nm_ready, 1)
                else:
                    ts(nm[:, u % 8:u % 8 + 1], mx[:, u % 2:u % 2 + 1], -SCALE, None, ALU.mult).then_inc(nm_ready, 1)
                if u:
                    latent_probs(u - 1)
                if u % 8 == 1 and pr >= 2:
                    o_natural(pr - 2)
                if u == 48:
                    group_scale(0)
            latent_probs(len(UNITS) - 1)
            o_natural(6)
            o_natural(7)

            group_scale(1)
            for k in range(1, KD, 2):
                dve.wait_ge(ont_done, k + 1)
                ts(oT[:, k, :], PS[:, k % 4, :], ncol[:, 16 + k:17 + k], None, ALU.mult).then_inc(ont_evac[1], 1)

            dve.wait_ge(x_again, 16)
            for ti in range(NT):
                b = 4 + 2 * (ti % 2)
                dve.wait_ge(mix_rstd, ti + 1)
                if ti:
                    dve.wait_ge(mixed, 2 * ti)
                V_.scalar_tensor_tensor(out=mix_tmp[:, :], in0=PS[:, b:b + 2, :].rearrange("p b n -> p (b n)"),
                                        scalar=rstd[:, S_MIX + ti:S_MIX + ti + 1], in1=g1p[:, :],
                                        op0=ALU.mult, op1=ALU.mult).then_inc(mixed, 1)
                dve.wait_ge(mixed, 2 * ti + 1)
                tt(x1[:, ti, :], x1[:, ti, :], mix_tmp[:, :], ALU.add).then_inc(mixed, 1)
                dve.wait_ge(high_cut, ti + 1)
                if ti:
                    dve.wait_ge(parts_ready, ti)
                tt(rest_tmp[:, :], xn2[:, ti % 2, :], xparts[:, 0, ti, :], ALU.subtract).then_inc(rest_ready, 1)
                dve.wait_ge(h2t_done, ti + 1)
                for k in range(4, KD):
                    last = ts(h2T[:, k, ti * P:(ti + 1) * P], PS[:, 1, (k - 4) * P:(k - 3) * P],
                              modcol[:, 3, 0, k:k + 1], modcol[:, 2, 0, k:k + 1], ALU.mult, ALU.add)
                last.then_inc(h2T_d, 1)
                dve.wait_ge(mid_cut, ti + 1)
                tt(xparts[:, 2, ti, :], rest_tmp[:, :], xparts[:, 1, ti, :], ALU.subtract).then_inc(parts_ready, 1)

            dve.wait_ge(lg_done, NT)
            w = NG + NE
            then(tt(lg[:, :, :], PS[:, 2, 0:NT * w].rearrange("p (t n) -> p t n", t=NT),
                    rbias[:, :].rearrange("p (o n) -> p o n", o=1).to_broadcast([P, NT, w]), ALU.add))

            def col(v, n):
                return v[:, :].rearrange("p (t o) -> p t o", o=1).to_broadcast([P, NT, n])

            def first_max(one_hot, top, values, n):
                tmp = one_hot
                rev = k_("rev")[:, EPG - n:EPG].rearrange("p (o n) -> p o n", o=1).to_broadcast([P, NT, n])
                then(V_.tensor_reduce(out=top[:, :], in_=values, axis=AX.X, op=ALU.max))
                then(tt(tmp[:, :, :], values, col(top, n), ALU.is_equal))
                then(tt(tmp[:, :, :], tmp[:, :, :], rev, ALU.mult))
                then(V_.tensor_reduce(out=mt_[:, :], in_=tmp[:, :, :], axis=AX.X, op=ALU.max))
                then(tt(one_hot[:, :, :], tmp[:, :, :], col(mt_, n), ALU.is_equal))

            gl = lg[:, :, 0:NG]
            first_max(ohg, gmax, gl, NG)
            tt(g1t[:, :, :], gl, col(gmax, NG), ALU.subtract).then_inc(gdiff, 1)
            el = lg[:, :, NG:].rearrange("p t (g e) -> p t g e", g=NG)
            then(tt(picked[:, :, :, :], el,
                    ohg[:, :, :].rearrange("p t (g o) -> p t g o", o=1).to_broadcast([P, NT, NG, EPG]), ALU.mult))
            then(V_.tensor_reduce(out=es[:, :, :], in_=picked[:, :, :, :].rearrange("p t g e -> p t e g"),
                                  axis=AX.X, op=ALU.add))
            first_max(oh1, m1, es[:, :, :], EPG)
            then(V_.scalar_tensor_tensor(out=e1t[:, :, :], in0=oh1[:, :, :], scalar=NEG, in1=es[:, :, :],
                                         op0=ALU.mult, op1=ALU.add))
            first_max(oh2, m2, e1t[:, :, :], EPG)
            tt(mt_[:, :], m2[:, :], m1[:, :], ALU.subtract).then_inc(d21_ready, 1)
            dve.wait_ge(gexp_ready, 1)
            then(V_.tensor_reduce(out=gsum[:, :], in_=gexp[:, :, :], axis=AX.X, op=ALU.add))
            then(V_.reciprocal(gw[:, :], gsum[:, :]))
            dve.wait_ge(e21_ready, 1)
            then(ts(w2t[:, :], e21[:, :], 1.0, None, ALU.add))
            then(V_.reciprocal(w1t[:, :], w2t[:, :]))
            then(tt(w1t[:, :], w1t[:, :], gw[:, :], ALU.mult))
            then(tt(w2t[:, :], w1t[:, :], e21[:, :], ALU.mult))
            tt(mke[:, :, :], oh1[:, :, :], oh2[:, :, :], ALU.add)
            tt(cwe[:, :, :], oh1[:, :, :], col(w1t, EPG), ALU.mult)
            then(tt(e1t[:, :, :], oh2[:, :, :], col(w2t, EPG), ALU.mult))
            then(tt(cwe[:, :, :], cwe[:, :, :], e1t[:, :, :], ALU.add))

            def by_group(v):
                return v[:, :, :].rearrange("p t (o e) -> p t o e", o=1).to_broadcast([P, NT, NG, EPG])

            gsel = ohg[:, :, :].rearrange("p t (g o) -> p t g o", o=1).to_broadcast([P, NT, NG, EPG])
            tt(maskb[:, :, :].rearrange("p t (g e) -> p t g e", g=NG), gsel, by_group(mke), ALU.mult).then_inc(mask_ready, 1)
            tt(maskf[:, :, :].rearrange("p t (g e) -> p t g e", g=NG), gsel, by_group(mke), ALU.mult)
            V_.memset(cw[:, :, NE:], 0.0)
            V_.memset(slotval[:, :, NE:], -1.0)
            then(tt(cw[:, :, 0:NE].rearrange("p t (g e) -> p t g e", g=NG), gsel, by_group(cwe), ALU.mult))
            dve.wait_ge(pos_done, 1)
            then(V_.scalar_tensor_tensor(out=slotval[:, :, 0:NE],
                                         in0=PS[:, 3, 0:NT * NE].rearrange("p (t n) -> p t n", t=NT), scalar=1.0,
                                         in1=maskf[:, :, :], op0=ALU.add, op1=ALU.mult))
            ts(slotval[:, :, 0:NE], slotval[:, :, 0:NE], -1.0, None, ALU.add).then_inc(shifted, 1)
            then(V_.tensor_reduce(out=cmaxf[:, :], in_=PS[:, 3, NT * NE:(NT + 1) * NE], axis=AX.X, op=ALU.max))
            cp(cmax[:, :], cmaxf[:, :]).then_inc(route_ready, 1)

            def match(pair):
                sv = slotval[:, :, bass.ds(pair * 2, 2)].rearrange("p t (e o) -> p t e o", o=1).to_broadcast([P, NT, 2, CAP])
                io = k_("iota").rearrange("p (o q c) -> p o q c", o=1, q=1).to_broadcast([P, NT, 2, CAP])
                tt(M[:, :, :, :], io, sv, ALU.is_equal).then_inc(M_ready, 1)

            def weigh(pair, n):
                dve.wait_ge(M_ready, n + 1)
                cv = cw[:, :, bass.ds(pair * 2, 2)].rearrange("p t (e o) -> p t e o", o=1).to_broadcast([P, NT, 2, CAP])
                tt(MW[:, :, :, :], M[:, :, :, :], cv, ALU.mult).then_inc(MW_ready, 1)

            def xT_lower(n):
                dve.wait_ge(gx_done, n * 2 + 2)
                for k in range(4):
                    last = ts(xT[:, k, :], PS[:, 0, k * P:(k + 1) * P], modcol[:, 3, 0, k:k + 1],
                              modcol[:, 2, 0, k:k + 1], ALU.mult, ALU.add)
                last.then_inc(xT_d, 1)

            def add_scattered(s17):
                dve.wait_ge(mt_ready, s17 + 1)
                for s in range(8):
                    dve.wait_ge(scat_done, s17 * 8 + (s + 1))
                    ti, n = s // 2, s % 2
                    a = acc[:, ti, n * 512:(n + 1) * 512]
                    tt(a, PS[:, (6, 7, 5)[s % 3], :], a, ALU.add).then_inc(acc_added, 1)

            def expert_pair(pair, it, s17, more=True):
                dve.wait_ge(gx_done, it * 2 + 2)
                dve.wait_ge(MW_ready, it + 1)
                if more:
                    match(pair + 1)
                add_scattered(s17)
                dve.wait_ge(mwt_done, it + 1)
                ts(MT[:, :], PS[:, 2, :], 0.0, None, ALU.not_equal)
                V_.tensor_reduce(out=wslot[:, :], in_=PS[:, 2, :], axis=AX.X, op=ALU.add).then_inc(mt_ready, 1)
                if more:
                    weigh(pair + 1, it + 1)
                dve.wait_ge(silu_ready, it + 1)
                dve.wait_ge(slot_used[3], it + 1)
                dve.wait_ge(mt_ready, s17 + 2)
                V_.scalar_tensor_tensor(out=hid[:, :], in0=gate_act[:, :], scalar=wslot[:, :], in1=PS[:, 4, :],
                                        op0=ALU.mult, op1=ALU.mult).then_inc(hid_ready, 1)
                if more:
                    xT_lower(it + 1)
                dve.wait_ge(hidT_done, it + 1)
                cp(hidT[:, :, :].rearrange("p f s -> p (f s)"), PS[:, 5, :]).then_inc(hidT_ready, 1)
                for n in range(2):
                    dve.wait_ge(yH_ready, 2 * it + (n + 1))
                    last = tt(yL[:, n * 512:(n + 1) * 512], PS[:, 6 + n, :], yH[:, n * 512:(n + 1) * 512].bitcast(F32),
                              ALU.subtract)
                last.then_inc(y_split, 1)

            def one_round(it0, s0):
                match(0)
                weigh(0, it0)
                xT_lower(it0)
                with dve.Fori(0, PAIRS - 1) as p:
                    expert_pair(p, it0 + p, s0 + p)
                expert_pair(PAIRS - 1, it0 + PAIRS - 1, s0 + PAIRS - 1, more=False)
                add_scattered(s0 + PAIRS)

            dve.wait_ge(shifted, 1)
            dve.wait_ge(zeroed, 4)
            one_round(0, 0)
            fullest = dve.value_load(cmax[0:1, 0:1], min_val=0, max_val=SEQ)
            with dve.If(fullest > CAP):
                with dve.Fori(1, ROUNDS) as r:
                    with dve.If(fullest > r * CAP):
                        dve.wait_ge(scat_done, r * 8 * (PAIRS + 1))
                        dve.wait_ge(gx_done, r * 2 * PAIRS)
                        V_.memset(MT[:, :].bitcast(F32), 0.0).then_inc(mt_ready, 1)
                        dve.wait_ge(shifted, r)
                        ts(slotval[:, :, :], slotval[:, :, :], float(-CAP), None, ALU.add).then_inc(shifted, 1)
                        dve.wait_ge(shifted, r + 1)
                        dve.wait_ge(y_split, r * (PAIRS + 1))
                        V_.memset(yL[:, :].bitcast(F32), 0.0).then_inc(y_split, 1)
                        dve.wait_ge(MW_ready, r * PAIRS)
                        one_round(r * PAIRS, r * (PAIRS + 1))
            cp(bss[:, 1:2], bss[:, 1:2]).then_inc(final_added, 1)
            for ti in range(NT):
                dve.wait_ge(end_rstd, ti + 1)
                a = acc[:, ti, :]
                then(V_.scalar_tensor_tensor(out=a, in0=a, scalar=rstd[:, S_END + ti:S_END + ti + 1], in1=g2p[:, :],
                                             op0=ALU.mult, op1=ALU.mult))
                tt(a, a, x1[:, ti, :], ALU.add).then_inc(end_ready, 1)

        @block.gpsimd
        def _(pool):
            G = nc.gpsimd
            own = [0]
            G.memset(spad[:, :, :], 0.0).then_inc(spad_zero, 1)
            pool.wait_ge(cst_in, 32)

            def inverse_root(n, sums, means, roots, a, b, done):
                G.tensor_scalar(means[:, a:b], sums[:, a:b], 1.0 / n, EPS, ALU.mult, ALU.add).then_inc(pool_own, 1)
                own[0] += 1
                pool.wait_ge(pool_own, own[0])
                G.tensor_tensor(roots[:, a:b], means[:, a:b], k_("half")[:, 0:1].to_broadcast([P, b - a]),
                                ALU.pow).then_inc(done, 1)

            pool.wait_ge(in_sq, NT + NC)
            inverse_root(D, ss, ms, rstd, S_IN, S_IN + 6, in_rstd)
            for ti in range(NT + NC):
                pool.wait_ge(bsq_ready, ti + 1)
                inverse_root(HD, bss, bms, brs, 0 if ti < NT else 8, 10, brstd_ready)
            for g in range(2):
                pool.wait_ge(grp_sq, 4 * (g + 1))
                inverse_root(512, ss, ms, rstd, S_GRP + 4 * g, S_GRP + 4 * g + 4, grp_rstd)
            for ti in range(NT):
                pool.wait_ge(mix_sq, ti + 1)
                inverse_root(D, ss, ms, rstd, S_MIX + ti, S_MIX + ti + 1, mix_rstd)
                pool.wait_ge(ffn_sq, ti + 1)
                inverse_root(D, ss, ms, rstd, S_FFN + ti, S_FFN + ti + 1, ffn_rstd)
            pool.wait_ge(proj_done, NT)
            for ti in range(NT):
                G.memset(acc[:, ti, :], 0.0).then_inc(zeroed, 1)
            G.memset(hid[:, :], 0.0).then_inc(hid_ready, 1)
            G.memset(MT[:, :].bitcast(F32), 0.0).then_inc(mt_ready, 1)
            pool.wait_ge(parts_ready, NT)
            pool.wait_ge(h2t_done, NT)
            G.memset(yH[:, :].bitcast(F32), 0.0).then_inc(zeroed, 1)
            G.memset(yL[:, :].bitcast(F32), 0.0).then_inc(y_split, 1)
            for ti in range(NT):
                pool.wait_ge(end_sq, ti + 1)
                inverse_root(D, ss, ms, rstd, S_END + ti, S_END + ti + 1, end_rstd)


_INS = ["x", "c", "ctx", "c_ctx", "w_mod", "b_mod", "attn_pre_norm", "attn_post_norm", "w_in", "a_sink",
        "b_q_norm", "b_k_norm", "a_out_norm", "b_out_norm", "w_out", "ffn_pre_norm", "ffn_post_norm",
        "w_group", "b_group", "w_router", "b_router", "w_gate", "w_up", "w_down"]


def kernel(**inputs):
    import numpy as _np
    import concourse.bacc as _bacc
    from concourse import mybir as _mybir
    from concourse.bass_utils import run_bass_kernel_spmd as _run

    nc = _bacc.Bacc("TRN2", target_bir_lowering=False, num_devices=1)
    arrays, args = {}, []
    for name in _INS + ["shape_constants"]:
        a = shape_constants() if name == "shape_constants" else _np.ascontiguousarray(inputs[name])
        arrays[f"in_{name}"] = a
        args.append(nc.dram_tensor(f"in_{name}", a.shape, _mybir.dt.from_np(a.dtype), kind="ExternalInput").ap())
    args.append(nc.dram_tensor("out_x", (1, SEQ, D), F32, kind="ExternalOutput").ap())
    backbone_layer(nc, *args)
    r = _run(nc, [arrays], core_ids=[0])
    return r.results[0]["out_x"]
```

```python
import numpy as np
import concourse.bass as bass
from concourse import mybir
from contextlib import ExitStack

F32 = mybir.dt.float32
F32R = mybir.dt.float32r
BF16 = mybir.dt.bfloat16
I32 = mybir.dt.int32
ALU = mybir.AluOpType
ACT = mybir.ActivationFunctionType
AX = mybir.AxisListType

P = 128
D = 1024
SEQ, CTX = 512, 256
NT, NC = SEQ // P, CTX // P
KEYS = SEQ + CTX
NKB = KEYS // P
KD = D // P
IN_DIM = 1536
HD = 64
HEADS = 16
KVH = 4
NG, EPG = 4, 8
NE = NG * EPG
FF = 512
KF = FF // P
EPS = 1e-6
NEG = -1e30
CHUNK = 512
NMOD = 6 * D // CHUNK
CAP = 64
PAIRS = NE // 2
ROUNDS = SEQ // CAP
SCALE = HD ** -0.5
GRID_W = 64
THETA = 10000.0

CST = {}
_at = 0
for _name, _width in (("ident", P), ("cos", NT * HD), ("sin", NT * HD), ("selb", P), ("sel2", 2),
                      ("iota", CAP), ("rev", EPG), ("half", 8), ("prev", P), ("next", P), ("before", P)):
    CST[_name] = (_at, _at + _width)
    _at += _width
CST_WIDTH = _at
CST_KEPT = CST["prev"][0]


def shape_constants():
    t = np.zeros((P, CST_WIDTH), np.float32)
    i, j = np.arange(P)[:, None], np.arange(P)[None, :]

    def put(name, v):
        t[:, CST[name][0]:CST[name][1]] = v

    put("ident", (i == j).astype(np.float32))
    axis = HD // 2
    inv = (THETA ** (-np.arange(0, axis, 2, dtype=np.float32) / axis)).astype(np.float32)
    tok = np.arange(SEQ)
    ang = np.concatenate([(tok // GRID_W).astype(np.float32)[:, None] * inv,
                          (tok % GRID_W).astype(np.float32)[:, None] * inv], axis=1)
    cos = np.repeat(np.cos(ang), 2, axis=1).reshape(NT, P, HD)
    sin = np.repeat(np.sin(ang), 2, axis=1).reshape(NT, P, HD)
    sin[:, :, 0::2] *= -1
    put("cos", cos.transpose(1, 0, 2).reshape(P, -1))
    put("sin", sin.transpose(1, 0, 2).reshape(P, -1))
    put("selb", np.repeat((np.arange(P) % 32 == 0)[:, None], P, axis=1))
    put("sel2", np.stack([np.arange(P) % 32 == 0, np.arange(P) % 32 == 1], axis=1))
    put("iota", np.arange(CAP)[None, :])
    put("rev", EPG - np.arange(EPG)[None, :])
    put("half", -0.5)
    put("prev", np.where(j >= i, 0.0, NEG))
    put("next", np.where(j <= i, 0.0, NEG))
    put("before", (i < j).astype(np.float32))
    return t


def backbone_layer(nc, x, c, ctx_tok, c_ctx, w_mod, b_mod, attn_pre, attn_post, w_in, a_sink, bq_norm, bk_norm,
                   a_out, b_out, w_out, ffn_pre, ffn_post, w_group, b_group, w_router, b_router,
                   w_gate, w_up, w_down, cst_dram, out):
    KB = 1024
    BASE = 16512
    END = 229344
    placed = [BASE + 192 * KB]

    def at(name, shape, dt, off):
        return nc.alloc_sbuf_tensor_at(name, shape, dt, offset=BASE + off)

    def keep(name, shape, dt):
        size = int(np.prod(shape[1:])) * (2 if dt == BF16 else 4)
        t = nc.alloc_sbuf_tensor_at(name, shape, dt, offset=placed[0])
        placed[0] += (size + 31) // 32 * 32
        assert placed[0] <= END, (name, placed[0])
        return t

    slot = [at(f"slot{j}", [P, 2, 4, CHUNK], F32, 16 * KB * j) for j in range(6)]
    mslot = [at(f"mslot{j}", [P, KD, CHUNK], F32, 16 * KB * j) for j in range(4)]
    Q = at("Q", [P, HEADS, SEQ], F32R, 32 * KB)
    junk_in = at("junk_in", [P, D], F32, 144 * KB)
    V = at("V", [P, NKB, KVH * HD], F32, 64 * KB)
    pn = at("pn", [P, IN_DIM], F32, 70 * KB)
    QS = at("QS", [P, HEADS, 2 * HD], F32R, 76 * KB)
    rope_tmp = at("rope_tmp", [P, 2, 10, HD], F32, 76 * KB)
    KS = at("KS", [P, KVH, 2, 2 * HD], F32R, 84 * KB)
    gains = at("gains", [P, 10, HD], F32, 88 * KB)
    bmod = at("bmod", [NMOD, CHUNK], F32, 88 * KB + 2560)
    modrow = at("modrow", [P, CHUNK], F32, 88 * KB + 2560 + 2048)
    spad = at("spad", [P, KD, 32], F32, 88 * KB + 2560 + 4096)
    PT = [at(f"PT{j}", [P, 2, NKB, SEQ], F32, o * KB) for j, o in enumerate((70, 0))]
    mix_tmp = at("mix_tmp", [P, D], F32, 64 * KB)
    rest_tmp = at("rest_tmp", [P, D], F32, 68 * KB)
    junk = at("junk", [P, D], F32, 72 * KB)
    grp_junk = at("grp_junk", [P, 512], F32, 166 * KB)
    end_junk = at("end_junk", [P, D], F32, 120 * KB)
    mixA = at("mixA", [P, D], F32, 76 * KB)
    oT = [at(f"oT{g}", [P, KD // 2, SEQ], F32, o * KB) for g, o in enumerate((24, 40))]
    win = at("win", [P, KD, IN_DIM], F32, 96 * KB)
    wout = at("wout", [P, KD, D], F32, 96 * KB)
    onat = at("onat", [P, NT, D], F32, 128 * KB)
    h2T = at("h2T", [P, KD, SEQ], F32, 128 * KB)
    hT = at("hT", [P, KD, KEYS], F32, 144 * KB)
    Pb = at("Pb", [P, 4, KEYS], F32, 144 * KB)
    oTs = at("oTs", [P, SEQ], F32, 156 * KB)
    xparts = at("xparts", [P, 3, NT, D], BF16, 144 * KB)
    xin = at("xin", [P, NT + NC, D], F32, 168 * KB)
    K = at("K", [P, KVH, 2, KEYS], F32R, 168 * KB)
    x1 = at("x1", [P, NT, D], F32, 168 * KB)
    xn2 = at("xn2", [P, 2, D], F32, 184 * KB)
    acc = at("acc", [P, NT, D], F32, 96 * KB)
    xT = at("xT", [P, KD, P], F32, 112 * KB)
    MT = at("MT", [P, SEQ], F32R, 116 * KB)
    MW = at("MW", [P, NT, 2, CAP], F32, 118 * KB)
    gate_act = at("gate_act", [P, FF], F32, 120 * KB)
    hid = at("hid", [P, FF], F32, 122 * KB)
    hidT = at("hidT", [P, KF, P], F32, 124 * KB)
    M = at("M", [P, NT, 2, CAP], BF16, 126 * KB)
    yH = at("yH", [P, D], F32R, 184 * KB)
    yL = at("yL", [P, D], F32R, 188 * KB)
    r_at = [136 * KB]

    def rt(name, shape, dt=F32):
        size = int(np.prod(shape[1:])) * (2 if dt == BF16 else 4)
        t = at(name, shape, dt, r_at[0])
        r_at[0] += (size + 31) // 32 * 32
        assert r_at[0] <= 144 * KB
        return t

    slotval = rt("slotval", [P, NT, NE + 2])
    cw = rt("cw", [P, NT, NE + 2])
    lg = rt("lg", [P, NT, NG + NE])
    gmax = rt("gmax", [P, NT])
    gexp = rt("gexp", [P, NT, NG])
    gsum = rt("gsum", [P, NT])
    gw = rt("gw", [P, NT])
    g1t = rt("g1t", [P, NT, NG])
    ohg = rt("ohg", [P, NT, NG])
    picked = rt("picked", [P, NT, NG, EPG])
    es = rt("es", [P, NT, EPG])
    e1t = rt("e1t", [P, NT, EPG])
    oh1 = rt("oh1", [P, NT, EPG])
    oh2 = rt("oh2", [P, NT, EPG])
    m1 = rt("m1", [P, NT])
    m2 = rt("m2", [P, NT])
    mt_ = rt("mt_", [P, NT])
    e21 = rt("e21", [P, NT])
    w1t = rt("w1t", [P, NT])
    w2t = rt("w2t", [P, NT])
    cwe = rt("cwe", [P, NT, EPG])
    mke = rt("mke", [P, NT, EPG])
    maskf = rt("maskf", [P, NT, NE])
    maskb = rt("maskb", [P, NT, NE], BF16)
    cmaxf = rt("cmaxf", [P, 1])
    cmax = rt("cmax", [P, 1], I32)
    wslot = rt("wslot", [P, 1])

    cst = keep("cst", [P, CST_KEPT], F32)
    cst_raw = at("cst_raw", [P, CST_WIDTH - CST_KEPT], F32, 148 * KB)
    identb = keep("identb", [P, P], BF16)
    maskw = keep("maskw", [P, 2, P], BF16)
    beforeb = keep("beforeb", [P, P], BF16)
    onesb = keep("onesb", [P, P], BF16)
    g1p = keep("g1p", [P, D], F32)
    g2p = keep("g2p", [P, D], F32)
    wr = keep("wr", [P, KD, NG + NE], F32)
    rbias = keep("rbias", [P, NG + NE], F32)
    sink = keep("sink", [P, 8], F32)
    stage = keep("stage", [40, P], F32)
    ncol = keep("ncol", [P, 24], F32)
    modcol = keep("modcol", [P, 4, 2, KD], F32)
    NS = 6 + 8 + 4 + 4 + 4
    ss = keep("ss", [P, NS], F32)
    ms = keep("ms", [P, NS], F32)
    rstd = keep("rstd", [P, NS], F32)
    bss = keep("bss", [P, 10], F32)
    bms = keep("bms", [P, 10], F32)
    brs = keep("brs", [P, 10], F32)
    mx = keep("mx", [P, 2], F32)
    nm = keep("nm", [P, 8], F32)
    rs = keep("rs", [P, 64], F32)
    esn = keep("esn", [P, 32], F32)
    neg_sink = keep("neg_sink", [P, 8], F32)
    dens = keep("dens", [P, 2, 8], F32)
    S_IN, S_GRP, S_MIX, S_FFN, S_END = 0, 6, 14, 18, 22

    def k_(name):
        return cst[:, CST[name][0]:CST[name][1]]

    ident = k_("ident")

    ctx = ExitStack()
    with ctx:
        PS = ctx.enter_context(nc.psum_tensor("PS", [P, 8, CHUNK], F32))

        def sem(name):
            return ctx.enter_context(nc.semaphore(name))

        (x_in, stage_in, cst_in, small_in, rowgain_in, w_out_in, x_again, outs) = map(sem, (
            "x_in", "stage_in", "cst_in", "small_in", "rowgain_in", "w_out_in", "x_again", "outs"))
        wmod_in = [sem(f"wmod_in{j}") for j in range(4)]
        w_in_in = [sem(f"w_in_in{n}") for n in range(3)]
        slot_full = [sem(f"slot_full{j}") for j in range(6)]
        slot_used = [sem(f"slot_used{j}") for j in range(6)]
        (act_own, dve_own, pool_own, bf_ready, spad_zero, cols_done, spad_ready, ncol_ready, in_sq, in_rstd, xn_ready,
         mod_done, modrow_ready, modx_done, modx_taken, xt_done, hTx_ready, hTc_ready, qkv_done,
         pn_ready, bsq_ready, brstd_ready, roped, high_ready, heads_ready, stk_t) = map(sem, (
            "act_own", "dve_own", "pool_own", "bf_ready", "spad_zero", "cols_done", "spad_ready", "ncol_ready",
            "in_sq", "in_rstd", "xn_ready", "mod_done", "modrow_ready", "modx_done", "modx_taken",
            "xt_done", "hTx_ready", "hTc_ready", "qkv_done", "pn_ready", "bsq_ready", "brstd_ready",
            "roped", "high_ready", "heads_ready", "stk_t"))
        stk_evac = [sem("stk_evac_act"), sem("stk_evac_dve")]
        (sc_done, nm_ready, p_ready, pt_done, ptl_ready, ptc_ready, sink_ready, av_done, o_evac, ot_done, onat_ready,
         grp_sq, grp_rstd, oT_ready, ont_done, mix_sq, mix_rstd, mixed, ffn_sq, ffn_rstd,
         xn2_ready, high_cut, mid_cut, rest_ready, parts_ready, h2t_done, h2T_a, h2T_d, lg_done, gdiff, gexp_ready,
         d21_ready, e21_ready, mask_ready, pos_done, route_ready) = map(sem, (
            "sc_done", "nm_ready", "p_ready", "pt_done", "ptl_ready", "ptc_ready", "sink_ready", "av_done", "o_evac",
            "ot_done", "onat_ready", "grp_sq", "grp_rstd", "oT_ready", "ont_done", "mix_sq",
            "mix_rstd", "mixed", "ffn_sq", "ffn_rstd", "xn2_ready", "high_cut", "mid_cut", "rest_ready",
            "parts_ready", "h2t_done", "h2T_a", "h2T_d", "lg_done", "gdiff", "gexp_ready", "d21_ready",
            "e21_ready", "mask_ready", "pos_done", "route_ready"))
        proj_done = [sem("projA_done"), sem("projB_done")]
        (zeroed, M_ready, MW_ready, gx_done, xT_a, xT_d, silu_ready, scat_done, acc_added,
         mwt_done, mt_ready, hid_ready, hidT_done, hidT_ready, yH_ready, y_split, shifted,
         end_sq, end_rstd, end_ready) = map(sem, (
            "zeroed", "M_ready", "MW_ready", "gx_done", "xT_a", "xT_d", "silu_ready",
            "scat_done", "acc_added", "mwt_done", "mt_ready", "hid_ready", "hidT_done", "hidT_ready",
            "yH_ready", "y_split", "shifted", "end_sq", "end_rstd", "end_ready"))
        final_added, y_half, bmod_in, sum_ready, ta_ready, ctx_in, xtx_out, xtc_out = map(sem, (
            "final_added", "y_half", "bmod_in", "sum_ready", "ta_ready", "ctx_in", "xtx_out", "xtc_out"))

        block = ctx.enter_context(nc.Block())

        GROUPS = {ti: (range(6) if ti < NT else range(4, 6)) for ti in range(NT + NC)}
        TURN = [0, 1, NT, 2, 3, NT + 1]
        LAST_TURN = len(TURN) - 1
        MODS = {1: 4, 3: 6, 4: 8}
        BANKS = [3 if ti < NT else 2 for ti in TURN]
        STK = {}
        for ti in TURN:
            for g in GROUPS[ti]:
                STK[ti, g] = len(STK)

        def stk_count(upto, parity):
            return (upto + 1 - parity) // 2

        UNITS = [(pr, qt, hh) for pr in range(8) for qt in range(NT) for hh in range(2)]

        def window(pr, qt):
            return (max(0, qt - 1), min(NT - 1, qt + 1)) if pr < 4 else (0, NT - 1)

        def score_span(pr, qt):
            lo, hi = window(pr, qt)
            n = (hi - lo + 1) * P
            return (0, n + CTX) if n + CTX <= CHUNK else (CHUNK - n, CHUNK + CTX)

        def kv_head(pr):
            return pr // 2

        def heads_evac(ti, parity, eng, copy):
            for g in GROUPS[ti]:
                n = STK[ti, g]
                if n % 2 != parity:
                    continue
                eng.wait_ge(stk_t, n + 1)
                src = PS[:, 3 * (TURN.index(ti) % 2) + g % 3, :]
                cols = slice(ti * P, (ti + 1) * P)
                if g < 4:
                    copy(Q[:, 4 * g:4 * g + 4, cols], src.rearrange("p (h t) -> p h t", h=4)).then_inc(stk_evac[parity], 1)
                else:
                    v = 2 * (g - 4)
                    copy(K[:, v:v + 2, :, cols],
                         src.rearrange("p (v o t) -> p v o t", v=2, o=2)).then_inc(stk_evac[parity], 1)

        def mod_slot(i):
            return i if i < 4 else i % 2

        SMALL = 16 * 7

        @block.sync
        def _(sp):
            row = lambda v, k: v.rearrange("(k p) -> k p", p=P)
            for v, a in ((c[0], 0), (c_ctx, 8), (attn_pre[0], 16), (ffn_pre[0], 24), (a_out[0], 32), (b_out[0], 36)):
                n = v.shape[0] // P
                sp.dma_start(stage[a:a + n, :], row(v, n)).then_inc(stage_in, 16)

            def load_mod(i):
                if i >= 4:
                    sp.wait_ge(mod_done, i - 3 if i < 6 else i - 1)
                sp.dma_start(mslot[mod_slot(i)][:, :, :],
                             w_mod[0][:, i * CHUNK:(i + 1) * CHUNK].rearrange("(k p) n -> p k n", p=P)
                             ).then_inc(wmod_in[mod_slot(i)], 16)

            load_mod(0)
            sp.dma_start(xin[:, 0:NT, :], x[0].rearrange("(t p) d -> p t d", p=P)).then_inc(x_in, 16)
            sp.dma_start(xin[:, NT:, :], ctx_tok[0].rearrange("(t p) d -> p t d", p=P)).then_inc(ctx_in, 16)
            for i in range(1, 4):
                load_mod(i)
            for n in range(3):
                sp.dma_start(win[:, :, n * 512:(n + 1) * 512],
                             w_in[0][:, n * 512:(n + 1) * 512].rearrange("(k p) n -> p k n", p=P)
                             ).then_inc(w_in_in[n], 16)
            for i in range(4, NMOD):
                load_mod(i)

            def load_slot(j, pair):
                w = (w_gate, w_up, w_down)[j // 2][0]
                rows = w.shape[1] // 2
                for e in range(2):
                    sp.dma_start(slot[j][:, e, :, :].rearrange("p k n -> p (k n)").rearrange(
                                     "p (k n) -> p k n", k=rows // P),
                                 w[bass.ds(pair * 2 + e, 1), (j % 2) * rows:(j % 2 + 1) * rows, :].rearrange(
                                     "a (k p) n -> p (a k) n", p=P)).then_inc(slot_full[j], 16)

            sp.wait_ge(qkv_done, 3 * NT + 2 * NC)
            sp.dma_start(wout[:, :, :], w_out[0].rearrange("(k p) n -> p k n", p=P)).then_inc(w_out_in, 16)
            sp.wait_ge(sc_done, len(UNITS))
            sp.dma_start(x1[:, :, :], x[0].rearrange("(t p) d -> p t d", p=P)).then_inc(x_again, 16)
            sp.wait_ge(av_done, 8)
            for j in (0, 3, 5):
                load_slot(j, 0)
            sp.wait_ge(proj_done[1], NT)
            load_slot(1, 0)
            load_slot(2, 0)
            sp.wait_ge(parts_ready, NT)
            sp.wait_ge(ffn_sq, NT)
            load_slot(4, 0)
            with sp.Fori(1, PAIRS) as p:
                for j in range(6):
                    sp.wait_ge(slot_used[j], p)
                    load_slot(j, p)
            sp.wait_ge(route_ready, 1)
            fullest = sp.value_load(cmax[0:1, 0:1], min_val=0, max_val=SEQ)
            with sp.If(fullest > CAP):
                with sp.Fori(1, ROUNDS) as r:
                    with sp.If(fullest > r * CAP):
                        with sp.Fori(0, PAIRS) as p:
                            for j in range(6):
                                sp.wait_ge(slot_used[j], r * PAIRS + p)
                                load_slot(j, p)
            for ti in range(NT):
                sp.wait_ge(end_ready, ti + 1)
                sp.dma_start(out[0, ti * P:(ti + 1) * P, :], acc[:, ti, :]).then_inc(outs, 16)
            sp.wait_ge(outs, 16 * NT)

        @block.tensor
        def _(pe):
            mm, tr = nc.tensor.matmul, nc.tensor.transpose
            pe.wait_ge(stage_in, 96)
            pe.wait_ge(cst_in, 32)
            tr(PS[:, 7, 0:40], stage[:, :], ident[0:40, 0:40]).then_inc(cols_done, 1)

            def mod_chunk(i):
                pe.wait_ge(wmod_in[mod_slot(i)], 16 if i < 4 else 16 * ((i - 4) // 2 + 2))
                if i:
                    pe.wait_ge(modrow_ready, i)
                for kk in range(2):
                    for g in range(4):
                        mm(PS[32 * g:32 * g + 32, 6, :], spad[:, 2 * g + kk, :], mslot[mod_slot(i)][:, 2 * g + kk, :],
                           start=(kk == 0), stop=(kk == 1 and g > 0))
                mm(PS[0:32, 6, :], ident[0:NMOD, i:i + 1].to_broadcast([NMOD, 32]), bmod[:, :],
                   start=False, stop=True).then_inc(mod_done, 1)

            def mod_spread(i):
                pe.wait_ge(modrow_ready, i + 1)
                if i:
                    pe.wait_ge(modx_taken, i)
                else:
                    pe.wait_ge(ncol_ready, 1)
                if i // 2 in (2, 5):
                    last = mm(PS[:, 7, :], k_("selb"), modrow[:, :], start=True, stop=True)
                else:
                    for b in range(4):
                        last = mm(PS[:, 7, 2 * b:2 * b + 2], modrow[:, b * P:(b + 1) * P], k_("sel2"),
                                  start=True, stop=True)
                last.then_inc(modx_done, 1)

            pe.wait_ge(spad_ready, 2)
            pe.wait_ge(bmod_in, 16)

            def x_transposes(ks):
                for k in ks:
                    b = 2 * (k % 3)
                    if k >= 3:
                        pe.wait_ge(xtx_out, k - 2)
                        pe.wait_ge(xtc_out, k - 2)
                    for ti in range(NT + NC):
                        o = PS[:, b + ti // 4, (ti % 4) * P:(ti % 4 + 1) * P]
                        last = tr(o, xin[:, ti, k * P:(k + 1) * P], ident)
                    last.then_inc(xt_done, 1)

            for i in (0, 1):
                mod_chunk(i)
                mod_spread(i)
            pe.wait_ge(xn_ready, NT + NC)
            x_transposes(range(0, KD // 2))
            mod_chunk(2)
            x_transposes(range(KD // 2, KD))
            mod_spread(2)
            mod_chunk(3)
            mod_spread(3)
            pe.wait_ge(xtx_out, KD)
            pe.wait_ge(xtc_out, KD)

            def project(t):
                ti = TURN[t]
                if t >= 2:
                    done = STK[TURN[t - 2], 5] + 1
                    pe.wait_ge(stk_evac[0], stk_count(done, 0))
                    pe.wait_ge(stk_evac[1], stk_count(done, 1))
                if ti == NT:
                    pe.wait_ge(hTc_ready, KD)
                b = 3 * (t % 2)
                for n in range(BANKS[t]):
                    if t == 0:
                        pe.wait_ge(w_in_in[n], 16)
                    o, lo, hi = ((PS[:, b + n, :], 512 * n, 512 * n + 512) if ti < NT
                                 else (PS[:, b + n, 0:256], 512 + 768 * n, 768 + 768 * n))
                    for k in range(KD):
                        if t == 0 and n == 0:
                            pe.wait_ge(hTx_ready, k + 1)
                        last = mm(o, hT[:, k, ti * P:(ti + 1) * P], win[:, k, lo:hi], start=(k == 0), stop=(k == KD - 1))
                    last.then_inc(qkv_done, 1)
                    if t in MODS and n < 2:
                        if n:
                            mod_spread(MODS[t])
                        mod_chunk(MODS[t] + n)
                if t in MODS:
                    mod_spread(MODS[t] + 1)

            def head_transposes(t):
                ti = TURN[t]
                pe.wait_ge(heads_ready, 2 * (t + 1))
                for g in GROUPS[ti]:
                    n = STK[ti, g]
                    b = 3 * (t % 2) + g % 3
                    if g >= 3 and ti < NT:
                        pe.wait_ge(stk_evac[(n - 3) % 2], (n - 3) // 2 + 1)
                    for q in range(4):
                        src = QS[:, 4 * g + q, :] if g < 4 else KS[:, 2 * (g - 4) + q // 2, q % 2, :]
                        last = tr(PS[:, b, q * P:(q + 1) * P], src.bitcast(F32), ident)
                    last.then_inc(stk_t, 1)

            for t in range(NT + NC):
                project(t)
                if t == LAST_TURN:
                    mod_spread(NMOD - 2)
                    mod_chunk(NMOD - 1)
                if t:
                    head_transposes(t - 1)
                if t == LAST_TURN - 1:
                    mod_chunk(NMOD - 2)
            mod_spread(NMOD - 1)
            head_transposes(LAST_TURN)
            pe.wait_ge(stk_evac[0], stk_count(len(STK), 0))
            pe.wait_ge(stk_evac[1], stk_count(len(STK), 1))
            pe.wait_ge(modx_taken, NMOD)

            pe.wait_ge(bf_ready, 1)
            def scores(u):
                pr, qt, hh = UNITS[u]
                if u >= 2:
                    pe.wait_ge(p_ready, u - 1)
                kv, h = kv_head(pr), 2 * pr + hh
                lo, hi = window(pr, qt)
                off, end = score_span(pr, qt)
                q = Q[:, h, qt * P:(qt + 1) * P]
                masks = [(m, jb) for m, jb in ((0, qt - 1), (1, qt + 1)) if pr < 4 and 0 <= jb < NT]
                S = PS[:, 2 * (u % 2):2 * (u % 2) + 2, :].rearrange("p b n -> p (b n)")
                if end <= CHUNK:
                    o = S[:, 0:end].rearrange("p (a n) -> p a n", a=2)
                    a = lo * P // CTX
                    keys = lambda part: K[:, kv, part, :].rearrange("p (c n) -> p c n", n=CTX)[:, a::2 - a, :]
                else:
                    o = S[:, off:CHUNK]
                    keys = lambda part: K[:, kv, part, lo * P:(hi + 1) * P]
                mm(o, q, keys(0), start=True, stop=False)
                last = mm(o, q, keys(1), start=False, stop=not masks)
                for m, jb in masks:
                    at_ = off + (jb - lo) * P
                    last = mm(S[:, at_:at_ + P], identb[:, :], maskw[:, m, :], start=False, stop=(m, jb) == masks[-1])
                if end > CHUNK:
                    mm(S[:, CHUNK:end], q, K[:, kv, 0, SEQ:], start=True, stop=False)
                    last = mm(S[:, CHUNK:end], q, K[:, kv, 1, SEQ:], start=False, stop=True)
                last.then_inc(sc_done, 1)

            def prob_transposes(u):
                pr, qt, hh = UNITS[u]
                lo, hi = window(pr, qt)
                pe.wait_ge(p_ready, u + 1)
                if u:
                    pe.wait_ge(ptl_ready, u)
                    pe.wait_ge(ptc_ready, u)
                off, end = score_span(pr, qt)
                for n in range(hi - lo + 1):
                    tr(PS[:, 4, n * P:(n + 1) * P], Pb[:, u % 4, off + n * P:off + (n + 1) * P], ident)
                for n in range(2):
                    last = tr(PS[:, 5, n * P:(n + 1) * P], Pb[:, u % 4, end - CTX + n * P:end - CTX + (n + 1) * P], ident)
                last.then_inc(pt_done, 1)

            def values(pr, n):
                kv = kv_head(pr)
                if n == 0:
                    pe.wait_ge(ptl_ready, 8 * (pr + 1))
                    pe.wait_ge(ptc_ready, 8 * (pr + 1))
                    if pr:
                        pe.wait_ge(o_evac, pr)
                kb = (4, 0, 1, 2, 3, 5)[n]
                q0, q1 = (0, SEQ) if kb >= 4 or pr >= 4 else (max(0, kb - 1) * P, (min(NT - 1, kb + 1) + 1) * P)
                for hh in range(2):
                    last = mm(PS[64 * hh:64 * hh + 64, 6, q0:q1], V[:, kb, kv * HD:(kv + 1) * HD],
                              PT[pr % 2][:, hh, kb, q0:q1], start=(n == 0), stop=(n == 5))
                if n == 5:
                    last.then_inc(av_done, 1)

            def o_transposes(pr):
                pe.wait_ge(o_evac, pr + 1)
                if pr:
                    pe.wait_ge(oT_ready, pr)
                for qt in range(NT):
                    last = tr(PS[:, 7, qt * P:(qt + 1) * P], oTs[:, qt * P:(qt + 1) * P], ident)
                last.then_inc(ot_done, 1)

            def o_again(pr):
                pe.wait_ge(onat_ready, pr + 1)
                for qt in range(NT):
                    last = tr(PS[:, 7, qt * P:(qt + 1) * P], onat[:, qt, pr * P:(pr + 1) * P], ident)
                last.then_inc(ont_done, 1)

            scores(0)
            scores(1)
            for u, (pr, qt, hh) in enumerate(UNITS):
                if pr >= 4:
                    prob_transposes(u)
                if u + 2 < len(UNITS):
                    scores(u + 2)
                if pr < 4:
                    prob_transposes(u)
                if pr and 1 <= u % 8 <= 6:
                    values(pr - 1, u % 8 - 1)
                if pr >= 2 and u % 8 == 3:
                    o_again(pr - 2)
                if pr and u % 8 == 7:
                    o_transposes(pr - 1)
            for n in range(NKB):
                values(7, n)
            o_again(6)

            def out_project(ti, g, halves=(0, 1)):
                for n in halves:
                    if ti and n == 0:
                        pe.wait_ge(sum_ready if g else ta_ready, ti)
                    if ti and g and n:
                        h2_transposes(ti - 1)
                    for k in range(KD // 2):
                        last = mm(PS[:, 4 + 2 * g + n, :], oT[g][:, k, ti * P:(ti + 1) * P],
                                  wout[:, 4 * g + k, n * 512:(n + 1) * 512], start=(k == 0), stop=(k == KD // 2 - 1))
                    if n:
                        last.then_inc(proj_done[g], 1)

            def h2_transposes(ti):
                pe.wait_ge(xn2_ready, ti + 1)
                if ti:
                    pe.wait_ge(h2T_a, ti)
                    pe.wait_ge(h2T_d, ti)
                for k in range(KD):
                    last = tr(PS[:, k // 4, (k % 4) * P:(k % 4 + 1) * P], xn2[:, ti % 2, k * P:(k + 1) * P], ident)
                last.then_inc(h2t_done, 1)

            def logits(ti):
                pe.wait_ge(h2T_a, ti + 1)
                pe.wait_ge(h2T_d, ti + 1)
                w = NG + NE
                for k in range(KD):
                    last = mm(PS[:, 2, ti * w:(ti + 1) * w], h2T[:, k, ti * P:(ti + 1) * P], wr[:, k, :],
                              start=(k == 0), stop=(k == KD - 1))
                last.then_inc(lg_done, 1)

            pe.wait_ge(w_out_in, 16)
            pe.wait_ge(oT_ready, 6)
            pe.wait_ge(ptl_ready, len(UNITS))
            pe.wait_ge(ptc_ready, len(UNITS))
            out_project(0, 0, (0,))
            o_transposes(7)
            out_project(0, 0, (1,))
            o_again(7)
            pe.wait_ge(oT_ready, 8)
            out_project(0, 1)
            for ti in range(1, NT):
                out_project(ti, 0)
                if ti >= 2:
                    logits(ti - 2)
                out_project(ti, 1)
            logits(NT - 2)
            h2_transposes(NT - 1)
            logits(NT - 1)

            pe.wait_ge(mask_ready, 1)
            for ti in range(NT):
                for tj in range(ti + 1):
                    mm(PS[:, 3, ti * NE:(ti + 1) * NE], beforeb[:, :] if tj == ti else onesb[:, :],
                       maskb[:, tj, :], start=(tj == 0), stop=(tj == ti))
            for tj in range(NT):
                last = mm(PS[:, 3, NT * NE:(NT + 1) * NE], onesb[:, :], maskb[:, tj, :], start=(tj == 0), stop=(tj == NT - 1))
            last.then_inc(pos_done, 1)

            def gather(n):
                pe.wait_ge(M_ready, n + 1)
                for k in range(KD):
                    for part in range(3):
                        for ti in range(NT):
                            last = mm(PS[:, k // 4, (k % 4) * P:(k % 4 + 1) * P],
                                      xparts[:, part, ti, k * P:(k + 1) * P],
                                      M[:, ti, :, :].rearrange("p e c -> p (e c)"),
                                      start=(part == 0 and ti == 0), stop=(part == 2 and ti == NT - 1))
                    if k % 4 == 3:
                        last.then_inc(gx_done, 1)

            SCAT_BANKS = (6, 7, 5)

            def scatter(s17):
                pe.wait_ge(y_split, s17 + 1)
                pe.wait_ge(mt_ready, s17 + 1)
                for s in range(8):
                    if s >= 3:
                        pe.wait_ge(acc_added, s17 * 8 + (s - 2))
                    ti, n = s // 2, s % 2
                    o = PS[:, SCAT_BANKS[s % 3], :]
                    lhs = MT[:, ti * P:(ti + 1) * P]
                    mm(o, lhs, yH[:, n * 512:(n + 1) * 512], start=True, stop=False)
                    mm(o, lhs, yL[:, n * 512:(n + 1) * 512], start=False, stop=True).then_inc(scat_done, 1)

            def product(m, it):
                for k in range(KD):
                    j = 2 * m + k // 4
                    if k % 4 == 0:
                        pe.wait_ge(slot_full[j], 32 * it + 32)
                    for e in range(2):
                        last = mm(PS[CAP * e:CAP * (e + 1), 3 + m, :], xT[:, k, CAP * e:CAP * (e + 1)],
                                  slot[j][:, e, k % 4, :], start=(k == 0), stop=(k == KD - 1))
                    if k % 4 == 3:
                        last.then_inc(slot_used[j], 1)

            def expert_pair(it, s17, more=True):
                pe.wait_ge(xT_a, it + 1)
                pe.wait_ge(xT_d, it + 1)
                pe.wait_ge(hid_ready, it + 1)
                product(0, it)
                scatter(s17)
                pe.wait_ge(MW_ready, it + 1)
                for ti in range(NT):
                    last = tr(PS[:, 2, ti * P:(ti + 1) * P], MW[:, ti, :, :].rearrange("p e c -> p (e c)"), ident)
                last.then_inc(mwt_done, 1)
                product(1, it)
                if more:
                    gather(it + 1)
                pe.wait_ge(hid_ready, it + 2)
                pe.wait_ge(acc_added, s17 * 8 + 8)
                for f in range(KF):
                    last = tr(PS[:, 5, f * P:(f + 1) * P], hid[:, f * P:(f + 1) * P], ident)
                last.then_inc(hidT_done, 1)
                pe.wait_ge(hidT_ready, it + 1)
                for j in (4, 5):
                    wd = slot[j][:, :, :, :].rearrange("p e k n -> p (e k n)").rearrange("p (e k n) -> p e k n", e=2, k=2)
                    pe.wait_ge(slot_full[j], 32 * it + 32)
                    for n in range(2):
                        for f in (2 * (j - 4), 2 * (j - 4) + 1):
                            for e in range(2):
                                last = mm(PS[CAP * e:CAP * (e + 1), 6 + n, :], hidT[:, f, CAP * e:CAP * (e + 1)],
                                          wd[:, e, f % 2, n * 512:(n + 1) * 512], start=(f == 0), stop=(f == KF - 1))
                        if j == 5 and n == 0:
                            last.then_inc(y_half, 1)
                    last.then_inc(slot_used[j], 1)

            def one_round(it0, s0):
                gather(it0)
                with pe.Fori(0, PAIRS - 1) as p:
                    expert_pair(it0 + p, s0 + p)
                expert_pair(it0 + PAIRS - 1, s0 + PAIRS - 1, more=False)
                scatter(s0 + PAIRS)

            one_round(0, 0)
            fullest = pe.value_load(cmax[0:1, 0:1], min_val=0, max_val=SEQ)
            with pe.If(fullest > CAP):
                with pe.Fori(1, ROUNDS) as r:
                    with pe.If(fullest > r * CAP):
                        one_round(r * PAIRS, r * (PAIRS + 1))

        @block.scalar
        def _(act):
            fn = nc.scalar.activation
            act.dma_start(cst[:, :], cst_dram[:, 0:CST_KEPT]).then_inc(cst_in, 16)
            act.dma_start(cst_raw[:, :], cst_dram[:, CST_KEPT:]).then_inc(cst_in, 16)

            def spread(v, shape):
                return v.rearrange("(a n) -> a n", a=1).to_broadcast(shape)

            act.dma_start(bmod[:, :], b_mod[0].rearrange("(i n) -> i n", n=CHUNK)).then_inc(bmod_in, 16)
            act.dma_start(wr[:, :, 0:NG], w_group[0].rearrange("(k p) n -> p k n", p=P)).then_inc(small_in, 16)
            act.dma_start(wr[:, :, NG:], w_router[0].rearrange("(k p) n -> p k n", p=P)).then_inc(small_in, 16)
            act.dma_start(rbias[:, 0:NG], spread(b_group[0], [P, NG])).then_inc(small_in, 16)
            act.dma_start(rbias[:, NG:], spread(b_router[0], [P, NE])).then_inc(small_in, 16)
            act.dma_start(sink[:, :], spread(a_sink[0], [P, 8])).then_inc(small_in, 16)
            act.dma_start(gains[:, 0, :], spread(bq_norm[0], [P, HD])).then_inc(small_in, 16)
            act.dma_start(gains[:, 8, :], spread(bk_norm[0], [P, HD])).then_inc(small_in, 16)
            act.dma_start(g1p[:, :], spread(attn_post[0], [P, D])).then_inc(rowgain_in, 16)
            act.dma_start(g2p[:, :], spread(ffn_post[0], [P, D])).then_inc(rowgain_in, 16)
            act.wait_ge(cols_done, 1)
            act.wait_ge(spad_zero, 1)
            for who in range(2):
                fn(spad[:, :, who], PS[:, 7, 8 * who:8 * who + 8], ACT.Silu).then_inc(spad_ready, 1)
            def mod_row(i):
                act.wait_ge(mod_done, i + 1)
                if i:
                    act.wait_ge(modx_done, i)
                fn(modrow[:, :], PS[:, 6, :], ACT.Copy).then_inc(modrow_ready, 1)

            mod_row(0)
            act.wait_ge(x_in, 16)
            for ti in range(NT + NC):
                if ti:
                    act.wait_ge(in_sq, ti)
                if ti == NT:
                    act.wait_ge(ctx_in, 16)
                fn(junk_in[:, :], xin[:, ti, :], ACT.Square, accum_out=ss[:, S_IN + ti:S_IN + ti + 1]).then_inc(in_sq, 1)
            act.wait_ge(in_rstd, 1)
            for ti in range(NT, NT + NC):
                fn(xin[:, ti, :], xin[:, ti, :], ACT.Copy, scale=rstd[:, S_IN + ti:S_IN + ti + 1]).then_inc(xn_ready, 1)

            def ctx_out(ks):
                for k in ks:
                    act.wait_ge(xt_done, k + 1)
                    fn(hT[:, k, SEQ:], PS[:, 2 * (k % 3) + 1, 0:CTX], ACT.Copy).then_inc(xtc_out, 1)

            mod_row(1)
            ctx_out(range(0, KD // 2))
            mod_row(2)
            ctx_out(range(KD // 2, KD))
            mod_row(3)
            act.wait_ge(modx_taken, 4)
            act.wait_ge(xtc_out, KD)
            for k in range(KD):
                fn(hT[:, k, SEQ:], hT[:, k, SEQ:], ACT.Identity,
                   bias=modcol[:, 0, 1, k:k + 1], scale=modcol[:, 1, 1, k:k + 1]).then_inc(hTc_ready, 1)

            def heads_out(t):
                ti = TURN[t]
                if t:
                    act.wait_ge(heads_ready, 2 * t)
                b = 3 * (t % 2)
                done = sum(BANKS[:t])
                for n in range(BANKS[t]):
                    act.wait_ge(qkv_done, done + n + 1)
                    if ti < NT:
                        fn(pn[:, n * 512:(n + 1) * 512], PS[:, b + n, :], ACT.Copy).then_inc(pn_ready, 1)
                    else:
                        fn(pn[:, 512 + 768 * n:768 + 768 * n], PS[:, b + n, 0:256], ACT.Copy).then_inc(pn_ready, 1)
                    if t in MODS and n < 2:
                        mod_row(MODS[t] + n)
                act.wait_ge(pn_ready, done + BANKS[t])
                pg = pn[:, :].rearrange("p (g s) -> p g s", g=2)
                fn(V[:, ti, :].rearrange("p (g s) -> p g s", g=2), pg[:, :, 640:768], ACT.Copy).then_inc(heads_ready, 1)
                if t:
                    heads_evac(TURN[t - 1], 0, act, act_copy)
                if t == LAST_TURN - 1:
                    mod_row(NMOD - 2)
                    mod_row(NMOD - 1)
                act.wait_ge(roped, t + 1)
                if ti < NT:
                    fn(QS[:, :, 0:HD].rearrange("p (g h) d -> p g h d", g=2),
                       pg[:, :, 0:512].rearrange("p g (h d) -> p g h d", d=HD), ACT.Copy)
                for g in range(2):
                    src = pg[:, g, 512:640].rearrange("p (v o d) -> p v o d", v=2, o=1).to_broadcast([P, 2, 2, HD])
                    last = fn(KS[:, 2 * g:2 * g + 2, 0, :].rearrange("p v (o d) -> p v o d", o=2), src, ACT.Copy)
                last.then_inc(high_ready, 1)

            act_copy = lambda o, i: fn(o, i, ACT.Copy)
            for t in range(NT + NC):
                heads_out(t)
            heads_evac(TURN[LAST_TURN], 0, act, act_copy)

            def context_probs(u):
                pr, qt, hh = UNITS[u]
                act.wait_ge(pt_done, u + 1)
                if pr >= 2:
                    act.wait_ge(av_done, pr - 1)
                fn(PT[pr % 2][:, hh, 4:6, qt * P:(qt + 1) * P], PS[:, 5, 0:CTX].rearrange("p (b t) -> p b t", b=2),
                   ACT.Copy).then_inc(ptc_ready, 1)

            def o_copy(pr):
                act.wait_ge(av_done, pr + 1)
                if pr:
                    act.wait_ge(ot_done, pr)
                fn(oTs[:, :], PS[:, 6, :], ACT.Copy).then_inc(o_evac, 1)

            def oT_out(pr):
                act.wait_ge(ont_done, pr + 1)
                fn(oT[pr // 4][:, pr % 4, :], PS[:, 7, :], ACT.Copy, scale=ncol[:, 16 + pr:17 + pr]).then_inc(oT_ready, 1)

            def group_squares(g, tiles=range(NT)):
                act.wait_ge(onat_ready, 4 * (g + 1))
                for qt in tiles:
                    n = g * NT + qt
                    if n:
                        act.wait_ge(grp_sq, n)
                    fn(grp_junk[:, :], onat[:, qt, g * 512:(g + 1) * 512], ACT.Square,
                       accum_out=ss[:, S_GRP + n:S_GRP + n + 1]).then_inc(grp_sq, 1)

            act.wait_ge(small_in, SMALL)
            for u, (pr, qt, hh) in enumerate(UNITS):
                off, end = score_span(pr, qt)
                act.wait_ge(nm_ready, u + 1)
                if u >= 4:
                    act.wait_ge(pt_done, u - 3)
                S = PS[:, 2 * (u % 2):2 * (u % 2) + 2, :].rearrange("p b n -> p (b n)")
                fn(Pb[:, u % 4, off:end], S[:, off:end], ACT.Exp, bias=nm[:, u % 8:u % 8 + 1], scale=SCALE,
                   accum_out=rs[:, u:u + 1]).then_inc(p_ready, 1)
                if pr < 4:
                    h = 2 * pr + hh
                    fn(esn[:, u:u + 1], sink[:, h:h + 1], ACT.Exp, bias=nm[:, u % 8:u % 8 + 1]).then_inc(sink_ready, 1)
                if u:
                    context_probs(u - 1)
                if u % 8 == 7 and pr:
                    o_copy(pr - 1)
                if pr >= 2 and u % 8 == 4:
                    oT_out(pr - 2)
                if 44 <= u < 44 + NT:
                    group_squares(0, [u - 44])
            context_probs(len(UNITS) - 1)

            oT_out(6)
            o_copy(7)

            def mix_a(ti):
                act.wait_ge(proj_done[0], ti + 1)
                act.wait_ge(grp_rstd, 1)
                if ti:
                    act.wait_ge(sum_ready, ti)
                fn(mixA[:, :], PS[:, 4:6, :].rearrange("p b n -> p (b n)"), ACT.Copy,
                   scale=rstd[:, S_GRP + ti:S_GRP + ti + 1]).then_inc(ta_ready, 1)

            oT_out(7)
            mix_a(0)
            group_squares(1)
            for ti in range(NT):
                act.wait_ge(sum_ready, ti + 1)
                if ti:
                    act.wait_ge(ffn_sq, ti)
                fn(junk[:, :], mix_tmp[:, :], ACT.Square,
                   accum_out=ss[:, S_MIX + ti:S_MIX + ti + 1]).then_inc(mix_sq, 1)
                act.wait_ge(mixed, 2 * ti + 2)
                act.wait_ge(mix_sq, ti + 1)
                fn(junk[:, :], x1[:, ti, :], ACT.Square,
                   accum_out=ss[:, S_FFN + ti:S_FFN + ti + 1]).then_inc(ffn_sq, 1)
                act.wait_ge(ffn_rstd, ti + 1)
                if ti >= 2:
                    act.wait_ge(h2t_done, ti - 1)
                    act.wait_ge(rest_ready, ti - 1)
                fn(xn2[:, ti % 2, :], x1[:, ti, :], ACT.Copy, scale=rstd[:, S_FFN + ti:S_FFN + ti + 1]).then_inc(xn2_ready, 1)
                act.wait_ge(xn2_ready, ti + 1)
                fn(xparts[:, 0, ti, :], xn2[:, ti % 2, :], ACT.Copy).then_inc(high_cut, 1)
                if ti + 1 < NT:
                    mix_a(ti + 1)
                act.wait_ge(h2t_done, ti + 1)
                for k in range(4):
                    last = fn(h2T[:, k, ti * P:(ti + 1) * P], PS[:, 0, k * P:(k + 1) * P], ACT.Identity,
                              bias=modcol[:, 2, 0, k:k + 1], scale=modcol[:, 3, 0, k:k + 1])
                last.then_inc(h2T_a, 1)
                act.wait_ge(rest_ready, ti + 1)
                fn(xparts[:, 1, ti, :], rest_tmp[:, :], ACT.Copy).then_inc(mid_cut, 1)

            act.wait_ge(gdiff, 1)
            fn(gexp[:, :, :], g1t[:, :, :], ACT.Exp).then_inc(gexp_ready, 1)
            act.wait_ge(d21_ready, 1)
            fn(e21[:, :], mt_[:, :], ACT.Exp).then_inc(e21_ready, 1)

            def xT_upper(n):
                act.wait_ge(gx_done, n * 2 + 2)
                for k in range(4, KD):
                    last = fn(xT[:, k, :], PS[:, 1, (k - 4) * P:(k - 3) * P], ACT.Identity,
                              bias=modcol[:, 2, 0, k:k + 1], scale=modcol[:, 3, 0, k:k + 1])
                last.then_inc(xT_a, 1)

            def expert_pair(it, s17, more=True):
                act.wait_ge(slot_used[1], it + 1)
                act.wait_ge(hid_ready, it + 1)
                fn(gate_act[:, :], PS[:, 3, :], ACT.Silu).then_inc(silu_ready, 1)
                if more:
                    xT_upper(it + 1)
                act.wait_ge(scat_done, s17 * 8 + 8)
                for n, done in enumerate((y_half, slot_used[5])):
                    act.wait_ge(done, it + 1)
                    fn(yH[:, n * 512:(n + 1) * 512], PS[:, 6 + n, :], ACT.Copy).then_inc(yH_ready, 1)

            def one_round(it0, s0):
                xT_upper(it0)
                with act.Fori(0, PAIRS - 1) as p:
                    expert_pair(it0 + p, s0 + p)
                expert_pair(it0 + PAIRS - 1, s0 + PAIRS - 1, more=False)

            act.wait_ge(h2T_a, NT)
            one_round(0, 0)
            fullest = act.value_load(cmax[0:1, 0:1], min_val=0, max_val=SEQ)
            with act.If(fullest > CAP):
                with act.Fori(1, ROUNDS) as r:
                    with act.If(fullest > r * CAP):
                        one_round(r * PAIRS, r * (PAIRS + 1))
            for ti in range(NT):
                act.wait_ge(end_sq, ti)
                if ti == 0:
                    act.wait_ge(final_added, 1)
                fn(end_junk[:, :], acc[:, ti, :], ACT.Square,
                   accum_out=ss[:, S_END + ti:S_END + ti + 1]).then_inc(end_sq, 1)

        @block.vector
        def _(dve):
            V_ = nc.vector
            tt, ts, cp = V_.tensor_tensor, V_.tensor_scalar, V_.tensor_copy
            own = [0]

            def then(ins):
                own[0] += 1
                ins.then_inc(dve_own, 1)
                dve.wait_ge(dve_own, own[0])

            dve.wait_ge(cst_in, 32)
            raw = lambda n: cst_raw[:, (CST[n][0] - CST_KEPT):(CST[n][1] - CST_KEPT)]
            cp(identb[:, :], ident)
            cp(maskw[:, 0, :], raw("prev"))
            cp(maskw[:, 1, :], raw("next"))
            cp(beforeb[:, :], raw("before"))
            V_.memset(onesb[:, :], 1.0).then_inc(bf_ready, 1)
            dve.wait_ge(spad_ready, 2)
            cp(ncol[:, :], PS[:, 7, 16:40]).then_inc(ncol_ready, 1)

            def mod_take(i):
                dve.wait_ge(modx_done, i + 1)
                part, half = i // 2, i % 2
                if part in (2, 5):
                    g = (g1p if part == 2 else g2p)[:, half * CHUNK:(half + 1) * CHUNK]
                    dve.wait_ge(rowgain_in, 32)
                    tt(g, PS[:, 7, :], g, ALU.mult).then_inc(modx_taken, 1)
                    return
                which = {0: 0, 1: 1, 3: 2, 4: 3}[part]
                for who in range(2):
                    src = PS[:, 7, 0:8].rearrange("p (b w) -> p b w", w=2)[:, :, who]
                    dst = modcol[:, which, who, 4 * half:4 * half + 4]
                    if which % 2 == 0:
                        last = cp(dst, src)
                    else:
                        base = 8 * (which // 2) + 4 * half
                        last = V_.scalar_tensor_tensor(out=dst, in0=src, scalar=1.0, in1=ncol[:, base:base + 4],
                                                       op0=ALU.add, op1=ALU.mult)
                last.then_inc(modx_taken, 1)

            dve.wait_ge(ncol_ready, 1)
            mod_take(0)
            dve.wait_ge(in_rstd, 1)
            for ti in range(NT):
                ts(xin[:, ti, :], xin[:, ti, :], rstd[:, S_IN + ti:S_IN + ti + 1], None, ALU.mult).then_inc(xn_ready, 1)
            mod_take(1)
            for k in range(KD):
                dve.wait_ge(xt_done, k + 1)
                cp(hT[:, k, 0:SEQ], PS[:, 2 * (k % 3), :]).then_inc(xtx_out, 1)
            dve.wait_ge(xtx_out, KD)
            for i in (2, 3):
                mod_take(i)
                dve.wait_ge(modx_taken, i + 1)
                for k in range(4 * (i - 2), 4 * (i - 1)):
                    ts(hT[:, k, 0:SEQ], hT[:, k, 0:SEQ], modcol[:, 1, 0, k:k + 1], modcol[:, 0, 0, k:k + 1],
                       ALU.mult, ALU.add).then_inc(hTx_ready, 1)
            dve.wait_ge(small_in, SMALL)
            then(ts(neg_sink[:, :], sink[:, :], -1.0, None, ALU.mult))
            cp(gains[:, 1:8, :], gains[:, 0:1, :].to_broadcast([P, 7, HD]))
            then(cp(gains[:, 9, :], gains[:, 8, :]))

            def heads(t):
                ti = TURN[t]
                latent = ti < NT
                dve.wait_ge(pn_ready, sum(BANKS[:t + 1]))
                if t:
                    dve.wait_ge(stk_t, STK[TURN[t - 1], 5] + 1)
                n0 = 0 if latent else 8
                nb = 10 - n0
                bh = pn[:, 768 + 64 * n0:768 + 640].rearrange("p (h d) -> p h d", d=HD)
                tmp = rope_tmp[:, 0, n0:10, :]
                then(tt(tmp, bh, bh, ALU.mult))
                V_.tensor_reduce(out=bss[:, n0:10], in_=tmp, axis=AX.X, op=ALU.add).then_inc(bsq_ready, 1)
                dve.wait_ge(brstd_ready, t + 1)
                then(tt(bh, bh, brs[:, n0:10].rearrange("p (h o) -> p h o", o=1).to_broadcast([P, nb, HD]), ALU.mult))
                last = tt(bh, bh, gains[:, n0:10, :], ALU.mult)
                pg = pn[:, :].rearrange("p (g s) -> p g s", g=2)
                if latent:
                    then(last)
                    qk = pg[:, :, 0:640].rearrange("p g (h d) -> p g h d", d=HD)
                    qk2 = pg[:, :, 0:640].rearrange("p g (h i w) -> p g h i w", i=HD // 2, w=2)
                    tm2 = rope_tmp[:, :, :, :].rearrange("p g h (i w) -> p g h i w", w=2)
                    a = CST["sin"][0] + ti * HD
                    sn = cst[:, a:a + HD].rearrange("p (o q i w) -> p o q i w", o=1, q=1, w=2)
                    a = CST["cos"][0] + ti * HD
                    cs = cst[:, a:a + HD].rearrange("p (o q d) -> p o q d", o=1, q=1).to_broadcast([P, 2, 10, HD])
                    for w in range(2):
                        last = tt(tm2[:, :, :, :, w], qk2[:, :, :, :, 1 - w],
                                  sn[:, :, :, :, w].to_broadcast([P, 2, 10, HD // 2]), ALU.mult)
                    then(last)
                    then(tt(qk, qk, cs, ALU.mult))
                    last = tt(qk, qk, rope_tmp[:, :, :, :], ALU.add)
                last.then_inc(roped, 1)
                dve.wait_ge(high_ready, t + 1)
                if latent:
                    for g in range(2):
                        tt(QS[:, 8 * g:8 * g + 8, HD:], pg[:, g, 0:512].rearrange("p (h d) -> p h d", d=HD),
                           QS[:, 8 * g:8 * g + 8, 0:HD].bitcast(F32), ALU.subtract)
                for g in range(2):
                    src = pg[:, g, 512:640].rearrange("p (v o d) -> p v o d", v=2, o=1).to_broadcast([P, 2, 2, HD])
                    last = tt(KS[:, 2 * g:2 * g + 2, 1, :].rearrange("p v (o d) -> p v o d", o=2), src,
                              KS[:, 2 * g:2 * g + 2, 0, :].rearrange("p v (o d) -> p v o d", o=2).bitcast(F32),
                              ALU.subtract)
                last.then_inc(heads_ready, 1)

            for t in range(NT + NC):
                heads(t)
                if t + 1 in MODS:
                    mod_take(MODS[t + 1])
                    mod_take(MODS[t + 1] + 1)
                if t == LAST_TURN - 1:
                    mod_take(NMOD - 2)
                heads_evac(TURN[t], 1, dve, cp)
            mod_take(NMOD - 1)

            def latent_probs(u):
                pr, qt, hh = UNITS[u]
                lo, hi = window(pr, qt)
                nb = hi - lo + 1
                dve.wait_ge(pt_done, u + 1)
                if pr >= 2:
                    dve.wait_ge(av_done, pr - 1)
                cp(PT[pr % 2][:, hh, lo:hi + 1, qt * P:(qt + 1) * P],
                   PS[:, 4, 0:nb * P].rearrange("p (b t) -> p b t", b=nb)).then_inc(ptl_ready, 1)

            def o_natural(pr):
                rsp = rs[:, 8 * pr:8 * pr + 8]
                den = dens[:, pr % 2, :]
                dve.wait_ge(p_ready, 8 * (pr + 1))
                if pr < 4:
                    dve.wait_ge(sink_ready, 8 * (pr + 1))
                    then(tt(den, rsp, esn[:, 8 * pr:8 * pr + 8], ALU.add))
                    rsp = den
                then(V_.reciprocal(den, rsp))
                dve.wait_ge(ot_done, pr + 1)
                r = den.rearrange("p (q h o) -> p q h o", h=2, o=1).to_broadcast([P, NT, 2, HD])
                tt(onat[:, :, pr * P:(pr + 1) * P].rearrange("p q (h d) -> p q h d", h=2),
                   PS[:, 7, :].rearrange("p (q h d) -> p q h d", q=NT, h=2), r, ALU.mult).then_inc(onat_ready, 1)

            dve.wait_ge(qkv_done, 3 * NT + 2 * NC)
            for u, (pr, qt, hh) in enumerate(UNITS):
                off, end = score_span(pr, qt)
                S = PS[:, 2 * (u % 2):2 * (u % 2) + 2, :].rearrange("p b n -> p (b n)")
                dve.wait_ge(sc_done, u + 1)
                then(V_.tensor_reduce(out=mx[:, u % 2:u % 2 + 1], in_=S[:, off:end], axis=AX.X, op=ALU.max))
                if u >= 8:
                    dve.wait_ge(p_ready, u - 7)
                    if 8 <= u < 40:
                        dve.wait_ge(sink_ready, u - 7)
                if pr < 4:
                    h = 2 * pr + hh
                    ts(nm[:, u % 8:u % 8 + 1], mx[:, u % 2:u % 2 + 1], -SCALE, neg_sink[:, h:h + 1],
                       ALU.mult, ALU.min).then_inc(nm_ready, 1)
                else:
                    ts(nm[:, u % 8:u % 8 + 1], mx[:, u % 2:u % 2 + 1], -SCALE, None, ALU.mult).then_inc(nm_ready, 1)
                if u:
                    latent_probs(u - 1)
                if u % 8 == 1 and pr >= 2:
                    o_natural(pr - 2)
            latent_probs(len(UNITS) - 1)
            o_natural(6)
            o_natural(7)

            def low_part(ti):
                dve.wait_ge(mid_cut, ti + 1)
                tt(xparts[:, 2, ti, :], rest_tmp[:, :], xparts[:, 1, ti, :], ALU.subtract).then_inc(parts_ready, 1)

            dve.wait_ge(grp_rstd, 2)
            dve.wait_ge(x_again, 16)
            for ti in range(NT):
                dve.wait_ge(ta_ready, ti + 1)
                dve.wait_ge(proj_done[1], ti + 1)
                if ti:
                    dve.wait_ge(mixed, 2 * ti)
                n = S_GRP + NT + ti
                V_.scalar_tensor_tensor(out=mix_tmp[:, :], in0=PS[:, 6:8, :].rearrange("p b n -> p (b n)"),
                                        scalar=rstd[:, n:n + 1], in1=mixA[:, :], op0=ALU.mult, op1=ALU.add
                                        ).then_inc(sum_ready, 1)
                if ti:
                    low_part(ti - 1)
                dve.wait_ge(mix_rstd, ti + 1)
                V_.scalar_tensor_tensor(out=mix_tmp[:, :], in0=mix_tmp[:, :],
                                        scalar=rstd[:, S_MIX + ti:S_MIX + ti + 1], in1=g1p[:, :],
                                        op0=ALU.mult, op1=ALU.mult).then_inc(mixed, 1)
                dve.wait_ge(mixed, 2 * ti + 1)
                tt(x1[:, ti, :], x1[:, ti, :], mix_tmp[:, :], ALU.add).then_inc(mixed, 1)
                dve.wait_ge(high_cut, ti + 1)
                if ti:
                    dve.wait_ge(parts_ready, ti)
                tt(rest_tmp[:, :], xn2[:, ti % 2, :], xparts[:, 0, ti, :], ALU.subtract).then_inc(rest_ready, 1)
                dve.wait_ge(h2t_done, ti + 1)
                for k in range(4, KD):
                    last = ts(h2T[:, k, ti * P:(ti + 1) * P], PS[:, 1, (k - 4) * P:(k - 3) * P],
                              modcol[:, 3, 0, k:k + 1], modcol[:, 2, 0, k:k + 1], ALU.mult, ALU.add)
                last.then_inc(h2T_d, 1)

            low_part(NT - 1)

            dve.wait_ge(lg_done, NT)
            w = NG + NE
            then(tt(lg[:, :, :], PS[:, 2, 0:NT * w].rearrange("p (t n) -> p t n", t=NT),
                    rbias[:, :].rearrange("p (o n) -> p o n", o=1).to_broadcast([P, NT, w]), ALU.add))

            def col(v, n):
                return v[:, :].rearrange("p (t o) -> p t o", o=1).to_broadcast([P, NT, n])

            def first_max(one_hot, top, values, n):
                tmp = one_hot
                rev = k_("rev")[:, EPG - n:EPG].rearrange("p (o n) -> p o n", o=1).to_broadcast([P, NT, n])
                then(V_.tensor_reduce(out=top[:, :], in_=values, axis=AX.X, op=ALU.max))
                then(tt(tmp[:, :, :], values, col(top, n), ALU.is_equal))
                then(tt(tmp[:, :, :], tmp[:, :, :], rev, ALU.mult))
                then(V_.tensor_reduce(out=mt_[:, :], in_=tmp[:, :, :], axis=AX.X, op=ALU.max))
                then(tt(one_hot[:, :, :], tmp[:, :, :], col(mt_, n), ALU.is_equal))

            gl = lg[:, :, 0:NG]
            first_max(ohg, gmax, gl, NG)
            tt(g1t[:, :, :], gl, col(gmax, NG), ALU.subtract).then_inc(gdiff, 1)
            el = lg[:, :, NG:].rearrange("p t (g e) -> p t g e", g=NG)
            then(tt(picked[:, :, :, :], el,
                    ohg[:, :, :].rearrange("p t (g o) -> p t g o", o=1).to_broadcast([P, NT, NG, EPG]), ALU.mult))
            then(V_.tensor_reduce(out=es[:, :, :], in_=picked[:, :, :, :].rearrange("p t g e -> p t e g"),
                                  axis=AX.X, op=ALU.add))
            first_max(oh1, m1, es[:, :, :], EPG)
            then(V_.scalar_tensor_tensor(out=e1t[:, :, :], in0=oh1[:, :, :], scalar=NEG, in1=es[:, :, :],
                                         op0=ALU.mult, op1=ALU.add))
            first_max(oh2, m2, e1t[:, :, :], EPG)
            tt(mt_[:, :], m2[:, :], m1[:, :], ALU.subtract).then_inc(d21_ready, 1)
            dve.wait_ge(gexp_ready, 1)
            then(V_.tensor_reduce(out=gsum[:, :], in_=gexp[:, :, :], axis=AX.X, op=ALU.add))
            then(V_.reciprocal(gw[:, :], gsum[:, :]))
            dve.wait_ge(e21_ready, 1)
            then(ts(w2t[:, :], e21[:, :], 1.0, None, ALU.add))
            then(V_.reciprocal(w1t[:, :], w2t[:, :]))
            then(tt(w1t[:, :], w1t[:, :], gw[:, :], ALU.mult))
            then(tt(w2t[:, :], w1t[:, :], e21[:, :], ALU.mult))
            tt(mke[:, :, :], oh1[:, :, :], oh2[:, :, :], ALU.add)
            tt(cwe[:, :, :], oh1[:, :, :], col(w1t, EPG), ALU.mult)
            then(tt(e1t[:, :, :], oh2[:, :, :], col(w2t, EPG), ALU.mult))
            then(tt(cwe[:, :, :], cwe[:, :, :], e1t[:, :, :], ALU.add))

            def by_group(v):
                return v[:, :, :].rearrange("p t (o e) -> p t o e", o=1).to_broadcast([P, NT, NG, EPG])

            gsel = ohg[:, :, :].rearrange("p t (g o) -> p t g o", o=1).to_broadcast([P, NT, NG, EPG])
            tt(maskb[:, :, :].rearrange("p t (g e) -> p t g e", g=NG), gsel, by_group(mke), ALU.mult).then_inc(mask_ready, 1)
            tt(maskf[:, :, :].rearrange("p t (g e) -> p t g e", g=NG), gsel, by_group(mke), ALU.mult)
            V_.memset(cw[:, :, NE:], 0.0)
            V_.memset(slotval[:, :, NE:], -1.0)
            then(tt(cw[:, :, 0:NE].rearrange("p t (g e) -> p t g e", g=NG), gsel, by_group(cwe), ALU.mult))
            dve.wait_ge(pos_done, 1)
            then(V_.scalar_tensor_tensor(out=slotval[:, :, 0:NE],
                                         in0=PS[:, 3, 0:NT * NE].rearrange("p (t n) -> p t n", t=NT), scalar=1.0,
                                         in1=maskf[:, :, :], op0=ALU.add, op1=ALU.mult))
            ts(slotval[:, :, 0:NE], slotval[:, :, 0:NE], -1.0, None, ALU.add).then_inc(shifted, 1)
            then(V_.tensor_reduce(out=cmaxf[:, :], in_=PS[:, 3, NT * NE:(NT + 1) * NE], axis=AX.X, op=ALU.max))
            cp(cmax[:, :], cmaxf[:, :]).then_inc(route_ready, 1)

            def match(pair):
                sv = slotval[:, :, bass.ds(pair * 2, 2)].rearrange("p t (e o) -> p t e o", o=1).to_broadcast([P, NT, 2, CAP])
                io = k_("iota").rearrange("p (o q c) -> p o q c", o=1, q=1).to_broadcast([P, NT, 2, CAP])
                tt(M[:, :, :, :], io, sv, ALU.is_equal).then_inc(M_ready, 1)

            def weigh(pair, n):
                dve.wait_ge(M_ready, n + 1)
                cv = cw[:, :, bass.ds(pair * 2, 2)].rearrange("p t (e o) -> p t e o", o=1).to_broadcast([P, NT, 2, CAP])
                tt(MW[:, :, :, :], M[:, :, :, :], cv, ALU.mult).then_inc(MW_ready, 1)

            def xT_lower(n):
                dve.wait_ge(gx_done, n * 2 + 2)
                for k in range(4):
                    last = ts(xT[:, k, :], PS[:, 0, k * P:(k + 1) * P], modcol[:, 3, 0, k:k + 1],
                              modcol[:, 2, 0, k:k + 1], ALU.mult, ALU.add)
                last.then_inc(xT_d, 1)

            def add_scattered(s17):
                dve.wait_ge(mt_ready, s17 + 1)
                for s in range(8):
                    dve.wait_ge(scat_done, s17 * 8 + (s + 1))
                    ti, n = s // 2, s % 2
                    a = acc[:, ti, n * 512:(n + 1) * 512]
                    tt(a, PS[:, (6, 7, 5)[s % 3], :], a, ALU.add).then_inc(acc_added, 1)

            def expert_pair(pair, it, s17, more=True):
                dve.wait_ge(gx_done, it * 2 + 2)
                dve.wait_ge(MW_ready, it + 1)
                if more:
                    match(pair + 1)
                add_scattered(s17)
                dve.wait_ge(mwt_done, it + 1)
                ts(MT[:, :], PS[:, 2, :], 0.0, None, ALU.not_equal)
                V_.tensor_reduce(out=wslot[:, :], in_=PS[:, 2, :], axis=AX.X, op=ALU.add).then_inc(mt_ready, 1)
                if more:
                    weigh(pair + 1, it + 1)
                dve.wait_ge(silu_ready, it + 1)
                dve.wait_ge(slot_used[3], it + 1)
                dve.wait_ge(mt_ready, s17 + 2)
                V_.scalar_tensor_tensor(out=hid[:, :], in0=gate_act[:, :], scalar=wslot[:, :], in1=PS[:, 4, :],
                                        op0=ALU.mult, op1=ALU.mult).then_inc(hid_ready, 1)
                if more:
                    xT_lower(it + 1)
                dve.wait_ge(hidT_done, it + 1)
                cp(hidT[:, :, :].rearrange("p f s -> p (f s)"), PS[:, 5, :]).then_inc(hidT_ready, 1)
                for n in range(2):
                    dve.wait_ge(yH_ready, 2 * it + (n + 1))
                    last = tt(yL[:, n * 512:(n + 1) * 512], PS[:, 6 + n, :], yH[:, n * 512:(n + 1) * 512].bitcast(F32),
                              ALU.subtract)
                last.then_inc(y_split, 1)

            def one_round(it0, s0):
                match(0)
                weigh(0, it0)
                xT_lower(it0)
                with dve.Fori(0, PAIRS - 1) as p:
                    expert_pair(p, it0 + p, s0 + p)
                expert_pair(PAIRS - 1, it0 + PAIRS - 1, s0 + PAIRS - 1, more=False)
                add_scattered(s0 + PAIRS)

            dve.wait_ge(shifted, 1)
            dve.wait_ge(zeroed, 4)
            one_round(0, 0)
            fullest = dve.value_load(cmax[0:1, 0:1], min_val=0, max_val=SEQ)
            with dve.If(fullest > CAP):
                with dve.Fori(1, ROUNDS) as r:
                    with dve.If(fullest > r * CAP):
                        dve.wait_ge(scat_done, r * 8 * (PAIRS + 1))
                        dve.wait_ge(gx_done, r * 2 * PAIRS)
                        V_.memset(MT[:, :].bitcast(F32), 0.0).then_inc(mt_ready, 1)
                        dve.wait_ge(shifted, r)
                        ts(slotval[:, :, :], slotval[:, :, :], float(-CAP), None, ALU.add).then_inc(shifted, 1)
                        dve.wait_ge(shifted, r + 1)
                        dve.wait_ge(y_split, r * (PAIRS + 1))
                        V_.memset(yL[:, :].bitcast(F32), 0.0).then_inc(y_split, 1)
                        dve.wait_ge(MW_ready, r * PAIRS)
                        one_round(r * PAIRS, r * (PAIRS + 1))
            cp(bss[:, 1:2], bss[:, 1:2]).then_inc(final_added, 1)
            for ti in range(NT):
                dve.wait_ge(end_rstd, ti + 1)
                a = acc[:, ti, :]
                then(V_.scalar_tensor_tensor(out=a, in0=a, scalar=rstd[:, S_END + ti:S_END + ti + 1], in1=g2p[:, :],
                                             op0=ALU.mult, op1=ALU.mult))
                tt(a, a, x1[:, ti, :], ALU.add).then_inc(end_ready, 1)

        @block.gpsimd
        def _(pool):
            G = nc.gpsimd
            own = [0]
            G.memset(spad[:, :, :], 0.0).then_inc(spad_zero, 1)
            pool.wait_ge(cst_in, 32)

            def inverse_root(n, sums, means, roots, a, b, done):
                G.tensor_scalar(means[:, a:b], sums[:, a:b], 1.0 / n, EPS, ALU.mult, ALU.add).then_inc(pool_own, 1)
                own[0] += 1
                pool.wait_ge(pool_own, own[0])
                G.tensor_tensor(roots[:, a:b], means[:, a:b], k_("half")[:, 0:1].to_broadcast([P, b - a]),
                                ALU.pow).then_inc(done, 1)

            pool.wait_ge(in_sq, NT + NC)
            inverse_root(D, ss, ms, rstd, S_IN, S_IN + 6, in_rstd)
            for t, ti in enumerate(TURN):
                pool.wait_ge(bsq_ready, t + 1)
                inverse_root(HD, bss, bms, brs, 0 if ti < NT else 8, 10, brstd_ready)
            for g in range(2):
                pool.wait_ge(grp_sq, 4 * (g + 1))
                inverse_root(512, ss, ms, rstd, S_GRP + 4 * g, S_GRP + 4 * g + 4, grp_rstd)
            for ti in range(NT):
                pool.wait_ge(mix_sq, ti + 1)
                inverse_root(D, ss, ms, rstd, S_MIX + ti, S_MIX + ti + 1, mix_rstd)
                pool.wait_ge(ffn_sq, ti + 1)
                inverse_root(D, ss, ms, rstd, S_FFN + ti, S_FFN + ti + 1, ffn_rstd)
            pool.wait_ge(proj_done[1], NT)
            for ti in range(NT):
                G.memset(acc[:, ti, :], 0.0).then_inc(zeroed, 1)
            G.memset(hid[:, :], 0.0).then_inc(hid_ready, 1)
            G.memset(MT[:, :].bitcast(F32), 0.0).then_inc(mt_ready, 1)
            pool.wait_ge(parts_ready, NT)
            pool.wait_ge(h2t_done, NT)
            G.memset(yH[:, :].bitcast(F32), 0.0).then_inc(zeroed, 1)
            G.memset(yL[:, :].bitcast(F32), 0.0).then_inc(y_split, 1)
            for ti in range(NT):
                pool.wait_ge(end_sq, ti + 1)
                inverse_root(D, ss, ms, rstd, S_END + ti, S_END + ti + 1, end_rstd)


_INS = ["x", "c", "ctx", "c_ctx", "w_mod", "b_mod", "attn_pre_norm", "attn_post_norm", "w_in", "a_sink",
        "b_q_norm", "b_k_norm", "a_out_norm", "b_out_norm", "w_out", "ffn_pre_norm", "ffn_post_norm",
        "w_group", "b_group", "w_router", "b_router", "w_gate", "w_up", "w_down"]


def kernel(**inputs):
    import numpy as _np
    import concourse.bacc as _bacc
    from concourse import mybir as _mybir
    from concourse.bass_utils import run_bass_kernel_spmd as _run

    nc = _bacc.Bacc("TRN2", target_bir_lowering=False, num_devices=1)
    arrays, args = {}, []
    for name in _INS + ["shape_constants"]:
        a = shape_constants() if name == "shape_constants" else _np.ascontiguousarray(inputs[name])
        arrays[f"in_{name}"] = a
        args.append(nc.dram_tensor(f"in_{name}", a.shape, _mybir.dt.from_np(a.dtype), kind="ExternalInput").ap())
    args.append(nc.dram_tensor("out_x", (1, SEQ, D), F32, kind="ExternalOutput").ap())
    backbone_layer(nc, *args)
    r = _run(nc, [arrays], core_ids=[0])
    return r.results[0]["out_x"]
```

```python
import numpy as np
import concourse.bass as bass
from concourse import mybir
from contextlib import ExitStack

F32 = mybir.dt.float32
F32R = mybir.dt.float32r
BF16 = mybir.dt.bfloat16
I32 = mybir.dt.int32
ALU = mybir.AluOpType
ACT = mybir.ActivationFunctionType
AX = mybir.AxisListType

P = 128
D = 1024
SEQ, CTX = 512, 256
NT, NC = SEQ // P, CTX // P
KEYS = SEQ + CTX
NKB = KEYS // P
KD = D // P
IN_DIM = 1536
HD = 64
HEADS = 16
KVH = 4
NG, EPG = 4, 8
NE = NG * EPG
FF = 512
KF = FF // P
EPS = 1e-6
NEG = -1e30
CHUNK = 512
NMOD = 6 * D // CHUNK
CAP = 64
PAIRS = NE // 2
ROUNDS = SEQ // CAP
SCALE = HD ** -0.5
GRID_W = 64
THETA = 10000.0

CST = {}
_at = 0
for _name, _width in (("ident", P), ("cos", NT * HD), ("sin", NT * HD), ("selb", P), ("sel2", 2),
                      ("iota", CAP), ("rev", EPG), ("half", 8), ("prev", P), ("next", P), ("before", P)):
    CST[_name] = (_at, _at + _width)
    _at += _width
CST_WIDTH = _at
CST_KEPT = CST["prev"][0]


def shape_constants():
    t = np.zeros((P, CST_WIDTH), np.float32)
    i, j = np.arange(P)[:, None], np.arange(P)[None, :]

    def put(name, v):
        t[:, CST[name][0]:CST[name][1]] = v

    put("ident", (i == j).astype(np.float32))
    axis = HD // 2
    inv = (THETA ** (-np.arange(0, axis, 2, dtype=np.float32) / axis)).astype(np.float32)
    tok = np.arange(SEQ)
    ang = np.concatenate([(tok // GRID_W).astype(np.float32)[:, None] * inv,
                          (tok % GRID_W).astype(np.float32)[:, None] * inv], axis=1)
    cos = np.repeat(np.cos(ang), 2, axis=1).reshape(NT, P, HD)
    sin = np.repeat(np.sin(ang), 2, axis=1).reshape(NT, P, HD)
    sin[:, :, 0::2] *= -1
    put("cos", cos.transpose(1, 0, 2).reshape(P, -1))
    put("sin", sin.transpose(1, 0, 2).reshape(P, -1))
    put("selb", np.repeat((np.arange(P) % 32 == 0)[:, None], P, axis=1))
    put("sel2", np.stack([np.arange(P) % 32 == 0, np.arange(P) % 32 == 1], axis=1))
    put("iota", np.arange(CAP)[None, :])
    put("rev", EPG - np.arange(EPG)[None, :])
    put("half", -0.5)
    put("prev", np.where(j >= i, 0.0, NEG))
    put("next", np.where(j <= i, 0.0, NEG))
    put("before", (i < j).astype(np.float32))
    return t


def backbone_layer(nc, x, c, ctx_tok, c_ctx, w_mod, b_mod, attn_pre, attn_post, w_in, a_sink, bq_norm, bk_norm,
                   a_out, b_out, w_out, ffn_pre, ffn_post, w_group, b_group, w_router, b_router,
                   w_gate, w_up, w_down, cst_dram, out):
    KB = 1024
    BASE = 16512
    END = 229344
    placed = [BASE + 192 * KB]

    def at(name, shape, dt, off):
        return nc.alloc_sbuf_tensor_at(name, shape, dt, offset=BASE + off)

    def keep(name, shape, dt):
        size = int(np.prod(shape[1:])) * (2 if dt == BF16 else 4)
        t = nc.alloc_sbuf_tensor_at(name, shape, dt, offset=placed[0])
        placed[0] += (size + 31) // 32 * 32
        assert placed[0] <= END, (name, placed[0])
        return t

    slot = [at(f"slot{j}", [P, 2, 4, CHUNK], F32, 16 * KB * j) for j in range(6)]
    mslot = [at(f"mslot{j}", [P, KD, CHUNK], F32, 16 * KB * j) for j in range(4)]
    Q = at("Q", [P, HEADS, SEQ], F32R, 32 * KB)
    junk_in = at("junk_in", [P, D], F32, 144 * KB)
    V = at("V", [P, NKB, KVH * HD], F32, 64 * KB)
    pn = at("pn", [P, IN_DIM], F32, 70 * KB)
    QS = at("QS", [P, HEADS, 2 * HD], F32R, 76 * KB)
    rope_tmp = [at(f"rope_tmp{g}", [P, 10, HD], F32, (76 + 4 * g) * KB) for g in range(2)]
    KS = at("KS", [P, KVH, 2, 2 * HD], F32R, 84 * KB)
    gains = at("gains", [P, 10, HD], F32, 88 * KB)
    bmod = at("bmod", [NMOD, CHUNK], F32, 88 * KB + 2560)
    modrow = at("modrow", [P, CHUNK], F32, 88 * KB + 2560 + 2048)
    spad = at("spad", [P, KD, 32], F32, 88 * KB + 2560 + 4096)
    ctx_tmp = at("ctx_tmp", [P, 2, HD], F32, 88 * KB + 2560 + 4096 + 1024)
    PT = [at(f"PT{j}", [P, 2, NKB, SEQ], F32, o * KB) for j, o in enumerate((70, 0))]
    mix_tmp = at("mix_tmp", [P, D], F32, 64 * KB)
    rest_tmp = at("rest_tmp", [P, D], F32, 68 * KB)
    junk = at("junk", [P, D], F32, 72 * KB)
    grp_junk = at("grp_junk", [P, 512], F32, 166 * KB)
    end_junk = at("end_junk", [P, D], F32, 120 * KB)
    mixg = at("mixg", [P, D], F32, 16 * KB)
    mixA = at("mixA", [P, D], F32, 76 * KB)
    oT = [at(f"oT{g}", [P, KD // 2, SEQ], F32, o * KB) for g, o in enumerate((24, 40))]
    win = at("win", [P, KD, IN_DIM], F32, 96 * KB)
    wout = at("wout", [P, KD, D], F32, 96 * KB)
    onat = at("onat", [P, NT, D], F32, 128 * KB)
    h2T = at("h2T", [P, KD, SEQ], F32, 128 * KB)
    hT = at("hT", [P, KD, KEYS], F32, 144 * KB)
    Pb = at("Pb", [P, 4, KEYS], F32, 144 * KB)
    oTs = at("oTs", [P, SEQ], F32, 156 * KB)
    xparts = at("xparts", [P, 3, NT, D], BF16, 144 * KB)
    xin = at("xin", [P, NT + NC, D], F32, 168 * KB)
    K = at("K", [P, KVH, 2, KEYS], F32R, 168 * KB)
    x1 = at("x1", [P, NT, D], F32, 168 * KB)
    xn2 = at("xn2", [P, 2, D], F32, 184 * KB)
    acc = at("acc", [P, NT, D], F32, 96 * KB)
    xT = at("xT", [P, KD, P], F32, 112 * KB)
    MT = at("MT", [P, SEQ], F32R, 116 * KB)
    MW = at("MW", [P, NT, 2, CAP], F32, 118 * KB)
    gate_act = at("gate_act", [P, FF], F32, 120 * KB)
    hid = at("hid", [P, FF], F32, 122 * KB)
    hidT = at("hidT", [P, KF, P], F32, 124 * KB)
    M = at("M", [P, NT, 2, CAP], BF16, 126 * KB)
    yH = at("yH", [P, D], F32R, 184 * KB)
    yL = at("yL", [P, D], F32R, 188 * KB)
    r_at = [136 * KB]

    def rt(name, shape, dt=F32):
        size = int(np.prod(shape[1:])) * (2 if dt == BF16 else 4)
        t = at(name, shape, dt, r_at[0])
        r_at[0] += (size + 31) // 32 * 32
        assert r_at[0] <= 144 * KB
        return t

    slotval = rt("slotval", [P, NT, NE + 2])
    cw = rt("cw", [P, NT, NE + 2])
    lg = rt("lg", [P, NT, NG + NE])
    gmax = rt("gmax", [P, NT])
    gexp = rt("gexp", [P, NT, NG])
    gsum = rt("gsum", [P, NT])
    gw = rt("gw", [P, NT])
    g1t = rt("g1t", [P, NT, NG])
    ohg = rt("ohg", [P, NT, NG])
    picked = rt("picked", [P, NT, NG, EPG])
    es = rt("es", [P, NT, EPG])
    e1t = rt("e1t", [P, NT, EPG])
    oh1 = rt("oh1", [P, NT, EPG])
    oh2 = rt("oh2", [P, NT, EPG])
    m1 = rt("m1", [P, NT])
    m2 = rt("m2", [P, NT])
    mt_ = rt("mt_", [P, NT])
    e21 = rt("e21", [P, NT])
    w1t = rt("w1t", [P, NT])
    w2t = rt("w2t", [P, NT])
    cwe = rt("cwe", [P, NT, EPG])
    mke = rt("mke", [P, NT, EPG])
    maskf = rt("maskf", [P, NT, NE])
    maskb = rt("maskb", [P, NT, NE], BF16)
    cmaxf = rt("cmaxf", [P, 1])
    cmax = rt("cmax", [P, 1], I32)
    wslot = rt("wslot", [P, 1])

    cst = keep("cst", [P, CST_KEPT], F32)
    cst_raw = at("cst_raw", [P, CST_WIDTH - CST_KEPT], F32, 148 * KB)
    identb = keep("identb", [P, P], BF16)
    maskw = keep("maskw", [P, 2, P], BF16)
    beforeb = keep("beforeb", [P, P], BF16)
    onesb = keep("onesb", [P, P], BF16)
    g1p = keep("g1p", [P, D], F32)
    g2p = keep("g2p", [P, D], F32)
    wr = keep("wr", [P, KD, NG + NE], F32)
    rbias = keep("rbias", [P, NG + NE], F32)
    sink = keep("sink", [P, 8], F32)
    stage = keep("stage", [40, P], F32)
    ncol = keep("ncol", [P, 24], F32)
    modcol = keep("modcol", [P, 4, 2, KD], F32)
    NS = 6 + 8 + 4 + 4 + 4
    ss = keep("ss", [P, NS], F32)
    ms = keep("ms", [P, NS], F32)
    rstd = keep("rstd", [P, NS], F32)
    bss = keep("bss", [P, 10], F32)
    bms = keep("bms", [P, 10], F32)
    brs = keep("brs", [P, 10], F32)
    mx = keep("mx", [P, 2], F32)
    nm = keep("nm", [P, 8], F32)
    rs = keep("rs", [P, 64], F32)
    esn = keep("esn", [P, 32], F32)
    neg_sink = keep("neg_sink", [P, 8], F32)
    dens = keep("dens", [P, 2, 8], F32)
    S_IN, S_GRP, S_MIX, S_FFN, S_END = 0, 6, 14, 18, 22

    def k_(name):
        return cst[:, CST[name][0]:CST[name][1]]

    ident = k_("ident")

    ctx = ExitStack()
    with ctx:
        PS = ctx.enter_context(nc.psum_tensor("PS", [P, 8, CHUNK], F32))

        def sem(name):
            return ctx.enter_context(nc.semaphore(name))

        (x_in, stage_in, cst_in, small_in, rowgain_in, w_out_in, x_again, outs) = map(sem, (
            "x_in", "stage_in", "cst_in", "small_in", "rowgain_in", "w_out_in", "x_again", "outs"))
        wmod_in = [sem(f"wmod_in{j}") for j in range(4)]
        w_in_in = [sem(f"w_in_in{n}") for n in range(3)]
        slot_full = [sem(f"slot_full{j}_{h}") for j in range(6) for h in range(2)]
        slot_used = [sem(f"slot_used{j}_{h}") for j in range(6) for h in range(2)]
        (dve_own, pool_own, bf_ready, spad_zero, cols_done, spad_ready, ncol_ready, in_sq, in_rstd, xn_ready,
         mod_done, modrow_ready, modx_done, modx_taken, xt_done, hTx_ready, hTc_ready, qkv_done,
         pn_ready, bsq_ready, brstd_ready, roped, high_ready, heads_ready, stk_t) = map(sem, (
            "dve_own", "pool_own", "bf_ready", "spad_zero", "cols_done", "spad_ready", "ncol_ready",
            "in_sq", "in_rstd", "xn_ready", "mod_done", "modrow_ready", "modx_done", "modx_taken",
            "xt_done", "hTx_ready", "hTc_ready", "qkv_done", "pn_ready", "bsq_ready", "brstd_ready",
            "roped", "high_ready", "heads_ready", "stk_t"))
        stk_evac = [sem("stk_evac_act"), sem("stk_evac_dve")]
        (sc_done, nm_ready, p_ready, pt_done, ptl_ready, ptc_ready, sink_ready, av_done, o_evac, ot_done, onat_ready,
         grp_sq, grp_rstd, oT_ready, ont_done, mix_sq, mix_rstd, ffn_sq, ffn_rstd,
         xn2_ready, high_cut, mid_cut, rest_ready, parts_ready, h2t_done, h2T_a, h2T_d, lg_done, gdiff, gexp_ready,
         d21_ready, e21_ready, mask_ready, pos_done, route_ready) = map(sem, (
            "sc_done", "nm_ready", "p_ready", "pt_done", "ptl_ready", "ptc_ready", "sink_ready", "av_done", "o_evac",
            "ot_done", "onat_ready", "grp_sq", "grp_rstd", "oT_ready", "ont_done", "mix_sq",
            "mix_rstd", "ffn_sq", "ffn_rstd", "xn2_ready", "high_cut", "mid_cut", "rest_ready",
            "parts_ready", "h2t_done", "h2T_a", "h2T_d", "lg_done", "gdiff", "gexp_ready", "d21_ready",
            "e21_ready", "mask_ready", "pos_done", "route_ready"))
        proj_done = [sem("projA_done"), sem("projB_done")]
        (zeroed, M_ready, MW_ready, gx_done, xT_a, xT_d, silu_ready, scat_done, acc_added,
         mwt_done, mt_ready, hid_ready, hidT_done, hidT_ready, yH_ready, y_split, shifted,
         end_sq, end_rstd, end_scaled) = map(sem, (
            "zeroed", "M_ready", "MW_ready", "gx_done", "xT_a", "xT_d", "silu_ready",
            "scat_done", "acc_added", "mwt_done", "mt_ready", "hid_ready", "hidT_done", "hidT_ready",
            "yH_ready", "y_split", "shifted", "end_sq", "end_rstd", "end_scaled"))
        end_ready = [sem("end_first_ready"), sem("end_second_ready")]
        final_added, y_half, bmod_in, sum_ready, ta_ready, ctx_in, xtx_out, xtc_out = map(sem, (
            "final_added", "y_half", "bmod_in", "sum_ready", "ta_ready", "ctx_in", "xtx_out", "xtc_out"))
        last_split, last_scat, row_done, row_taken, wr_ready, mixg_ready, x1_ready = map(sem, (
            "last_split", "last_scat", "row_done", "row_taken", "wr_ready", "mixg_ready", "x1_ready"))

        block = ctx.enter_context(nc.Block())

        GROUPS = {ti: (range(6) if ti < NT else range(4, 6)) for ti in range(NT + NC)}
        TURN = [0, 1, NT, 2, 3, NT + 1]
        LAST_TURN = len(TURN) - 1
        MODS = {1: 4, 4: 8}
        SHADOW = {2: 6, 5: 10}
        BANKS = [3 if ti < NT else 2 for ti in TURN]
        ROPED = [sum(2 if ti < NT else 1 for ti in TURN[:t]) for t in range(len(TURN))]
        STK = {}
        for ti in TURN:
            for g in GROUPS[ti]:
                STK[ti, g] = len(STK)

        def stk_count(upto, parity):
            return (upto + 1 - parity) // 2

        UNITS = [(pr, qt, hh) for pr in range(8) for qt in range(NT) for hh in range(2)]

        def window(pr, qt):
            return (max(0, qt - 1), min(NT - 1, qt + 1)) if pr < 4 else (0, NT - 1)

        def score_span(pr, qt):
            lo, hi = window(pr, qt)
            n = (hi - lo + 1) * P
            return (0, n + CTX) if n + CTX <= CHUNK else (CHUNK - n, CHUNK + CTX)

        def kv_head(pr):
            return pr // 2

        def heads_evac(ti, parity, eng, copy):
            for g in GROUPS[ti]:
                n = STK[ti, g]
                if n % 2 != parity:
                    continue
                eng.wait_ge(stk_t, n + 1)
                src = PS[:, 3 * (TURN.index(ti) % 2) + g % 3, :]
                cols = slice(ti * P, (ti + 1) * P)
                if g < 4:
                    copy(Q[:, 4 * g:4 * g + 4, cols], src.rearrange("p (h t) -> p h t", h=4)).then_inc(stk_evac[parity], 1)
                else:
                    v = 2 * (g - 4)
                    copy(K[:, v:v + 2, :, cols],
                         src.rearrange("p (v o t) -> p v o t", v=2, o=2)).then_inc(stk_evac[parity], 1)

        def down_slot(j):
            return slot[j][:, :, :, :].rearrange("p e k n -> p (e k n)").rearrange("p (e k n) -> p e k n", e=2, k=2)

        def both(ti):
            return PS[:, 2 * ti:2 * ti + 2, :].rearrange("p b n -> p (b n)")

        def mod_slot(i):
            return i if i < 4 else i % 2

        SMALL = 16 * 7

        @block.sync
        def _(sp):
            row = lambda v, k: v.rearrange("(k p) -> k p", p=P)
            for v, a in ((c[0], 0), (c_ctx, 8), (attn_pre[0], 16), (ffn_pre[0], 24), (a_out[0], 32), (b_out[0], 36)):
                n = v.shape[0] // P
                sp.dma_start(stage[a:a + n, :], row(v, n)).then_inc(stage_in, 16)

            def load_mod(i):
                if i >= 4:
                    sp.wait_ge(mod_done, i - 3 if i < 6 else i - 1)
                sp.dma_start(mslot[mod_slot(i)][:, :, :],
                             w_mod[0][:, i * CHUNK:(i + 1) * CHUNK].rearrange("(k p) n -> p k n", p=P)
                             ).then_inc(wmod_in[mod_slot(i)], 16)

            load_mod(0)
            sp.dma_start(xin[:, 0:NT, :], x[0].rearrange("(t p) d -> p t d", p=P)).then_inc(x_in, 16)
            sp.dma_start(xin[:, NT:, :], ctx_tok[0].rearrange("(t p) d -> p t d", p=P)).then_inc(ctx_in, 16)
            for i in range(1, 4):
                load_mod(i)
            for n in range(3):
                sp.dma_start(win[:, :, n * 512:(n + 1) * 512],
                             w_in[0][:, n * 512:(n + 1) * 512].rearrange("(k p) n -> p k n", p=P)
                             ).then_inc(w_in_in[n], 16)
            for i in range(4, NMOD):
                load_mod(i)

            def load_half(i, pair):
                j, h = i // 2, i % 2
                w = (w_gate, w_up, w_down)[j // 2][0]
                rows = w.shape[1] // 4
                at_ = (2 * (j % 2) + h) * rows
                if j >= 4:
                    sp.dma_start(down_slot(j)[:, :, h, :], w[bass.ds(pair * 2, 2), at_:at_ + rows, :].rearrange(
                                     "a p n -> p a n")).then_inc(slot_full[i], 16)
                    return
                for e in range(2):
                    sp.dma_start(slot[j][:, e, 2 * h:2 * h + 2, :],
                                 w[bass.ds(pair * 2 + e, 1), at_:at_ + rows, :].rearrange(
                                     "a (k p) n -> p (a k) n", p=P)).then_inc(slot_full[i], 16)

            def load_slot(j, pair):
                for h in range(2):
                    load_half(2 * j + h, pair)

            sp.wait_ge(qkv_done, 3 * NT + 2 * NC)
            sp.dma_start(wout[:, :, :], w_out[0].rearrange("(k p) n -> p k n", p=P)).then_inc(w_out_in, 16)
            sp.wait_ge(sc_done, len(UNITS))
            sp.dma_start(x1[:, :, :], x[0].rearrange("(t p) d -> p t d", p=P)).then_inc(x_again, 16)
            sp.wait_ge(av_done, 8)
            for j in (0, 3, 5):
                load_slot(j, 0)
            sp.wait_ge(proj_done[1], NT)
            load_slot(2, 0)
            sp.wait_ge(x1_ready, NT)
            load_slot(1, 0)
            sp.wait_ge(parts_ready, NT)
            sp.wait_ge(ffn_sq, NT)
            load_slot(4, 0)
            with sp.Fori(1, PAIRS) as p:
                for i in range(12):
                    sp.wait_ge(slot_used[i], p)
                    load_half(i, p)
            sp.wait_ge(route_ready, 1)
            fullest = sp.value_load(cmax[0:1, 0:1], min_val=0, max_val=SEQ)
            with sp.If(fullest > CAP):
                with sp.Fori(1, ROUNDS) as r:
                    with sp.If(fullest > r * CAP):
                        with sp.Fori(0, PAIRS) as p:
                            for i in range(12):
                                sp.wait_ge(slot_used[i], r * PAIRS + p)
                                load_half(i, p)
            for ti in (0, 2, 1, 3):
                sp.wait_ge(end_ready[ti // (NT // 2)], ti % (NT // 2) + 1)
                sp.dma_start(out[0, ti * P:(ti + 1) * P, :], acc[:, ti, :]).then_inc(outs, 16)
            sp.wait_ge(outs, 16 * NT)

        @block.tensor
        def _(pe):
            mm, tr = nc.tensor.matmul, nc.tensor.transpose
            pe.wait_ge(stage_in, 96)
            pe.wait_ge(cst_in, 32)
            tr(PS[:, 7, 0:40], stage[:, :], ident[0:40, 0:40]).then_inc(cols_done, 1)

            def mod_chunk(i):
                pe.wait_ge(wmod_in[mod_slot(i)], 16 if i < 4 else 16 * ((i - 4) // 2 + 2))
                if i:
                    pe.wait_ge(modrow_ready, i)
                for kk in range(2):
                    for g in range(4):
                        mm(PS[32 * g:32 * g + 32, 6, :], spad[:, 2 * g + kk, :], mslot[mod_slot(i)][:, 2 * g + kk, :],
                           start=(kk == 0), stop=(kk == 1 and g > 0))
                mm(PS[0:32, 6, :], ident[0:NMOD, i:i + 1].to_broadcast([NMOD, 32]), bmod[:, :],
                   start=False, stop=True).then_inc(mod_done, 1)

            def mod_spread(i):
                pe.wait_ge(modrow_ready, i + 1)
                if i:
                    pe.wait_ge(modx_taken, i)
                else:
                    pe.wait_ge(ncol_ready, 1)
                if i // 2 in (2, 5):
                    last = mm(PS[:, 7, :], k_("selb"), modrow[:, :], start=True, stop=True)
                else:
                    for b in range(4):
                        last = mm(PS[:, 7, 2 * b:2 * b + 2], modrow[:, b * P:(b + 1) * P], k_("sel2"),
                                  start=True, stop=True)
                last.then_inc(modx_done, 1)

            pe.wait_ge(spad_ready, 2)
            pe.wait_ge(bmod_in, 16)

            def x_transposes(ks):
                for k in ks:
                    b = 2 * (k % 3)
                    if k >= 3:
                        pe.wait_ge(xtx_out, k - 2)
                        pe.wait_ge(xtc_out, k - 2)
                    for ti in range(NT + NC):
                        o = PS[:, b + ti // 4, (ti % 4) * P:(ti % 4 + 1) * P]
                        last = tr(o, xin[:, ti, k * P:(k + 1) * P], ident)
                    last.then_inc(xt_done, 1)

            for i in (0, 1):
                mod_chunk(i)
                mod_spread(i)
            pe.wait_ge(xn_ready, NT + NC)
            x_transposes(range(0, KD // 2))
            mod_chunk(2)
            x_transposes(range(KD // 2, KD))
            mod_spread(2)
            mod_chunk(3)
            mod_spread(3)
            pe.wait_ge(xtx_out, KD)
            pe.wait_ge(xtc_out, KD)

            def head_transposes(t, groups=None):
                ti = TURN[t]
                pe.wait_ge(heads_ready, 2 * (t + 1))
                for g in groups or GROUPS[ti]:
                    n = STK[ti, g]
                    b = 3 * (t % 2) + g % 3
                    if g >= 3 and ti < NT:
                        pe.wait_ge(stk_evac[(n - 3) % 2], (n - 3) // 2 + 1)
                    for q in range(4):
                        src = QS[:, 4 * g + q, :] if g < 4 else KS[:, 2 * (g - 4) + q // 2, q % 2, :]
                        last = tr(PS[:, b, q * P:(q + 1) * P], src.bitcast(F32), ident)
                    last.then_inc(stk_t, 1)

            def project(t):
                ti = TURN[t]
                if ti == NT:
                    pe.wait_ge(hTc_ready, KD)
                b = 3 * (t % 2)
                for n in range(BANKS[t]):
                    if t == 0:
                        pe.wait_ge(w_in_in[n], 16)
                    if t >= 2:
                        for g in range(3 + n, 6 if n == BANKS[t] - 1 else 4 + n):
                            if g in GROUPS[TURN[t - 2]]:
                                done = STK[TURN[t - 2], g]
                                pe.wait_ge(stk_evac[done % 2], done // 2 + 1)
                    o, lo, hi = ((PS[:, b + n, :], 512 * n, 512 * n + 512) if ti < NT
                                 else (PS[:, b + n, 0:256], 512 + 768 * n, 768 + 768 * n))
                    for k in range(KD):
                        if t == 0 and n == 0:
                            pe.wait_ge(hTx_ready, k + 1)
                        last = mm(o, hT[:, k, ti * P:(ti + 1) * P], win[:, k, lo:hi], start=(k == 0), stop=(k == KD - 1))
                        if k == KD - 1:
                            last.then_inc(qkv_done, 1)
                        if t in MODS and n == 2 and k == 1:
                            mod_spread(MODS[t] + 1)
                        groups = GROUPS[TURN[t - 1]]
                        if t and n == 2 and k >= 2 and k - 2 < len(groups):
                            head_transposes(t - 1, [groups[k - 2]])
                    if t in MODS and n < 2:
                        if n:
                            mod_spread(MODS[t])
                        mod_chunk(MODS[t] + n)

            def router_row():
                pe.wait_ge(small_in, SMALL)
                pe.wait_ge(pn_ready, sum(BANKS))
                for k in range(KD):
                    last = mm(PS[:, 3, 0:NG + NE], modcol[:, 2, 0, k:k + 1].to_broadcast([P, P]), wr[:, k, :],
                              start=(k == 0), stop=(k == KD - 1))
                last.then_inc(row_done, 1)

            for t in range(NT + NC):
                project(t)
                if t in SHADOW:
                    mod_spread(SHADOW[t])
                    mod_chunk(SHADOW[t] + 1)
                if t and BANKS[t] == 2:
                    head_transposes(t - 1)
                if t in SHADOW:
                    mod_spread(SHADOW[t] + 1)
                if t + 1 in SHADOW:
                    mod_chunk(SHADOW[t + 1])
            router_row()
            head_transposes(LAST_TURN)
            pe.wait_ge(stk_evac[0], stk_count(len(STK), 0))
            pe.wait_ge(stk_evac[1], stk_count(len(STK), 1))
            pe.wait_ge(modx_taken, NMOD)

            pe.wait_ge(bf_ready, 1)
            def scores(u):
                pr, qt, hh = UNITS[u]
                if u >= 2:
                    pe.wait_ge(p_ready, u - 1)
                kv, h = kv_head(pr), 2 * pr + hh
                lo, hi = window(pr, qt)
                off, end = score_span(pr, qt)
                q = Q[:, h, qt * P:(qt + 1) * P]
                masks = [(m, jb) for m, jb in ((0, qt - 1), (1, qt + 1)) if pr < 4 and 0 <= jb < NT]
                S = PS[:, 2 * (u % 2):2 * (u % 2) + 2, :].rearrange("p b n -> p (b n)")
                if end <= CHUNK:
                    o = S[:, 0:end].rearrange("p (a n) -> p a n", a=2)
                    a = lo * P // CTX
                    keys = lambda part: K[:, kv, part, :].rearrange("p (c n) -> p c n", n=CTX)[:, a::2 - a, :]
                else:
                    o = S[:, off:CHUNK]
                    keys = lambda part: K[:, kv, part, lo * P:(hi + 1) * P]
                mm(o, q, keys(0), start=True, stop=False)
                last = mm(o, q, keys(1), start=False, stop=not masks)
                for m, jb in masks:
                    at_ = off + (jb - lo) * P
                    last = mm(S[:, at_:at_ + P], identb[:, :], maskw[:, m, :], start=False, stop=(m, jb) == masks[-1])
                if end > CHUNK:
                    mm(S[:, CHUNK:end], q, K[:, kv, 0, SEQ:], start=True, stop=False)
                    last = mm(S[:, CHUNK:end], q, K[:, kv, 1, SEQ:], start=False, stop=True)
                last.then_inc(sc_done, 1)

            def prob_transposes(u):
                pr, qt, hh = UNITS[u]
                lo, hi = window(pr, qt)
                pe.wait_ge(p_ready, u + 1)
                if u:
                    pe.wait_ge(ptl_ready, u)
                    pe.wait_ge(ptc_ready, u)
                off, end = score_span(pr, qt)
                for n in range(hi - lo + 1):
                    tr(PS[:, 4, n * P:(n + 1) * P], Pb[:, u % 4, off + n * P:off + (n + 1) * P], ident)
                for n in range(2):
                    last = tr(PS[:, 5, n * P:(n + 1) * P], Pb[:, u % 4, end - CTX + n * P:end - CTX + (n + 1) * P], ident)
                last.then_inc(pt_done, 1)

            def values(pr, n):
                kv = kv_head(pr)
                if n == 0:
                    pe.wait_ge(ptl_ready, 8 * (pr + 1))
                    pe.wait_ge(ptc_ready, 8 * (pr + 1))
                    if pr:
                        pe.wait_ge(o_evac, pr)
                kb = (4, 0, 1, 2, 3, 5)[n]
                q0, q1 = (0, SEQ) if kb >= 4 or pr >= 4 else (max(0, kb - 1) * P, (min(NT - 1, kb + 1) + 1) * P)
                for hh in range(2):
                    last = mm(PS[64 * hh:64 * hh + 64, 6, q0:q1], V[:, kb, kv * HD:(kv + 1) * HD],
                              PT[pr % 2][:, hh, kb, q0:q1], start=(n == 0), stop=(n == 5))
                if n == 5:
                    last.then_inc(av_done, 1)

            def o_transposes(pr):
                pe.wait_ge(o_evac, pr + 1)
                if pr:
                    pe.wait_ge(oT_ready, pr)
                for qt in range(NT):
                    last = tr(PS[:, 7, qt * P:(qt + 1) * P], oTs[:, qt * P:(qt + 1) * P], ident)
                last.then_inc(ot_done, 1)

            def o_again(pr):
                pe.wait_ge(onat_ready, pr + 1)
                for qt in range(NT):
                    last = tr(PS[:, 7, qt * P:(qt + 1) * P], onat[:, qt, pr * P:(pr + 1) * P], ident)
                last.then_inc(ont_done, 1)

            scores(0)
            pe.wait_ge(row_taken, 1)
            scores(1)
            for u, (pr, qt, hh) in enumerate(UNITS):
                if pr >= 4:
                    prob_transposes(u)
                if u + 2 < len(UNITS):
                    scores(u + 2)
                if pr < 4:
                    prob_transposes(u)
                if pr and 1 <= u % 8 <= 6:
                    values(pr - 1, u % 8 - 1)
                if pr >= 2 and u % 8 == 3:
                    o_again(pr - 2)
                if pr and u % 8 == 7:
                    o_transposes(pr - 1)
            for n in range(NKB):
                values(7, n)
            o_again(6)

            def out_project(ti, g, halves=(0, 1)):
                for n in halves:
                    if ti and n == 0:
                        pe.wait_ge(sum_ready if g else ta_ready, ti)
                    if ti and g and n:
                        h2_transposes(ti - 1)
                    for k in range(KD // 2):
                        last = mm(PS[:, 4 + 2 * g + n, :], oT[g][:, k, ti * P:(ti + 1) * P],
                                  wout[:, 4 * g + k, n * 512:(n + 1) * 512], start=(k == 0), stop=(k == KD // 2 - 1))
                    if n:
                        last.then_inc(proj_done[g], 1)

            def h2_transposes(ti):
                pe.wait_ge(x1_ready, ti + 1)
                if ti:
                    pe.wait_ge(h2T_a, ti)
                    pe.wait_ge(h2T_d, ti)
                for k in range(KD):
                    last = tr(PS[:, k // 4, (k % 4) * P:(k % 4 + 1) * P], x1[:, ti, k * P:(k + 1) * P], ident)
                last.then_inc(h2t_done, 1)

            def logits(ti):
                if ti == 0:
                    pe.wait_ge(wr_ready, 1)
                pe.wait_ge(h2T_a, ti + 1)
                pe.wait_ge(h2T_d, ti + 1)
                w = NG + NE
                for k in range(KD):
                    last = mm(PS[:, 2, ti * w:(ti + 1) * w], h2T[:, k, ti * P:(ti + 1) * P], wr[:, k, :],
                              start=(k == 0), stop=(k == KD - 1))
                last.then_inc(lg_done, 1)

            pe.wait_ge(w_out_in, 16)
            pe.wait_ge(oT_ready, 6)
            pe.wait_ge(ptl_ready, len(UNITS))
            pe.wait_ge(ptc_ready, len(UNITS))
            out_project(0, 0, (0,))
            o_transposes(7)
            out_project(0, 0, (1,))
            o_again(7)
            pe.wait_ge(oT_ready, 8)
            out_project(0, 1)
            for ti in range(1, NT):
                out_project(ti, 0)
                if ti >= 2:
                    logits(ti - 2)
                out_project(ti, 1)
            logits(NT - 2)
            h2_transposes(NT - 1)
            logits(NT - 1)

            pe.wait_ge(mask_ready, 1)
            for ti in range(NT):
                for tj in range(ti + 1):
                    mm(PS[:, 3, ti * NE:(ti + 1) * NE], beforeb[:, :] if tj == ti else onesb[:, :],
                       maskb[:, tj, :], start=(tj == 0), stop=(tj == ti))
            for tj in range(NT):
                last = mm(PS[:, 3, NT * NE:(NT + 1) * NE], onesb[:, :], maskb[:, tj, :], start=(tj == 0), stop=(tj == NT - 1))
            last.then_inc(pos_done, 1)

            SCAT_BANKS = (6, 7, 5)

            def gather(n, ks=range(KD)):
                if 0 in ks:
                    pe.wait_ge(M_ready, n + 1)
                for k in ks:
                    for part in range(3):
                        for ti in range(NT):
                            last = mm(PS[:, k // 4, (k % 4) * P:(k % 4 + 1) * P],
                                      xparts[:, part, ti, k * P:(k + 1) * P],
                                      M[:, ti, :, :].rearrange("p e c -> p (e c)"),
                                      start=(part == 0 and ti == 0), stop=(part == 2 and ti == NT - 1))
                    if k % 4 == 3:
                        last.then_inc(gx_done, 1)

            def scatter(s, bank, done, start=True):
                o = PS[:, bank, :]
                lhs = MT[:, s // 2 * P:(s // 2 + 1) * P]
                half = slice(s % 2 * CHUNK, (s % 2 + 1) * CHUNK)
                mm(o, lhs, yH[:, half], start=start, stop=False)
                mm(o, lhs, yL[:, half], start=False, stop=True).then_inc(done, 1)

            def product(m, it, between=None):
                for k in range(KD):
                    j = 2 * m + k // 4
                    if m == 0 and k == 4:
                        pe.wait_ge(xT_a, it + 1)
                    if k % 2 == 0:
                        pe.wait_ge(slot_full[4 * m + k // 2], 32 * it + 32)
                    for e in range(2):
                        last = mm(PS[CAP * e:CAP * (e + 1), 3 + m, :], xT[:, k, CAP * e:CAP * (e + 1)],
                                  slot[j][:, e, k % 4, :], start=(k == 0), stop=(k == KD - 1))
                    if k % 2 == 1:
                        last.then_inc(slot_used[4 * m + k // 2], 1)
                    if between:
                        between(k)

            def expert_pair(it, more=True):
                pe.wait_ge(xT_d, it + 1)
                pe.wait_ge(hid_ready, it + 1)

                def scatter_step(s):
                    if s >= 3:
                        pe.wait_ge(acc_added, it * 8 + (s - 2))
                    scatter(s, SCAT_BANKS[s % 3], scat_done)

                def two_steps(k):
                    if k == 4:
                        pe.wait_ge(mt_ready, it + 1)
                        pe.wait_ge(y_split, it + 1)
                    if k >= 4:
                        scatter_step(2 * (k - 4))
                        scatter_step(2 * (k - 4) + 1)

                product(0, it, between=None if more else two_steps)
                pe.wait_ge(MW_ready, it + 1)
                pe.wait_ge(mt_ready, it + 1)
                for ti in range(NT):
                    last = tr(PS[:, 2, ti * P:(ti + 1) * P], MW[:, ti, :, :].rearrange("p e c -> p (e c)"), ident)
                last.then_inc(mwt_done, 1)
                pe.wait_ge(y_split, it + 1)
                product(1, it, between=scatter_step if more else None)
                if more:
                    gather(it + 1, range(0, 6))
                pe.wait_ge(hid_ready, it + 2)
                pe.wait_ge(acc_added, it * 8 + 8)
                for f in range(KF):
                    last = tr(PS[:, 5, f * P:(f + 1) * P], hid[:, f * P:(f + 1) * P], ident)
                last.then_inc(hidT_done, 1)
                if more:
                    gather(it + 1, range(6, KD))
                pe.wait_ge(hidT_ready, it + 1)
                for f in range(KF):
                    pe.wait_ge(slot_full[8 + f], 16 * it + 16)
                    for n in range(2):
                        for e in range(2):
                            last = mm(PS[CAP * e:CAP * (e + 1), 6 + n, :], hidT[:, f, CAP * e:CAP * (e + 1)],
                                      down_slot(4 + f // 2)[:, e, f % 2, n * 512:(n + 1) * 512],
                                      start=(f == 0), stop=(f == KF - 1))
                        if f == KF - 1 and n == 0:
                            last.then_inc(y_half, 1)
                    last.then_inc(slot_used[8 + f], 1)

            pe.wait_ge(parts_ready, NT)

            def one_round(it0):
                gather(it0)
                with pe.Fori(0, PAIRS - 1) as p:
                    expert_pair(it0 + p)
                expert_pair(it0 + PAIRS - 1, more=False)

            one_round(0)
            fullest = pe.value_load(cmax[0:1, 0:1], min_val=0, max_val=SEQ)
            with pe.If(fullest > CAP):
                with pe.Fori(1, ROUNDS) as r:
                    with pe.If(fullest > r * CAP):
                        one_round(r * PAIRS)
            for n in range(2):
                mm(PS[:, n, :], ident, acc[:, 0, n * CHUNK:(n + 1) * CHUNK], start=True, stop=False)
            pe.wait_ge(last_split, 1)
            for s in range(8):
                scatter(s, s, last_scat, start=s >= 2)

        @block.scalar
        def _(act):
            fn = nc.scalar.activation
            act.dma_start(cst[:, :], cst_dram[:, 0:CST_KEPT]).then_inc(cst_in, 16)
            act.dma_start(cst_raw[:, :], cst_dram[:, CST_KEPT:]).then_inc(cst_in, 16)

            def spread(v, shape):
                return v.rearrange("(a n) -> a n", a=1).to_broadcast(shape)

            act.dma_start(bmod[:, :], b_mod[0].rearrange("(i n) -> i n", n=CHUNK)).then_inc(bmod_in, 16)
            act.dma_start(wr[:, :, 0:NG], w_group[0].rearrange("(k p) n -> p k n", p=P)).then_inc(small_in, 16)
            act.dma_start(wr[:, :, NG:], w_router[0].rearrange("(k p) n -> p k n", p=P)).then_inc(small_in, 16)
            act.dma_start(rbias[:, 0:NG], spread(b_group[0], [P, NG])).then_inc(small_in, 16)
            act.dma_start(rbias[:, NG:], spread(b_router[0], [P, NE])).then_inc(small_in, 16)
            act.dma_start(sink[:, :], spread(a_sink[0], [P, 8])).then_inc(small_in, 16)
            act.dma_start(gains[:, 0, :], spread(bq_norm[0], [P, HD])).then_inc(small_in, 16)
            act.dma_start(gains[:, 8, :], spread(bk_norm[0], [P, HD])).then_inc(small_in, 16)
            act.dma_start(g1p[:, :], spread(attn_post[0], [P, D])).then_inc(rowgain_in, 16)
            act.dma_start(g2p[:, :], spread(ffn_post[0], [P, D])).then_inc(rowgain_in, 16)
            act.wait_ge(cols_done, 1)
            act.wait_ge(spad_zero, 1)
            for who in range(2):
                fn(spad[:, :, who], PS[:, 7, 8 * who:8 * who + 8], ACT.Silu).then_inc(spad_ready, 1)
            def mod_row(i):
                act.wait_ge(mod_done, i + 1)
                if i:
                    act.wait_ge(modx_done, i)
                fn(modrow[:, :], PS[:, 6, :], ACT.Copy).then_inc(modrow_ready, 1)

            mod_row(0)
            act.wait_ge(x_in, 16)
            for ti in range(NT + NC):
                if ti:
                    act.wait_ge(in_sq, ti)
                if ti == NT:
                    act.wait_ge(ctx_in, 16)
                fn(junk_in[:, :], xin[:, ti, :], ACT.Square, accum_out=ss[:, S_IN + ti:S_IN + ti + 1]).then_inc(in_sq, 1)
            act.wait_ge(in_rstd, 1)
            for ti in range(NT, NT + NC):
                fn(xin[:, ti, :], xin[:, ti, :], ACT.Copy, scale=rstd[:, S_IN + ti:S_IN + ti + 1]).then_inc(xn_ready, 1)

            def ctx_out(ks):
                for k in ks:
                    act.wait_ge(xt_done, k + 1)
                    fn(hT[:, k, SEQ:], PS[:, 2 * (k % 3) + 1, 0:CTX], ACT.Copy).then_inc(xtc_out, 1)

            mod_row(1)
            ctx_out(range(0, KD // 2))
            mod_row(2)
            ctx_out(range(KD // 2, KD))
            mod_row(3)
            act.wait_ge(modx_taken, 4)
            act.wait_ge(xtc_out, KD)
            for k in range(KD):
                fn(hT[:, k, SEQ:], hT[:, k, SEQ:], ACT.Identity,
                   bias=modcol[:, 0, 1, k:k + 1], scale=modcol[:, 1, 1, k:k + 1]).then_inc(hTc_ready, 1)

            def heads_out(t):
                ti = TURN[t]
                if t:
                    act.wait_ge(heads_ready, 2 * t)
                b = 3 * (t % 2)
                done = sum(BANKS[:t])
                for n in range(BANKS[t]):
                    if t and n == 2:
                        heads_evac(TURN[t - 1], 0, act, act_copy)
                    act.wait_ge(qkv_done, done + n + 1)
                    if ti < NT:
                        fn(pn[:, n * 512:(n + 1) * 512], PS[:, b + n, :], ACT.Copy).then_inc(pn_ready, 1)
                    else:
                        fn(pn[:, 512 + 768 * n:768 + 768 * n], PS[:, b + n, 0:256], ACT.Copy).then_inc(pn_ready, 1)
                    if t in MODS and n < 2:
                        mod_row(MODS[t] + n)
                act.wait_ge(pn_ready, done + BANKS[t])
                pg = pn[:, :].rearrange("p (g s) -> p g s", g=2)
                fn(V[:, ti, :].rearrange("p (g s) -> p g s", g=2), pg[:, :, 640:768], ACT.Copy).then_inc(heads_ready, 1)
                if t and BANKS[t] == 2:
                    heads_evac(TURN[t - 1], 0, act, act_copy)
                if t + 1 in SHADOW:
                    mod_row(SHADOW[t + 1])
                if t:
                    act.wait_ge(stk_t, STK[TURN[t - 1], 5] + 1)
                for g in range(2):
                    if ti < NT:
                        act.wait_ge(roped, ROPED[t] + g + 1)
                        fn(QS[:, 8 * g:8 * g + 8, 0:HD], pg[:, g, 0:512].rearrange("p (h d) -> p h d", d=HD), ACT.Copy)
                    elif g:
                        act.wait_ge(roped, ROPED[t] + 1)
                    src = pg[:, g, 512:640].rearrange("p (v o d) -> p v o d", v=2, o=1).to_broadcast([P, 2, 2, HD])
                    fn(KS[:, 2 * g:2 * g + 2, 0, :].rearrange("p v (o d) -> p v o d", o=2), src, ACT.Copy
                       ).then_inc(high_ready, 1)
                if t + 1 in SHADOW:
                    mod_row(SHADOW[t + 1] + 1)

            act_copy = lambda o, i: fn(o, i, ACT.Copy)
            for t in range(NT + NC):
                heads_out(t)
            heads_evac(TURN[LAST_TURN], 0, act, act_copy)

            def context_probs(u):
                pr, qt, hh = UNITS[u]
                act.wait_ge(pt_done, u + 1)
                if pr >= 2:
                    act.wait_ge(av_done, pr - 1)
                fn(PT[pr % 2][:, hh, 4:6, qt * P:(qt + 1) * P], PS[:, 5, 0:CTX].rearrange("p (b t) -> p b t", b=2),
                   ACT.Copy).then_inc(ptc_ready, 1)

            def o_copy(pr):
                act.wait_ge(av_done, pr + 1)
                if pr:
                    act.wait_ge(ot_done, pr)
                fn(oTs[:, :], PS[:, 6, :], ACT.Copy).then_inc(o_evac, 1)

            def oT_out(pr):
                act.wait_ge(ont_done, pr + 1)
                fn(oT[pr // 4][:, pr % 4, :], PS[:, 7, :], ACT.Copy, scale=ncol[:, 16 + pr:17 + pr]).then_inc(oT_ready, 1)

            def group_squares(g, tiles=range(NT)):
                act.wait_ge(onat_ready, 4 * (g + 1))
                for qt in tiles:
                    n = g * NT + qt
                    if n:
                        act.wait_ge(grp_sq, n)
                    fn(grp_junk[:, :], onat[:, qt, g * 512:(g + 1) * 512], ACT.Square,
                       accum_out=ss[:, S_GRP + n:S_GRP + n + 1]).then_inc(grp_sq, 1)

            fn(dens[:, 0, 0:1], k_("half")[:, 0:1], ACT.Exp)
            act.wait_ge(small_in, SMALL)
            for u, (pr, qt, hh) in enumerate(UNITS):
                off, end = score_span(pr, qt)
                if u and pr >= 4:
                    context_probs(u - 1)
                act.wait_ge(nm_ready, u + 1)
                if u >= 4:
                    act.wait_ge(pt_done, u - 3)
                S = PS[:, 2 * (u % 2):2 * (u % 2) + 2, :].rearrange("p b n -> p (b n)")
                fn(Pb[:, u % 4, off:end], S[:, off:end], ACT.Exp, bias=nm[:, u % 8:u % 8 + 1], scale=SCALE,
                   accum_out=rs[:, u:u + 1]).then_inc(p_ready, 1)
                if u and pr < 4:
                    context_probs(u - 1)
                if pr < 4:
                    h = 2 * pr + hh
                    fn(esn[:, u:u + 1], sink[:, h:h + 1], ACT.Exp, bias=nm[:, u % 8:u % 8 + 1]).then_inc(sink_ready, 1)
                if u % 8 == 7 and pr:
                    o_copy(pr - 1)
                if pr >= 2 and u % 8 == 4:
                    oT_out(pr - 2)
                if 44 <= u < 44 + NT:
                    group_squares(0, [u - 44])
            context_probs(len(UNITS) - 1)

            oT_out(6)
            o_copy(7)

            def mix_a(ti):
                act.wait_ge(proj_done[0], ti + 1)
                act.wait_ge(grp_rstd, 1)
                if ti:
                    act.wait_ge(sum_ready, ti)
                fn(mixA[:, :], PS[:, 4:6, :].rearrange("p b n -> p (b n)"), ACT.Copy,
                   scale=rstd[:, S_GRP + ti:S_GRP + ti + 1]).then_inc(ta_ready, 1)

            oT_out(7)
            mix_a(0)
            group_squares(1)

            def h2T_out(ti):
                act.wait_ge(h2t_done, ti + 1)
                fn(h2T[:, 0:4, ti * P:(ti + 1) * P], PS[:, 0, :].rearrange("p (k t) -> p k t", k=4), ACT.Copy
                   ).then_inc(h2T_a, 1)

            for ti in range(NT):
                act.wait_ge(sum_ready, ti + 1)
                if ti:
                    act.wait_ge(ffn_sq, ti)
                fn(junk[:, :], mix_tmp[:, :], ACT.Square,
                   accum_out=ss[:, S_MIX + ti:S_MIX + ti + 1]).then_inc(mix_sq, 1)
                act.wait_ge(x1_ready, ti + 1)
                act.wait_ge(mix_sq, ti + 1)
                fn(junk[:, :], x1[:, ti, :], ACT.Square,
                   accum_out=ss[:, S_FFN + ti:S_FFN + ti + 1]).then_inc(ffn_sq, 1)
                if ti == NT - 1:
                    h2T_out(ti)
                act.wait_ge(ffn_rstd, ti + 1)
                if ti >= 2:
                    act.wait_ge(rest_ready, ti - 1)
                fn(xn2[:, ti % 2, :], x1[:, ti, :], ACT.Copy, scale=rstd[:, S_FFN + ti:S_FFN + ti + 1]).then_inc(xn2_ready, 1)
                act.wait_ge(xn2_ready, ti + 1)
                fn(xparts[:, 0, ti, :], xn2[:, ti % 2, :], ACT.Copy).then_inc(high_cut, 1)
                if ti + 1 < NT:
                    mix_a(ti + 1)
                    h2T_out(ti)
                act.wait_ge(rest_ready, ti + 1)
                fn(xparts[:, 1, ti, :], rest_tmp[:, :], ACT.Copy).then_inc(mid_cut, 1)

            act.wait_ge(gdiff, 1)
            fn(gexp[:, :, :], g1t[:, :, :], ACT.Exp).then_inc(gexp_ready, 1)
            act.wait_ge(d21_ready, 1)
            fn(e21[:, :], mt_[:, :], ACT.Exp).then_inc(e21_ready, 1)

            def xT_upper(n):
                act.wait_ge(gx_done, n * 2 + 2)
                for k in range(4, KD):
                    last = fn(xT[:, k, :], PS[:, 1, (k - 4) * P:(k - 3) * P], ACT.Identity,
                              bias=modcol[:, 2, 0, k:k + 1], scale=modcol[:, 3, 0, k:k + 1])
                last.then_inc(xT_a, 1)

            def expert_pair(it, more=True):
                act.wait_ge(slot_used[3], it + 1)
                act.wait_ge(hid_ready, it + 1)
                fn(gate_act[:, :], PS[:, 3, :], ACT.Silu).then_inc(silu_ready, 1)
                if more:
                    xT_upper(it + 1)
                act.wait_ge(scat_done, it * 8 + 8)
                for n, done in enumerate((y_half, slot_used[11])):
                    act.wait_ge(done, it + 1)
                    fn(yH[:, n * 512:(n + 1) * 512], PS[:, 6 + n, :], ACT.Copy).then_inc(yH_ready, 1)

            def one_round(it0):
                xT_upper(it0)
                with act.Fori(0, PAIRS - 1) as p:
                    expert_pair(it0 + p)
                expert_pair(it0 + PAIRS - 1, more=False)

            act.wait_ge(h2T_a, NT)
            one_round(0)
            fullest = act.value_load(cmax[0:1, 0:1], min_val=0, max_val=SEQ)
            with act.If(fullest > CAP):
                with act.Fori(1, ROUNDS) as r:
                    with act.If(fullest > r * CAP):
                        one_round(r * PAIRS)
            for ti in range(NT):
                if ti:
                    act.wait_ge(final_added, ti)
                    act.wait_ge(end_sq, ti)
                else:
                    act.wait_ge(last_scat, 2)
                fn(end_junk[:, :], acc[:, ti, :] if ti else both(0), ACT.Square,
                   accum_out=ss[:, S_END + ti:S_END + ti + 1]).then_inc(end_sq, 1)

        @block.vector
        def _(dve):
            V_ = nc.vector
            tt, ts, cp = V_.tensor_tensor, V_.tensor_scalar, V_.tensor_copy
            own = [0]

            def then(ins):
                own[0] += 1
                ins.then_inc(dve_own, 1)
                dve.wait_ge(dve_own, own[0])

            dve.wait_ge(cst_in, 32)
            raw = lambda n: cst_raw[:, (CST[n][0] - CST_KEPT):(CST[n][1] - CST_KEPT)]
            cp(identb[:, :], ident)
            cp(maskw[:, 0, :], raw("prev"))
            cp(maskw[:, 1, :], raw("next"))
            cp(beforeb[:, :], raw("before"))
            V_.memset(onesb[:, :], 1.0).then_inc(bf_ready, 1)
            dve.wait_ge(spad_ready, 2)
            cp(ncol[:, :], PS[:, 7, 16:40]).then_inc(ncol_ready, 1)

            def mod_take(i):
                dve.wait_ge(modx_done, i + 1)
                part, half = i // 2, i % 2
                if part in (2, 5):
                    g = (g1p if part == 2 else g2p)[:, half * CHUNK:(half + 1) * CHUNK]
                    dve.wait_ge(rowgain_in, 32)
                    tt(g, PS[:, 7, :], g, ALU.mult).then_inc(modx_taken, 1)
                    return
                which = {0: 0, 1: 1, 3: 2, 4: 3}[part]
                for who in range(2):
                    src = PS[:, 7, 0:8].rearrange("p (b w) -> p b w", w=2)[:, :, who]
                    dst = modcol[:, which, who, 4 * half:4 * half + 4]
                    if which % 2 == 0:
                        last = cp(dst, src)
                    else:
                        base = 8 * (which // 2) + 4 * half
                        last = V_.scalar_tensor_tensor(out=dst, in0=src, scalar=1.0, in1=ncol[:, base:base + 4],
                                                       op0=ALU.add, op1=ALU.mult)
                last.then_inc(modx_taken, 1)

            dve.wait_ge(ncol_ready, 1)
            mod_take(0)
            dve.wait_ge(in_rstd, 1)
            for ti in range(NT):
                ts(xin[:, ti, :], xin[:, ti, :], rstd[:, S_IN + ti:S_IN + ti + 1], None, ALU.mult).then_inc(xn_ready, 1)
            mod_take(1)
            for k in range(KD):
                dve.wait_ge(xt_done, k + 1)
                cp(hT[:, k, 0:SEQ], PS[:, 2 * (k % 3), :]).then_inc(xtx_out, 1)
            dve.wait_ge(xtx_out, KD)
            for i in (2, 3):
                mod_take(i)
                dve.wait_ge(modx_taken, i + 1)
                for k in range(4 * (i - 2), 4 * (i - 1)):
                    ts(hT[:, k, 0:SEQ], hT[:, k, 0:SEQ], modcol[:, 1, 0, k:k + 1], modcol[:, 0, 0, k:k + 1],
                       ALU.mult, ALU.add).then_inc(hTx_ready, 1)
            dve.wait_ge(small_in, SMALL)
            then(ts(neg_sink[:, :], sink[:, :], -1.0, None, ALU.mult))
            cp(gains[:, 1:8, :], gains[:, 0:1, :].to_broadcast([P, 7, HD]))
            then(cp(gains[:, 9, :], gains[:, 8, :]))

            def heads_squares(t):
                dve.wait_ge(pn_ready, sum(BANKS[:t + 1]))
                if TURN[t] < NT:
                    n0, tmp = 0, rope_tmp[1][:, :, :]
                    if t:
                        dve.wait_ge(stk_t, STK[TURN[t - 1], 5] + 1)
                else:
                    n0, tmp = 8, ctx_tmp[:, :, :]
                bh = pn[:, 768 + 64 * n0:768 + 640].rearrange("p (h d) -> p h d", d=HD)
                then(tt(tmp, bh, bh, ALU.mult))
                V_.tensor_reduce(out=bss[:, n0:10], in_=tmp, axis=AX.X, op=ALU.add).then_inc(bsq_ready, 1)

            def heads(t):
                ti = TURN[t]
                latent = ti < NT
                n0 = 0 if latent else 8
                nb = 10 - n0
                bh = pn[:, 768 + 64 * n0:768 + 640].rearrange("p (h d) -> p h d", d=HD)
                pg = pn[:, :].rearrange("p (g s) -> p g s", g=2)

                def rotate(g):
                    qk = pg[:, g, 0:640].rearrange("p (h d) -> p h d", d=HD)
                    qk2 = pg[:, g, 0:640].rearrange("p (h i w) -> p h i w", i=HD // 2, w=2)
                    tmp = rope_tmp[g][:, :, :].rearrange("p h (i w) -> p h i w", w=2)
                    a = CST["sin"][0] + ti * HD
                    sn = cst[:, a:a + HD].rearrange("p (q i w) -> p q i w", q=1, w=2)
                    a = CST["cos"][0] + ti * HD
                    cs = cst[:, a:a + HD].rearrange("p (q d) -> p q d", q=1).to_broadcast([P, 10, HD])
                    for w in range(2):
                        last = tt(tmp[:, :, :, w], qk2[:, :, :, 1 - w],
                                  sn[:, :, :, w].to_broadcast([P, 10, HD // 2]), ALU.mult)
                    then(last)
                    then(tt(qk, qk, cs, ALU.mult))
                    tt(qk, qk, rope_tmp[g][:, :, :], ALU.add).then_inc(roped, 1)

                if latent:
                    heads_squares(t)
                    rotate(0)
                dve.wait_ge(brstd_ready, t + 1)
                then(tt(bh, bh, brs[:, n0:10].rearrange("p (h o) -> p h o", o=1).to_broadcast([P, nb, HD]), ALU.mult))
                last = tt(bh, bh, gains[:, n0:10, :], ALU.mult)
                if latent:
                    then(last)
                    rotate(1)
                else:
                    last.then_inc(roped, 1)
                if t:
                    dve.wait_ge(stk_t, STK[TURN[t - 1], 5] + 1)
                for g in range(2):
                    dve.wait_ge(high_ready, 2 * t + g + 1)
                    if latent:
                        tt(QS[:, 8 * g:8 * g + 8, HD:], pg[:, g, 0:512].rearrange("p (h d) -> p h d", d=HD),
                           QS[:, 8 * g:8 * g + 8, 0:HD].bitcast(F32), ALU.subtract)
                    src = pg[:, g, 512:640].rearrange("p (v o d) -> p v o d", v=2, o=1).to_broadcast([P, 2, 2, HD])
                    last = tt(KS[:, 2 * g:2 * g + 2, 1, :].rearrange("p v (o d) -> p v o d", o=2), src,
                              KS[:, 2 * g:2 * g + 2, 0, :].rearrange("p v (o d) -> p v o d", o=2).bitcast(F32),
                              ALU.subtract)
                last.then_inc(heads_ready, 1)

            for t in range(NT + NC):
                heads(t)
                if t + 1 in MODS:
                    mod_take(MODS[t + 1])
                    mod_take(MODS[t + 1] + 1)
                if t in SHADOW:
                    mod_take(SHADOW[t] + 1)
                if t + 1 in SHADOW:
                    mod_take(SHADOW[t + 1])
                if t == LAST_TURN:
                    dve.wait_ge(row_done, 1)
                    tt(rbias[:, :], PS[:, 3, 0:NG + NE], rbias[:, :], ALU.add).then_inc(row_taken, 1)
                if t < LAST_TURN and TURN[t + 1] >= NT:
                    heads_squares(t + 1)
                heads_evac(TURN[t], 1, dve, cp)
            def latent_probs(u):
                pr, qt, hh = UNITS[u]
                lo, hi = window(pr, qt)
                nb = hi - lo + 1
                dve.wait_ge(pt_done, u + 1)
                if pr >= 2:
                    dve.wait_ge(av_done, pr - 1)
                cp(PT[pr % 2][:, hh, lo:hi + 1, qt * P:(qt + 1) * P],
                   PS[:, 4, 0:nb * P].rearrange("p (b t) -> p b t", b=nb)).then_inc(ptl_ready, 1)

            def o_natural(pr):
                rsp = rs[:, 8 * pr:8 * pr + 8]
                den = dens[:, pr % 2, :]
                dve.wait_ge(p_ready, 8 * (pr + 1))
                if pr < 4:
                    dve.wait_ge(sink_ready, 8 * (pr + 1))
                    then(tt(den, rsp, esn[:, 8 * pr:8 * pr + 8], ALU.add))
                    rsp = den
                then(V_.reciprocal(den, rsp))
                dve.wait_ge(ot_done, pr + 1)
                r = den.rearrange("p (q h o) -> p q h o", h=2, o=1).to_broadcast([P, NT, 2, HD])
                tt(onat[:, :, pr * P:(pr + 1) * P].rearrange("p q (h d) -> p q h d", h=2),
                   PS[:, 7, :].rearrange("p (q h d) -> p q h d", q=NT, h=2), r, ALU.mult).then_inc(onat_ready, 1)

            dve.wait_ge(qkv_done, 3 * NT + 2 * NC)
            for u, (pr, qt, hh) in enumerate(UNITS):
                off, end = score_span(pr, qt)
                S = PS[:, 2 * (u % 2):2 * (u % 2) + 2, :].rearrange("p b n -> p (b n)")
                dve.wait_ge(sc_done, u + 1)
                then(V_.tensor_reduce(out=mx[:, u % 2:u % 2 + 1], in_=S[:, off:end], axis=AX.X, op=ALU.max))
                if u >= 8:
                    dve.wait_ge(p_ready, u - 7)
                    if 8 <= u < 40:
                        dve.wait_ge(sink_ready, u - 7)
                if pr < 4:
                    h = 2 * pr + hh
                    ts(nm[:, u % 8:u % 8 + 1], mx[:, u % 2:u % 2 + 1], -SCALE, neg_sink[:, h:h + 1],
                       ALU.mult, ALU.min).then_inc(nm_ready, 1)
                else:
                    ts(nm[:, u % 8:u % 8 + 1], mx[:, u % 2:u % 2 + 1], -SCALE, None, ALU.mult).then_inc(nm_ready, 1)
                if u:
                    latent_probs(u - 1)
                if u % 8 == 1 and pr >= 2:
                    o_natural(pr - 2)
            latent_probs(len(UNITS) - 1)
            o_natural(6)
            o_natural(7)

            def h2T_out(ti):
                dve.wait_ge(h2t_done, ti + 1)
                cp(h2T[:, 4:8, ti * P:(ti + 1) * P], PS[:, 1, :].rearrange("p (k t) -> p k t", k=4)).then_inc(h2T_d, 1)

            def low_part(ti):
                dve.wait_ge(mid_cut, ti + 1)
                tt(xparts[:, 2, ti, :], rest_tmp[:, :], xparts[:, 1, ti, :], ALU.subtract).then_inc(parts_ready, 1)

            dve.wait_ge(grp_rstd, 2)
            dve.wait_ge(x_again, 16)
            for ti in range(NT):
                dve.wait_ge(ta_ready, ti + 1)
                dve.wait_ge(proj_done[1], ti + 1)
                if ti:
                    dve.wait_ge(mixg_ready, ti)
                    dve.wait_ge(mix_sq, ti)
                n = S_GRP + NT + ti
                V_.scalar_tensor_tensor(out=mix_tmp[:, :], in0=PS[:, 6:8, :].rearrange("p b n -> p (b n)"),
                                        scalar=rstd[:, n:n + 1], in1=mixA[:, :], op0=ALU.mult, op1=ALU.add
                                        ).then_inc(sum_ready, 1)
                if ti:
                    dve.wait_ge(x1_ready, ti)
                dve.wait_ge(sum_ready, ti + 1)
                tt(mixg[:, :], mix_tmp[:, :], g1p[:, :], ALU.mult).then_inc(mixg_ready, 1)
                if ti:
                    low_part(ti - 1)
                dve.wait_ge(mix_rstd, ti + 1)
                dve.wait_ge(mixg_ready, ti + 1)
                V_.scalar_tensor_tensor(out=x1[:, ti, :], in0=mixg[:, :],
                                        scalar=rstd[:, S_MIX + ti:S_MIX + ti + 1], in1=x1[:, ti, :],
                                        op0=ALU.mult, op1=ALU.add).then_inc(x1_ready, 1)
                if ti == NT - 1:
                    h2T_out(ti)
                dve.wait_ge(high_cut, ti + 1)
                if ti:
                    dve.wait_ge(parts_ready, ti)
                tt(rest_tmp[:, :], xn2[:, ti % 2, :], xparts[:, 0, ti, :], ALU.subtract).then_inc(rest_ready, 1)
                if ti < NT - 1:
                    h2T_out(ti)
            dve.wait_ge(lg_done, NT)
            w = NG + NE
            dve.wait_ge(ffn_rstd, NT)
            for ti in range(NT):
                last = V_.scalar_tensor_tensor(out=lg[:, ti, :], in0=PS[:, 2, ti * w:(ti + 1) * w],
                                               scalar=rstd[:, S_FFN + ti:S_FFN + ti + 1], in1=rbias[:, :],
                                               op0=ALU.mult, op1=ALU.add)
            then(last)

            def col(v, n):
                return v[:, :].rearrange("p (t o) -> p t o", o=1).to_broadcast([P, NT, n])

            def first_max(one_hot, top, values, n):
                tmp = one_hot
                rev = k_("rev")[:, EPG - n:EPG].rearrange("p (o n) -> p o n", o=1).to_broadcast([P, NT, n])
                then(V_.tensor_reduce(out=top[:, :], in_=values, axis=AX.X, op=ALU.max))
                then(tt(tmp[:, :, :], values, col(top, n), ALU.is_equal))
                then(tt(tmp[:, :, :], tmp[:, :, :], rev, ALU.mult))
                then(V_.tensor_reduce(out=mt_[:, :], in_=tmp[:, :, :], axis=AX.X, op=ALU.max))
                then(tt(one_hot[:, :, :], tmp[:, :, :], col(mt_, n), ALU.is_equal))

            gl = lg[:, :, 0:NG]
            first_max(ohg, gmax, gl, NG)
            tt(g1t[:, :, :], gl, col(gmax, NG), ALU.subtract).then_inc(gdiff, 1)
            el = lg[:, :, NG:].rearrange("p t (g e) -> p t g e", g=NG)
            then(tt(picked[:, :, :, :], el,
                    ohg[:, :, :].rearrange("p t (g o) -> p t g o", o=1).to_broadcast([P, NT, NG, EPG]), ALU.mult))
            then(V_.tensor_reduce(out=es[:, :, :], in_=picked[:, :, :, :].rearrange("p t g e -> p t e g"),
                                  axis=AX.X, op=ALU.add))
            first_max(oh1, m1, es[:, :, :], EPG)
            then(V_.scalar_tensor_tensor(out=e1t[:, :, :], in0=oh1[:, :, :], scalar=NEG, in1=es[:, :, :],
                                         op0=ALU.mult, op1=ALU.add))
            first_max(oh2, m2, e1t[:, :, :], EPG)
            tt(mt_[:, :], m2[:, :], m1[:, :], ALU.subtract).then_inc(d21_ready, 1)
            then(tt(mke[:, :, :], oh1[:, :, :], oh2[:, :, :], ALU.add))

            def by_group(v):
                return v[:, :, :].rearrange("p t (o e) -> p t o e", o=1).to_broadcast([P, NT, NG, EPG])

            gsel = ohg[:, :, :].rearrange("p t (g o) -> p t g o", o=1).to_broadcast([P, NT, NG, EPG])
            tt(maskb[:, :, :].rearrange("p t (g e) -> p t g e", g=NG), gsel, by_group(mke), ALU.mult).then_inc(mask_ready, 1)
            tt(maskf[:, :, :].rearrange("p t (g e) -> p t g e", g=NG), gsel, by_group(mke), ALU.mult)
            V_.memset(cw[:, :, NE:], 0.0)
            then(V_.memset(slotval[:, :, NE:], -1.0))
            dve.wait_ge(pos_done, 1)
            then(V_.scalar_tensor_tensor(out=slotval[:, :, 0:NE],
                                         in0=PS[:, 3, 0:NT * NE].rearrange("p (t n) -> p t n", t=NT), scalar=1.0,
                                         in1=maskf[:, :, :], op0=ALU.add, op1=ALU.mult))
            ts(slotval[:, :, 0:NE], slotval[:, :, 0:NE], -1.0, None, ALU.add).then_inc(shifted, 1)

            def expert_weights():
                dve.wait_ge(gexp_ready, 1)
                then(V_.tensor_reduce(out=gsum[:, :], in_=gexp[:, :, :], axis=AX.X, op=ALU.add))
                then(V_.reciprocal(gw[:, :], gsum[:, :]))
                dve.wait_ge(e21_ready, 1)
                then(ts(w2t[:, :], e21[:, :], 1.0, None, ALU.add))
                then(V_.reciprocal(w1t[:, :], w2t[:, :]))
                then(tt(w1t[:, :], w1t[:, :], gw[:, :], ALU.mult))
                then(tt(w2t[:, :], w1t[:, :], e21[:, :], ALU.mult))
                tt(cwe[:, :, :], oh1[:, :, :], col(w1t, EPG), ALU.mult)
                then(tt(e1t[:, :, :], oh2[:, :, :], col(w2t, EPG), ALU.mult))
                then(tt(cwe[:, :, :], cwe[:, :, :], e1t[:, :, :], ALU.add))
                then(tt(cw[:, :, 0:NE].rearrange("p t (g e) -> p t g e", g=NG), gsel, by_group(cwe), ALU.mult))
                then(V_.tensor_reduce(out=cmaxf[:, :], in_=PS[:, 3, NT * NE:(NT + 1) * NE], axis=AX.X, op=ALU.max))
                cp(cmax[:, :], cmaxf[:, :]).then_inc(route_ready, 1)

            def match(pair):
                sv = slotval[:, :, bass.ds(pair * 2, 2)].rearrange("p t (e o) -> p t e o", o=1).to_broadcast([P, NT, 2, CAP])
                io = k_("iota").rearrange("p (o q c) -> p o q c", o=1, q=1).to_broadcast([P, NT, 2, CAP])
                tt(M[:, :, :, :], io, sv, ALU.is_equal).then_inc(M_ready, 1)

            def weigh(pair, n):
                dve.wait_ge(M_ready, n + 1)
                cv = cw[:, :, bass.ds(pair * 2, 2)].rearrange("p t (e o) -> p t e o", o=1).to_broadcast([P, NT, 2, CAP])
                tt(MW[:, :, :, :], M[:, :, :, :], cv, ALU.mult).then_inc(MW_ready, 1)

            def xT_lower(n):
                dve.wait_ge(gx_done, n * 2 + 1)
                for k in range(4):
                    last = ts(xT[:, k, :], PS[:, 0, k * P:(k + 1) * P], modcol[:, 3, 0, k:k + 1],
                              modcol[:, 2, 0, k:k + 1], ALU.mult, ALU.add)
                last.then_inc(xT_d, 1)

            def expert_pair(pair, it, more=True):
                if more:
                    dve.wait_ge(gx_done, it * 2 + 2)
                    dve.wait_ge(MW_ready, it + 1)
                    match(pair + 1)
                for s in range(8):
                    dve.wait_ge(scat_done, it * 8 + (s + 1))
                    a = acc[:, s // 2, s % 2 * CHUNK:(s % 2 + 1) * CHUNK]
                    tt(a, PS[:, (6, 7, 5)[s % 3], :], a, ALU.add).then_inc(acc_added, 1)
                dve.wait_ge(mwt_done, it + 1)
                ts(MT[:, :], PS[:, 2, :], 0.0, None, ALU.not_equal)
                V_.tensor_reduce(out=wslot[:, :], in_=PS[:, 2, :], axis=AX.X, op=ALU.add).then_inc(mt_ready, 1)
                dve.wait_ge(silu_ready, it + 1)
                dve.wait_ge(slot_used[7], it + 1)
                dve.wait_ge(mt_ready, it + 2)
                V_.scalar_tensor_tensor(out=hid[:, :], in0=gate_act[:, :], scalar=wslot[:, :], in1=PS[:, 4, :],
                                        op0=ALU.mult, op1=ALU.mult).then_inc(hid_ready, 1)
                if more:
                    weigh(pair + 1, it + 1)
                dve.wait_ge(hidT_done, it + 1)
                cp(hidT[:, :, :].rearrange("p f s -> p (f s)"), PS[:, 5, :]).then_inc(hidT_ready, 1)
                if more:
                    xT_lower(it + 1)
                for n in range(2):
                    dve.wait_ge(yH_ready, 2 * it + (n + 1))
                    last = tt(yL[:, n * 512:(n + 1) * 512], PS[:, 6 + n, :], yH[:, n * 512:(n + 1) * 512].bitcast(F32),
                              ALU.subtract)
                last.then_inc(y_split, 1)

            def one_round(it0, first=False):
                match(0)
                if first:
                    expert_weights()
                    dve.wait_ge(zeroed, 4)
                weigh(0, it0)
                xT_lower(it0)
                with dve.Fori(0, PAIRS - 1) as p:
                    expert_pair(p, it0 + p)
                expert_pair(PAIRS - 1, it0 + PAIRS - 1, more=False)

            dve.wait_ge(shifted, 1)
            one_round(0, first=True)
            fullest = dve.value_load(cmax[0:1, 0:1], min_val=0, max_val=SEQ)
            with dve.If(fullest > CAP):
                with dve.Fori(1, ROUNDS) as r:
                    with dve.If(fullest > r * CAP):
                        dve.wait_ge(shifted, r)
                        ts(slotval[:, :, :], slotval[:, :, :], float(-CAP), None, ALU.add).then_inc(shifted, 1)
                        dve.wait_ge(shifted, r + 1)
                        dve.wait_ge(gx_done, r * 2 * PAIRS)
                        dve.wait_ge(MW_ready, r * PAIRS)
                        one_round(r * PAIRS)
            cp(bss[:, 1:2], bss[:, 1:2]).then_inc(last_split, 1)

            def last_rows(ti):
                dve.wait_ge(last_scat, 2 * (ti + 1))
                tt(acc[:, ti, :], both(ti), acc[:, ti, :], ALU.add).then_inc(final_added, 1)

            def scale(ti):
                dve.wait_ge(end_rstd, ti + 1)
                V_.scalar_tensor_tensor(out=acc[:, ti, :], in0=acc[:, ti, :] if ti else both(0),
                                        scalar=rstd[:, S_END + ti:S_END + ti + 1], in1=g2p[:, :],
                                        op0=ALU.mult, op1=ALU.mult).then_inc(end_scaled, 1)

            def add_residual(ti):
                dve.wait_ge(end_scaled, ti + 1)
                tt(acc[:, ti, :], acc[:, ti, :], x1[:, ti, :], ALU.add).then_inc(end_ready[1], 1)

            last_rows(1)
            scale(0)
            last_rows(2)
            last_rows(3)
            scale(1)
            for ti in (2, 3):
                scale(ti)
                add_residual(ti)

        @block.gpsimd
        def _(pool):
            G = nc.gpsimd
            own = [0]
            G.memset(spad[:, :, :], 0.0).then_inc(spad_zero, 1)
            pool.wait_ge(cst_in, 32)

            def inverse_root(n, sums, means, roots, a, b, done):
                G.tensor_scalar(means[:, a:b], sums[:, a:b], 1.0 / n, EPS, ALU.mult, ALU.add).then_inc(pool_own, 1)
                own[0] += 1
                pool.wait_ge(pool_own, own[0])
                G.tensor_tensor(roots[:, a:b], means[:, a:b], k_("half")[:, 0:1].to_broadcast([P, b - a]),
                                ALU.pow).then_inc(done, 1)

            pool.wait_ge(in_sq, NT + NC)
            inverse_root(D, ss, ms, rstd, S_IN, S_IN + 6, in_rstd)
            for t, ti in enumerate(TURN):
                pool.wait_ge(bsq_ready, t + 1)
                inverse_root(HD, bss, bms, brs, 0 if ti < NT else 8, 10, brstd_ready)
            pool.wait_ge(row_done, 1)
            G.tensor_tensor(wr[:, :, :], wr[:, :, :], modcol[:, 3, 0, :].rearrange("p (k o) -> p k o", o=1).to_broadcast(
                [P, KD, NG + NE]), ALU.mult).then_inc(wr_ready, 1)
            for g in range(2):
                pool.wait_ge(grp_sq, 4 * (g + 1))
                inverse_root(512, ss, ms, rstd, S_GRP + 4 * g, S_GRP + 4 * g + 4, grp_rstd)
            for ti in range(NT):
                pool.wait_ge(mix_sq, ti + 1)
                inverse_root(D, ss, ms, rstd, S_MIX + ti, S_MIX + ti + 1, mix_rstd)
                pool.wait_ge(ffn_sq, ti + 1)
                inverse_root(D, ss, ms, rstd, S_FFN + ti, S_FFN + ti + 1, ffn_rstd)
            pool.wait_ge(proj_done[1], NT)
            for ti in range(NT):
                G.memset(acc[:, ti, :], 0.0).then_inc(zeroed, 1)
            G.memset(hid[:, :], 0.0).then_inc(hid_ready, 1)
            G.memset(MT[:, :].bitcast(F32), 0.0).then_inc(mt_ready, 1)
            pool.wait_ge(mid_cut, NT)
            G.tensor_tensor(xparts[:, 2, NT - 1, :], rest_tmp[:, :], xparts[:, 1, NT - 1, :],
                            ALU.subtract).then_inc(parts_ready, 1)
            pool.wait_ge(h2t_done, NT)
            G.memset(yH[:, :].bitcast(F32), 0.0).then_inc(zeroed, 1)
            G.memset(yL[:, :].bitcast(F32), 0.0).then_inc(y_split, 1)
            for tiles in ((0, 1), (2, 3)):
                for ti in tiles:
                    pool.wait_ge(end_sq, ti + 1)
                    inverse_root(D, ss, ms, rstd, S_END + ti, S_END + ti + 1, end_rstd)
                ti = tiles[0] // 2
                pool.wait_ge(end_scaled, ti + 1)
                G.tensor_tensor(acc[:, ti, :], acc[:, ti, :], x1[:, ti, :], ALU.add).then_inc(end_ready[0], 1)


_INS = ["x", "c", "ctx", "c_ctx", "w_mod", "b_mod", "attn_pre_norm", "attn_post_norm", "w_in", "a_sink",
        "b_q_norm", "b_k_norm", "a_out_norm", "b_out_norm", "w_out", "ffn_pre_norm", "ffn_post_norm",
        "w_group", "b_group", "w_router", "b_router", "w_gate", "w_up", "w_down"]


def kernel(**inputs):
    import numpy as _np
    import concourse.bacc as _bacc
    from concourse import mybir as _mybir
    from concourse.bass_utils import run_bass_kernel_spmd as _run

    nc = _bacc.Bacc("TRN2", target_bir_lowering=False, num_devices=1)
    arrays, args = {}, []
    for name in _INS + ["shape_constants"]:
        a = shape_constants() if name == "shape_constants" else _np.ascontiguousarray(inputs[name])
        arrays[f"in_{name}"] = a
        args.append(nc.dram_tensor(f"in_{name}", a.shape, _mybir.dt.from_np(a.dtype), kind="ExternalInput").ap())
    args.append(nc.dram_tensor("out_x", (1, SEQ, D), F32, kind="ExternalOutput").ap())
    backbone_layer(nc, *args)
    r = _run(nc, [arrays], core_ids=[0])
    return r.results[0]["out_x"]
```
